# Optimizing a Trainium2 kernel written in Bass

```python
import math
import jax, jax.numpy as jnp
from jax import lax
import numpy as np

D_MODEL = 1024
BATCH = 1
SEQ = 256
DEPTH = 1

GRID_W = 64
CTX_LEN = 256
HEAD_DIM = 64
D_MIX = D_MODEL
NA_HEADS = (D_MIX // 2) // HEAD_DIM
NA_WIDTH = NA_HEADS * HEAD_DIM
NA_WIN_R = 8
NA_WIN_C = 16
DIFF_QK = HEAD_DIM
DIFF_V = 2 * DIFF_QK
DIFF_HEADS = (D_MIX - NA_WIDTH) // DIFF_V
DIFF_WIDTH = DIFF_HEADS * DIFF_V
DIFF_QK_WIDTH = 2 * DIFF_HEADS * DIFF_QK
QKV_WIDTH = 3 * NA_WIDTH + 2 * DIFF_QK_WIDTH + DIFF_WIDTH
Q_BLOCK = 128
ROPE_THETA = 10000.0
PEER_HEADS = 8
PEER_NKEYS = 128
PEER_EXPERTS = PEER_NKEYS * PEER_NKEYS
PEER_QDIM = 256
PEER_TOPK = 16
TOKEN_BLOCK = 128
N_MOD = 6
EPS = 1e-6

kernel_name = "hybrid_natten_diffattn_peer_block"

def rmsnorm(x, g):
    xf = x.astype(jnp.float32)
    y = xf * lax.rsqrt(jnp.mean(xf * xf, axis=-1, keepdims=True) + EPS)
    return (y * g.astype(jnp.float32)).astype(x.dtype)

def modulate(h, shift, scale):
    return h * (1.0 + scale) + shift

def axial_rope_tables(n_tokens, dim):
    t = jnp.arange(n_tokens)
    row = (t // GRID_W).astype(jnp.float32)
    col = (t % GRID_W).astype(jnp.float32)
    n_freq = dim // 4
    inv = ROPE_THETA ** (-jnp.arange(n_freq, dtype=jnp.float32) / n_freq)
    ang = jnp.concatenate([row[:, None] * inv, col[:, None] * inv], axis=-1)
    return jnp.cos(ang), jnp.sin(ang)

def apply_rope(x, cos, sin):
    xp = x.reshape(x.shape[:-1] + (x.shape[-1] // 2, 2))
    x0, x1 = xp[..., 0], xp[..., 1]
    cos = cos.astype(x.dtype)
    sin = sin.astype(x.dtype)
    return jnp.stack([x0 * cos - x1 * sin, x0 * sin + x1 * cos], axis=-1).reshape(x.shape)

def split_projection(p):
    B, L, _ = p.shape
    cuts = [int(i) for i in np.cumsum([NA_WIDTH, NA_WIDTH, NA_WIDTH, DIFF_QK_WIDTH, DIFF_QK_WIDTH])]
    qa, ka, va, qd, kd, vd = jnp.split(p, cuts, axis=-1)
    heads_a = lambda t: t.reshape(B, L, NA_HEADS, HEAD_DIM).transpose(0, 2, 1, 3)
    heads_qk = lambda t: t.reshape(B, L, 2, DIFF_HEADS, DIFF_QK).transpose(0, 2, 3, 1, 4)
    heads_v = lambda t: t.reshape(B, L, DIFF_HEADS, DIFF_V).transpose(0, 2, 1, 3)
    return heads_a(qa), heads_a(ka), heads_a(va), heads_qk(qd), heads_qk(kd), heads_v(vd)

def merge_heads(out_a, out_d, w_out):
    B, _, L, _ = out_a.shape
    ya = out_a.transpose(0, 2, 1, 3).reshape(B, L, NA_WIDTH)
    yd = out_d.transpose(0, 2, 1, 3).reshape(B, L, DIFF_WIDTH)
    return jnp.concatenate([ya, yd], axis=-1) @ w_out

def neighbourhood_attention(q, k, v, k_ctx, v_ctx, rel_bias):
    B, H, T, d = q.shape
    C = k_ctx.shape[2]
    rows = T // GRID_W
    kr = min(NA_WIN_R, rows)
    kc = NA_WIN_C
    qg = q.reshape(B, H, rows, GRID_W, d)
    kg = k.reshape(B, H, rows, GRID_W, d)
    vg = v.reshape(B, H, rows, GRID_W, d)
    cols = jnp.arange(GRID_W)
    c_start = jnp.clip(cols - kc // 2, 0, GRID_W - kc)
    c_idx = c_start[:, None] + jnp.arange(kc)[None, :]
    c_off = c_idx - cols[:, None] + (NA_WIN_C - 1)
    scale = d ** -0.5

    def row_block(r):
        r_start = jnp.clip(r - kr // 2, 0, rows - kr)
        q_r = lax.dynamic_index_in_dim(qg, r, axis=2, keepdims=False)
        k_r = lax.dynamic_slice_in_dim(kg, r_start, kr, axis=2)
        v_r = lax.dynamic_slice_in_dim(vg, r_start, kr, axis=2)
        k_nb = k_r[:, :, :, c_idx]
        v_nb = v_r[:, :, :, c_idx]
        r_off = r_start + jnp.arange(kr) - r + (NA_WIN_R - 1)
        bias = rel_bias[:, r_off][:, :, c_off].transpose(0, 2, 1, 3)
        s_loc = jnp.einsum('bhwd,bhawkd->bhwak', q_r, k_nb) * scale + bias[None]
        s_ctx = jnp.einsum('bhwd,bhcd->bhwc', q_r, k_ctx) * scale
        s = jnp.concatenate([s_ctx, s_loc.reshape(B, H, GRID_W, kr * kc)], axis=-1)
        p = jax.nn.softmax(s.astype(jnp.float32), axis=-1).astype(v.dtype)
        p_ctx = p[..., :C]
        p_loc = p[..., C:].reshape(B, H, GRID_W, kr, kc)
        return (jnp.einsum('bhwc,bhcd->bhwd', p_ctx, v_ctx)
                + jnp.einsum('bhwak,bhawkd->bhwd', p_loc, v_nb))

    out = lax.map(row_block, jnp.arange(rows))
    return out.transpose(1, 2, 0, 3, 4).reshape(B, H, T, d)

def dense_attention(q, k, v):
    s = jnp.einsum('bhqd,bhkd->bhqk', q, k) * (q.shape[-1] ** -0.5)
    p = jax.nn.softmax(s.astype(jnp.float32), axis=-1).astype(v.dtype)
    return jnp.einsum('bhqk,bhkd->bhqd', p, v)

def diff_lambda_value(lam_params, lambda_init):
    lp = lam_params.astype(jnp.float32)
    return jnp.exp(jnp.sum(lp[0] * lp[1])) - jnp.exp(jnp.sum(lp[2] * lp[3])) + lambda_init

def diff_attention_block(q, k, v, lam):
    s = jnp.einsum('bmhqd,bmhkd->bmhqk', q, k).astype(jnp.float32) * (q.shape[-1] ** -0.5)
    p = jax.nn.softmax(s, axis=-1)
    a = p[:, 0] - lam * p[:, 1]
    return jnp.einsum('bhqk,bhkd->bhqd', a.astype(v.dtype), v)

def diff_attention_latent(q, k, v, k_ctx, v_ctx, lam):
    B, M, H, T, d = q.shape
    k_all = jnp.concatenate([k_ctx, k], axis=3)
    v_all = jnp.concatenate([v_ctx, v], axis=2)
    nb = T // Q_BLOCK
    qb = q.reshape(B, M, H, nb, Q_BLOCK, d).transpose(3, 0, 1, 2, 4, 5)
    out = lax.map(lambda qq: diff_attention_block(qq, k_all, v_all, lam), qb)
    return out.transpose(1, 2, 0, 3, 4).reshape(B, H, T, v.shape[-1])

def peer_ffn(h, w_q, keys, u, v):
    shp = h.shape
    hb = h.reshape(-1, TOKEN_BLOCK, shp[-1])

    def block(xb):
        tb = xb.shape[0]
        q = (xb @ w_q).reshape(tb, PEER_HEADS, 2, PEER_QDIM // 2)
        s = jnp.einsum('thpd,hpnd->thpn', q, keys).astype(jnp.float32)
        s_top, i_top = lax.top_k(s, PEER_TOPK)
        cand = s_top[:, :, 0, :, None] + s_top[:, :, 1, None, :]
        cand_idx = i_top[:, :, 0, :, None] * PEER_NKEYS + i_top[:, :, 1, None, :]
        best, pos = lax.top_k(cand.reshape(tb, PEER_HEADS, PEER_TOPK * PEER_TOPK), PEER_TOPK)
        experts = jnp.take_along_axis(cand_idx.reshape(tb, PEER_HEADS, -1), pos, axis=-1)
        gates = jax.nn.softmax(best, axis=-1).astype(xb.dtype)
        u_sel = u[experts]
        v_sel = v[experts]
        act = jax.nn.gelu(jnp.einsum('td,thkd->thk', xb, u_sel), approximate=False)
        return jnp.einsum('thk,thkd->td', gates * act, v_sel)

    return lax.map(block, hb).reshape(shp)

def setup_inputs(seed: int = 0) -> dict:
    key = jax.random.key(seed)
    ks = jax.random.split(key, 16)
    nrm = lambda k, shape, s: s * jax.random.normal(k, shape, jnp.float32)
    return {
        "x": nrm(ks[0], (BATCH, SEQ, D_MODEL), 1.0),
        "c": nrm(ks[1], (BATCH, D_MODEL), 1.0),
        "ctx": nrm(ks[2], (BATCH, CTX_LEN, D_MODEL), 1.0),
        "c_ctx": nrm(ks[3], (D_MODEL,), 1.0),
        "w_ada": nrm(ks[4], (DEPTH, D_MODEL, N_MOD * D_MODEL), 0.5 * D_MODEL ** -0.5),
        "b_ada": nrm(ks[5], (DEPTH, N_MOD * D_MODEL), 0.02),
        "g_norm": 1.0 + nrm(ks[6], (DEPTH, 4, D_MODEL), 0.02),
        "w_in": nrm(ks[7], (DEPTH, D_MODEL, QKV_WIDTH), D_MODEL ** -0.5),
        "na_rel_bias": nrm(ks[8], (DEPTH, NA_HEADS, 2 * NA_WIN_R - 1, 2 * NA_WIN_C - 1), 0.1),
        "diff_lambda": nrm(ks[9], (DEPTH, 4, DIFF_QK), 0.1),
        "diff_subln": 1.0 + nrm(ks[10], (DEPTH, DIFF_V), 0.02),
        "w_out": nrm(ks[11], (DEPTH, D_MIX, D_MODEL), D_MIX ** -0.5),
        "peer_wq": nrm(ks[12], (DEPTH, D_MODEL, PEER_HEADS * PEER_QDIM), D_MODEL ** -0.5),
        "peer_keys": nrm(ks[13], (DEPTH, PEER_HEADS, 2, PEER_NKEYS, PEER_QDIM // 2), (PEER_QDIM // 2) ** -0.5),
        "peer_u": nrm(ks[14], (DEPTH, PEER_EXPERTS, D_MODEL), D_MODEL ** -0.5),
        "peer_v": nrm(ks[15], (DEPTH, PEER_EXPERTS, D_MODEL), D_MODEL ** -0.5),
    }

def reference(x, c, ctx, c_ctx, w_ada, b_ada, g_norm, w_in, na_rel_bias, diff_lambda,
              diff_subln, w_out, peer_wq, peer_keys, peer_u, peer_v):
    T = x.shape[1]
    cos, sin = axial_rope_tables(T, DIFF_QK)
    x_lat, x_ctx = x, ctx
    for l in range(DEPTH):
        lambda_init = 0.8 - 0.6 * math.exp(-0.3 * l)
        mod_lat = (jax.nn.silu(c) @ w_ada[l] + b_ada[l])[:, None, :]
        mod_ctx = (jax.nn.silu(c_ctx) @ w_ada[l] + b_ada[l])[None, None, :]
        sh1, sc1, gt1, sh2, sc2, gt2 = jnp.split(mod_lat, N_MOD, axis=-1)
        csh1, csc1, cgt1, csh2, csc2, cgt2 = jnp.split(mod_ctx, N_MOD, axis=-1)
        lam = diff_lambda_value(diff_lambda[l], lambda_init)

        h_lat = modulate(rmsnorm(x_lat, g_norm[l, 0]), sh1, sc1)
        h_ctx = modulate(rmsnorm(x_ctx, g_norm[l, 0]), csh1, csc1)
        qa, ka, va, qd, kd, vd = split_projection(h_lat @ w_in[l])
        qa_c, ka_c, va_c, qd_c, kd_c, vd_c = split_projection(h_ctx @ w_in[l])
        qd = apply_rope(qd, cos, sin)
        kd = apply_rope(kd, cos, sin)

        out_a = neighbourhood_attention(qa, ka, va, ka_c, va_c, na_rel_bias[l])
        out_d = diff_attention_latent(qd, kd, vd, kd_c, vd_c, lam)
        out_d = rmsnorm(out_d, diff_subln[l]) * (1.0 - lambda_init)
        y = merge_heads(out_a, out_d, w_out[l])
        x_lat_new = x_lat + gt1 * rmsnorm(y, g_norm[l, 1])

        h2 = modulate(rmsnorm(x_lat_new, g_norm[l, 2]), sh2, sc2)
        x_lat_new = x_lat_new + gt2 * rmsnorm(peer_ffn(h2, peer_wq[l], peer_keys[l], peer_u[l], peer_v[l]), g_norm[l, 3])

        if l < DEPTH - 1:
            out_a_c = dense_attention(qa_c, ka_c, va_c)
            out_d_c = rmsnorm(diff_attention_block(qd_c, kd_c, vd_c, lam), diff_subln[l]) * (1.0 - lambda_init)
            y_c = merge_heads(out_a_c, out_d_c, w_out[l])
            x_ctx = x_ctx + cgt1 * rmsnorm(y_c, g_norm[l, 1])
            h2c = modulate(rmsnorm(x_ctx, g_norm[l, 2]), csh2, csc2)
            x_ctx = x_ctx + cgt2 * rmsnorm(peer_ffn(h2c, peer_wq[l], peer_keys[l], peer_u[l], peer_v[l]), g_norm[l, 3])
        x_lat = x_lat_new
    return x_lat


_drawn_inputs = setup_inputs


def setup_inputs(seed=0):
    import zlib

    import numpy as np

    out = dict(_drawn_inputs(seed))
    spreads = {}
    factors = {'na_rel_bias': 3.813, 'diff_lambda': 2.72}
    for name, (base, spread) in spreads.items():
        noise = np.random.default_rng([zlib.crc32(name.encode()), seed]).standard_normal(out[name].shape)
        drawn = base * np.exp(spread * noise) if base else spread * noise
        out[name] = __import__('jax').numpy.asarray(drawn.astype(out[name].dtype))
    for name, factor in factors.items():
        out[name] = (out[name] * factor).astype(out[name].dtype)
    return out
```

```python
import concourse.bass as bass
from concourse import mybir
from contextlib import ExitStack, contextmanager

D = 1024
T = 256
CTX = 256
LC = T + CTX
P = 128
NC = D // P
HD = 64
GRID_W = 64
WIN_C = 16
WIN_R = 8
NA_HEADS = 8
DIFF_HEADS = 4
LAMBDA_INIT = 0.2
EPS = 1e-6
SCALE = HD ** -0.5
PH = 8
NK = 128
TOPK = 16
NMOD = 6
MASKED = -1e30
REMOVED = -3.0e38
PW = 1024

KP0, QP0, VP0, WO0, WQ0, U0, V0 = 0, 8, 16, 24, 32, 48, 176
PIECES = 304
ADA_N = 256
ADA_BLOCKS = NMOD * D // ADA_N
ADA_FIRST = 2 * D // ADA_N
SH1, SC1, GT1, SH2, SC2, GT2 = (k * NC for k in range(NMOD))

C_ID, C_ONE, C_IOTA, C_PERM, C_SEL, C_I16, C_END = 0, 128, 256, 384, 512, 514, 530
S_B, S_G, S_LN, S_END = 0, 48, 80, 81
R_COS, R_SIN, R_MASK, R_LAM, R_END = 0, 256, 512, 768, 1024


class Steps:

    def __init__(self, eng, sem):
        self.eng, self.sem, self.n, self.local = eng, sem, 0, 0

    def add(self, ins):
        ins.then_inc(self.sem, 1)
        self.n = self.n + 1
        self.local += 1

    def wait(self):
        self.eng.wait_ge(self.sem, self.n)

    def link(self, ins):
        self.add(ins)
        self.wait()

    def link_drained(self, ins):
        self.add(ins)
        self.eng.drain()


@contextmanager
def repeat(eng, times, steps, per_time):
    base, local = steps.n, steps.local
    with eng.Fori(0, times) as i:
        steps.n = base + i * per_time
        yield i
    assert steps.local - local == per_time, (steps.local - local, per_time)
    steps.n = base + times * per_time


def program(nc, xT_d, cT_d, cst_d, small_d, tab_d, ada_d, bias_d, keys_d, stream_d, out_d):
    f32, f32r, u32 = mybir.dt.float32, mybir.dt.float32r, mybir.dt.uint32
    ALU = mybir.AluOpType
    ACT = mybir.ActivationFunctionType
    AX = mybir.AxisListType.X
    ds = bass.ds

    whole = ExitStack()
    with whole:
        def on(stack, name, shape, dt=f32):
            return stack.enter_context(nc.sbuf_tensor(name, shape, dt))

        def sem(name):
            return whole.enter_context(nc.semaphore(name))

        raw = on(whole, "raw", [P, 4, PW])
        hi = on(whole, "hi", [P, 2, PW], f32r)
        lo = on(whole, "lo", [P, 2, PW], f32r)
        x1T = on(whole, "x1T", [P, NC, T])
        cst = on(whole, "cst", [P, C_END])
        small = on(whole, "small", [P, S_END])
        mod = on(whole, "mod", [P, NMOD * NC, 2])
        gs = on(whole, "gs", [P, 2, NC, 2])
        gg = on(whole, "gg", [P, 2, NC])
        fin = on(whole, "fin", [P, 16])
        epsc = on(whole, "epsc", [P, 1])

        place1 = ExitStack()
        tok_hi = on(place1, "tok_hi", [P, NC, T], f32r)
        tok_lo = on(place1, "tok_lo", [P, NC, T], f32r)
        place1.close()
        x1n = on(whole, "x1n", [P, 2, D])
        ggB = on(whole, "ggB", [P, D])
        w_hi = on(whole, "w_hi", [P, 2, T], f32r)
        w_lo = on(whole, "w_lo", [P, 2, T], f32r)

        place2 = ExitStack()
        xT = on(place2, "xT", [P, NC, LC])
        kT = on(place2, "kT", [P, NC, LC])
        qraw = on(place2, "qraw", [P, 4, T])
        qz = on(place2, "qz", [P, 16, T])
        vN = on(place2, "vN", [P, 4, D])
        ada = on(place2, "ada", [P, 4, NC, ADA_N])
        cT = on(place2, "cT", [P, NC, 2])
        cS = on(place2, "cS", [P, NC, 32])
        rows = on(place2, "rows", [P, 2, ADA_N])
        rstd = on(place2, "rstd", [P, LC])
        tab = on(place2, "tab", [P, R_END])
        lamt = on(place2, "lamt", [P, 2, HD])
        lam = on(place2, "lam", [P, 4])
        mraw = on(place2, "mraw", [P, 4])
        nmax = on(place2, "nmax", [P, 4])
        rsum = on(place2, "rsum", [P, 4])
        rinv = on(place2, "rinv", [P, 4])
        hplace = ExitStack()
        h_hi = on(hplace, "h_hi", [P, NC, LC], f32r)
        h_lo = on(hplace, "h_lo", [P, NC, LC], f32r)
        hplace.close()
        prob_e = on(hplace, "prob_e", [P, 4, LC])
        prob = on(hplace, "prob", [P, 2, LC])
        probT = on(hplace, "probT", [P, 2, 4, T])
        attf = on(hplace, "attf", [P, NC, T])
        hplace.close()
        ysq = on(hplace, "ysq", [P, NC, T])
        ytmp = on(hplace, "ytmp", [P, NC, T])
        hplace.close()
        place2.close()
        xn = vN[:, :, :].rearrange("p a (b t) -> p (a b) t", t=LC)
        xsq = kT
        bias = ada[:, 0:2, :, :].rearrange("p a c n -> p (a c) n")

        early = ExitStack()
        qT = on(early, "qT", [P, 16, T])
        keys = on(early, "keys", [P, 16, NK])
        early.close()
        TAIL = 96
        late = ExitStack()
        on(late, "below_tail", [P, TAIL * T])
        sc = on(late, "sc", [P, 32, NK])
        sv = on(late, "sv", [P, 32, TOPK])
        si = on(late, "si", [P, 32, TOPK])
        work = on(late, "work", [P, 2, NK])
        m16 = on(late, "m16", [P, TOPK])
        i16 = on(late, "i16", [P, TOPK], u32)
        cand = on(late, "cand", [P, 2, TOPK * TOPK])
        ab = on(late, "ab", [P, 2, TOPK], u32)
        abf = on(late, "abf", [P, 2, TOPK])
        eq = on(late, "eq", [P, 2, TOPK, TOPK])
        best = on(late, "best", [P, 2, PH, TOPK])
        ijs = on(late, "ijs", [P, 2, 2, PH, TOPK])
        gate = on(late, "gate", [P, 2 * PH, TOPK])
        gsum = on(late, "gsum", [P, 2 * PH])
        late.close()

        act_t = on(whole, "act_t", [P, NK, T])
        slot = on(whole, "slot", [P, 3, T])
        ohi = on(whole, "ohi", [P, 8, NK])
        idx = on(whole, "idx", [P, 8])
        ghj = on(whole, "ghj", [P, 8, NK])
        fout = act_t[:, 0:16, :].rearrange("p (a c) t -> p a (c t)", a=4)

        PB = [whole.enter_context(nc.psum_tensor(f"PB{b}", [P, 512], f32)) for b in range(8)]

        x_loaded, c_loaded, cst_loaded, small_loaded, tab_loaded = map(
            sem, ["x_loaded", "c_loaded", "cst_loaded", "small_loaded", "tab_loaded"])
        bias_loaded, keys_loaded = sem("bias_loaded"), sem("keys_loaded")
        ada_loaded = [sem(f"ada_loaded{k}") for k in range(4)]
        raw_loaded = [sem(f"raw_loaded{k}") for k in range(4)]
        hi_ready, lo_ready = sem("hi_ready"), sem("lo_ready")
        hi_used, piece_done = sem("hi_used"), sem("piece_done")
        dve_step, act_step, pool_step = sem("dve_step"), sem("act_step"), sem("pool_step")
        zeroed, silu_done, xsq_done, xss_done, std_done = map(
            sem, ["zeroed", "silu_done", "xsq_done", "xss_done", "std_done"])
        ada_used, rows_ready, mod_summed, mod_ready = map(
            sem, ["ada_used", "rows_ready", "mod_summed", "mod_ready"])
        h_ready, h_hi_ready, h_lo_ready = sem("h_ready"), sem("h_hi_ready"), sem("h_lo_ready")
        kq_copied, v_copied = sem("kq_copied"), sem("v_copied")
        swapped, roped = sem("swapped"), sem("roped")
        lam_dot, lam_exp = sem("lam_dot"), sem("lam_exp")
        bias_ready = sem("bias_ready")
        scored, max_ready, exp_done, prob_ready = map(sem, ["scored", "max_ready", "exp_done", "prob_ready"])
        transposed, probT_ready, pv_done, att_copied = map(
            sem, ["transposed", "probT_ready", "pv_done", "att_copied"])
        dsq_done, dss_done, dstd_done, att_ready = map(
            sem, ["dsq_done", "dss_done", "dstd_done", "att_ready"])
        tok_hi_ready, tok_lo_ready = sem("tok_hi_ready"), sem("tok_lo_ready")
        ysq_done, yss_done, ystd_done, x1_ready = map(sem, ["ysq_done", "yss_done", "ystd_done", "x1_ready"])
        x1sq_done, x1ss_done, x1std_done, h2_ready = map(
            sem, ["x1sq_done", "x1ss_done", "x1std_done", "h2_ready"])
        q_copied, s_done, s_copied = sem("q_copied"), sem("s_done"), sem("s_copied")
        act_done = sem("act_done")
        best_ready, gexp_done, gate_ready, slotT_done, slot_ready = map(
            sem, ["best_ready", "gexp_done", "gate_ready", "slotT_done", "slot_ready"])
        ohi_ready, ghj_ready, gate_done, weighted = map(sem, ["ohi_ready", "ghj_ready", "gate_done", "weighted"])
        final_rows, final_rows_copied = sem("final_rows"), sem("final_rows_copied")
        w_hi_ready, w_lo_ready = sem("w_hi_ready"), sem("w_lo_ready")
        fsq_done, fss_ready, fstd_done, out_ready, out_stored = map(
            sem, ["fsq_done", "fss_ready", "fstd_done", "out_ready", "out_stored"])

        ident = cst[:, C_ID:C_ID + P]
        ones = cst[:, C_ONE:C_ONE + P]
        iota = cst[:, C_IOTA:C_IOTA + P]
        perm = cst[:, C_PERM:C_PERM + P]
        sel = cst[:, C_SEL:C_SEL + 2]
        iota16 = cst[:, C_I16:C_I16 + TOPK]

        units = [("d", h, t) for h in range(DIFF_HEADS) for t in range(2)]
        units += [("n", h, t) for h in range(NA_HEADS) for t in range(2)]
        maps_of, k = [], 0
        for kind, _, _ in units:
            n = 2 if kind == "d" else 1
            maps_of.append(list(range(k, k + n)))
            k += n
        N_UNITS = len(units)
        N_AHEADS = DIFF_HEADS + NA_HEADS
        unit_of_map = [u for u, ks in enumerate(maps_of) for _ in ks]

        block = whole.enter_context(nc.Block())

        @block.sync
        def _(sp):
            def load(n, k):
                sp.dma_start(raw[:, k, :], stream_d[ds(n, 1), :, :].rearrange("a p w -> p (a w)")
                             ).then_inc(raw_loaded[k], 16)

            for k in range(4):
                load(k, k)
            with sp.Fori(1, PIECES // 4) as i:
                for k in range(4):
                    sp.wait_ge(lo_ready, 4 * i + k - 3)
                    load(4 * i + k, k)
            for k in range(4):
                sp.wait_ge(out_ready, k + 1)
                sp.dma_start(out_d[0, (k // 2) * P:(k // 2 + 1) * P, (k % 2) * 512:(k % 2 + 1) * 512],
                             fout[:, k, 0:512]).then_inc(out_stored, 16)
            sp.wait_ge(out_stored, 64)

        @block.gpsimd
        def _(pool):
            own = Steps(pool, pool_step)
            def load_ada(b, k):
                pool.dma_start(ada[:, k, :, :],
                               ada_d[ds(b, 1), :, :].rearrange("a p (c n) -> p (a c) n", c=NC)
                               ).then_inc(ada_loaded[k], 16)

            for k in range(4):
                load_ada(k, k)
            with pool.Fori(1, ADA_BLOCKS // 4) as i:
                for k in range(4):
                    pool.wait_ge(ada_used, 4 * i + k - 3)
                    load_ada(4 * i + k, k)
            pool.wait_ge(ada_used, ADA_BLOCKS)
            pool.dma_start(bias, bias_d).then_inc(bias_loaded, 16)
            pool.wait_ge(bias_loaded, 16)
            pool.wait_ge(tab_loaded, 16)
            nc.gpsimd.tensor_tensor(bias, bias, tab[:, None, R_MASK:R_MASK + T].to_broadcast([P, 16, T]),
                                    ALU.add).then_inc(bias_ready, 1)
            pool.wait_ge(x1_ready, NC)
            pool.wait_ge(pv_done, N_AHEADS)
            pool.dma_start(keys[:, :, :], keys_d).then_inc(keys_loaded, 16)
            pool.wait_ge(slot_ready, 3)
            pool.wait_ge(act_done, NK)

            def one_hot(q, half):
                own.link_drained(nc.gpsimd.tensor_copy(idx[:, 4 * half:4 * half + 4], slot[:, 0, ds(4 * q, 4)]))
                for e in range(4 * half, 4 * half + 4):
                    nc.gpsimd.tensor_scalar(ohi[:, e, :], iota, idx[:, e:e + 1], None,
                                            ALU.is_equal).then_inc(ohi_ready, 1)

            one_hot(0, 0)
            one_hot(1, 1)
            with repeat(pool, T // 8 - 1, own, 2) as i:
                for half in range(2):
                    pool.wait_ge(gate_done, 2 * i + half + 1)
                    one_hot(2 * i + half + 2, half)

        @block.scalar
        def _(act):
            def hi_of(m, turn, k):
                act.wait_ge(raw_loaded[k], 16 * turn + 16)
                if not (isinstance(m, int) and m < 2):
                    act.wait_ge(hi_used, m - 1)
                    act.wait_ge(lo_ready, m - 1)
                nc.scalar.copy(hi[:, k % 2, :], raw[:, k, :]).then_inc(hi_ready, 1)

            def lead(n):
                m = n + 2
                if m < PIECES:
                    hi_of(m, m // 4, m % 4)

            act.dma_start(cT[:, :, :], cT_d).then_inc(c_loaded, 16)
            act.dma_start(xT[:, :, :], xT_d).then_inc(x_loaded, 16)
            act.dma_start(cst[:, :], cst_d).then_inc(cst_loaded, 16)
            act.dma_start(small[:, :], small_d).then_inc(small_loaded, 16)
            act.dma_start(tab[:, :], tab_d).then_inc(tab_loaded, 16)

            act.wait_ge(c_loaded, 16)
            act.wait_ge(zeroed, 1)
            nc.scalar.activation(cS[:, :, 0:2], cT[:, :, :], ACT.Silu).then_inc(silu_done, 1)
            act.wait_ge(x_loaded, 16)
            for g in range(4):
                nc.scalar.activation(xsq[:, 2 * g:2 * g + 2, :], xT[:, 2 * g:2 * g + 2, :],
                                     ACT.Square).then_inc(xsq_done, 1)
            hi_of(0, 0, 0)
            hi_of(1, 0, 1)
            act.wait_ge(zeroed, 2)
            act.wait_ge(xss_done, 1)
            nc.scalar.activation(rstd[:, :], PB[3][:, :], ACT.Sqrt, bias=epsc[:, 0:1],
                                 scale=1.0 / D).then_inc(std_done, 1)
            for c in range(NC):
                act.wait_ge(h_ready, c + 1)
                nc.scalar.copy(h_hi[:, c, :], xn[:, c, :]).then_inc(h_hi_ready, 1)

            with act.Fori(0, 2) as i:
                for k in range(4):
                    n = 4 * i + k
                    hi_of(n + 2, i + (k + 2) // 4, (k + 2) % 4)
                    act.wait_ge(piece_done, n + 1)
                    nc.scalar.copy(kT[:, ds(n, 1), :].rearrange("p a t -> p (a t)"),
                                   PB[4 + k % 2][:, :]).then_inc(kq_copied, 1)
            act.wait_ge(zeroed, 3)
            for n in range(QP0, VP0):
                lead(n)
                act.wait_ge(piece_done, n + 1)
                src = PB[4 + n % 2]
                if n < QP0 + 4:
                    nc.scalar.copy(qraw[:, n - QP0, :], src[:, 0:T]).then_inc(kq_copied, 1)
                else:
                    h = DIFF_HEADS * 2 + 2 * (n - QP0 - 4)
                    nc.scalar.mul(qz[0:HD, h, :], src[0:HD, 0:T], SCALE)
                    nc.scalar.mul(qz[HD:P, h + 1, :], src[HD:P, 0:T], SCALE).then_inc(kq_copied, 1)
            for g in range(2):
                for n in range(VP0 + 4 * g, VP0 + 4 * g + 4):
                    lead(n)
                act.wait_ge(piece_done, VP0 + 4 * g + 4)
                for tt in range(4):
                    nc.scalar.copy(vN[:, tt, 512 * g:512 * g + 512], PB[tt][:, :]).then_inc(v_copied, 1)

            act.wait_ge(lam_dot, 1)
            nc.scalar.activation(lam[:, 0:2], lam[:, 2:4], ACT.Exp).then_inc(lam_exp, 1)

            def exps(u):
                for k in maps_of[u]:
                    act.wait_ge(max_ready, k + 1)
                    if k >= 4:
                        act.wait_ge(prob_ready, unit_of_map[k - 4] + 1)
                    nc.scalar.activation(prob_e[:, k % 4, :], PB[k % 4][:, :], ACT.Exp,
                                         bias=nmax[:, k % 4:k % 4 + 1],
                                         scale=SCALE if units[u][0] == "d" else 1.0,
                                         accum_out=rsum[:, k % 4:k % 4 + 1]).then_inc(exp_done, 1)

            exps(0)
            for u in range(N_UNITS):
                if u + 1 < N_UNITS:
                    exps(u + 1)
                act.wait_ge(transposed, u + 1)
                head, tile = u // 2, u % 2
                if head >= 2:
                    act.wait_ge(pv_done, head - 1)
                nc.scalar.copy(probT[:, head % 2, :, tile * P:(tile + 1) * P],
                               PB[4 + u % 2][:, :].rearrange("p (c q) -> p c q", c=4)
                               ).then_inc(probT_ready, 1)

            act.wait_ge(att_copied, DIFF_HEADS)
            act.wait_ge(prob_ready, N_UNITS)
            nc.scalar.activation(prob_e[:, 0:2, :].rearrange("p a t -> p (a t)"),
                                 attf[:, 4:8, :].rearrange("p a t -> p (a t)"), ACT.Square).then_inc(dsq_done, 1)
            for b in range(2):
                act.wait_ge(dss_done, b + 1)
                nc.scalar.activation(prob_e[:, 2 + b, :], PB[b][:, :], ACT.Sqrt, bias=epsc[:, 0:1],
                                     scale=1.0 / P).then_inc(dstd_done, 1)
            for c in range(NC):
                act.wait_ge(att_ready, c + 1)
                nc.scalar.copy(tok_hi[:, c, :], attf[:, c, :]).then_inc(tok_hi_ready, 1)

            for n in range(WO0, WQ0):
                lead(n)
            for b in range(4):
                act.wait_ge(piece_done, WO0 + 2 * b + 2)
                if b == 0:
                    act.wait_ge(tok_lo_ready, NC)
                nc.scalar.activation(ysq[:, 2 * b:2 * b + 2, :].rearrange("p a t -> p (a t)"), PB[b][:, :],
                                     ACT.Square).then_inc(ysq_done, 1)
            act.wait_ge(yss_done, 1)
            nc.scalar.activation(rstd[:, 0:T], PB[4][:, 0:T], ACT.Sqrt, bias=epsc[:, 0:1],
                                 scale=1.0 / D).then_inc(ystd_done, 1)
            for c in range(NC):
                act.wait_ge(x1_ready, c + 1)
                nc.scalar.activation(ysq[:, c, :], x1T[:, c, :], ACT.Square).then_inc(x1sq_done, 1)
            act.wait_ge(x1ss_done, 1)
            nc.scalar.activation(rstd[:, 0:T], PB[5][:, 0:T], ACT.Sqrt, bias=epsc[:, 0:1],
                                 scale=1.0 / D).then_inc(x1std_done, 1)
            for c in range(NC):
                act.wait_ge(h2_ready, c + 1)
                nc.scalar.copy(tok_hi[:, c, :], ytmp[:, c, :]).then_inc(tok_hi_ready, 1)

            act.wait_ge(tok_lo_ready, 2 * NC)
            with act.Fori(0, 4) as i:
                for k in range(4):
                    n = WQ0 + 4 * i + k
                    hi_of(n + 2, WQ0 // 4 + i + (k + 2) // 4, (k + 2) % 4)
                    act.wait_ge(piece_done, n + 1)
                    nc.scalar.copy(qT[:, ds(4 * i + k, 1), :].rearrange("p a t -> p (a t)"),
                                   PB[6 + k % 2][:, 0:T]).then_inc(q_copied, 1)
            for g in range(8):
                act.wait_ge(s_done, g + 1)
                nc.scalar.copy(sc[:, 4 * g:4 * g + 4, :].rearrange("p a n -> p (a n)"),
                               PB[g % 4][:, :]).then_inc(s_copied, 1)

            def gelus(first, last):
                with act.Fori(first // 4, last // 4) as i:
                    for k in range(4):
                        n = U0 + 4 * i + k
                        hi_of(n + 2, U0 // 4 + i + (k + 2) // 4, (k + 2) % 4)
                        act.wait_ge(piece_done, n + 1)
                        nc.scalar.activation(act_t[:, ds(4 * i + k, 1), :].rearrange("p a t -> p (a t)"),
                                             PB[k % 2][:, 0:T], ACT.Gelu).then_inc(act_done, 1)

            gelus(0, 100)
            act.wait_ge(best_ready, 1)
            nc.scalar.activation(gate[:, :, :], gate[:, :, :], ACT.Exp).then_inc(gexp_done, 1)
            gelus(100, 108)
            act.wait_ge(slotT_done, 1)
            gelus(108, NK)

            for g in range(6):
                act.wait_ge(final_rows, g + 1)
                dst = (x1n[:, g // 2, (g % 2) * 512:(g % 2 + 1) * 512] if g < 4
                       else ggB[:, (g - 4) * 512:(g - 3) * 512])
                nc.scalar.copy(dst, PB[g][:, :]).then_inc(final_rows_copied, 1)

            act.wait_ge(weighted, T // 4)

            def weight_hi(i, k):
                nc.scalar.copy(w_hi[:, k % 2, :], act_t[:, ds(i, 1), :].rearrange("p a t -> p (a t)")
                               ).then_inc(w_hi_ready, 1)

            weight_hi(0, 0)
            weight_hi(1, 1)
            with act.Fori(0, NK // 4 - 1) as i:
                for k in range(4):
                    n = V0 + 4 * i + k
                    hi_of(n + 2, V0 // 4 + i + (k + 2) // 4, (k + 2) % 4)
                    act.wait_ge(piece_done, n + 1)
                    weight_hi(4 * i + k + 2, k)
            for n in range(PIECES - 4, PIECES - 2):
                lead(n)
                act.wait_ge(piece_done, n + 1)
                weight_hi(n - V0 + 2, n % 4)

            act.wait_ge(piece_done, PIECES)
            for g in range(4):
                nc.scalar.activation(fout[:, g, 0:512], PB[g][:, :], ACT.Square,
                                     accum_out=fin[:, g:g + 1]).then_inc(fsq_done, 1)
            act.wait_ge(fss_ready, 1)
            nc.scalar.activation(fin[:, 6:8], fin[:, 4:6], ACT.Sqrt, bias=epsc[:, 0:1],
                                 scale=1.0 / D).then_inc(fstd_done, 1)

        @block.vector
        def _(dve):
            own = Steps(dve, dve_step)
            v = nc.vector

            def lo_of(m, k):
                dve.wait_ge(hi_ready, m + 1)
                if not (isinstance(m, int) and m < 2):
                    dve.wait_ge(piece_done, m - 1)
                v.tensor_tensor(lo[:, k % 2, :], raw[:, k, :], hi[:, k % 2, :].bitcast(f32),
                                ALU.subtract).then_inc(lo_ready, 1)

            def lead(n):
                if n + 2 < PIECES:
                    lo_of(n + 2, (n + 2) % 4)

            v.memset(cS[:, :, :], 0.0).then_inc(zeroed, 1)
            v.memset(epsc[:, :], EPS).then_inc(zeroed, 1)
            v.memset(qz[:, :, :], 0.0).then_inc(zeroed, 1)
            lo_of(0, 0)
            lo_of(1, 1)
            dve.wait_ge(std_done, 1)
            own.link(v.reciprocal(rstd[:, :], rstd[:, :]))
            for c in range(NC):
                own.add(v.tensor_tensor(xn[:, c, :], xT[:, c, :], rstd[:, :], ALU.mult))
            own.wait()

            def modulation(first, last):
                own.link(v.tensor_tensor(mod[:, first:last, :],
                                         PB[2][:, 2 * first:2 * last].rearrange("p (c m) -> p c m", m=2),
                                         small[:, S_B + first:S_B + last, None].to_broadcast([P, last - first, 2]),
                                         ALU.add))

            def ada_rows(b):
                dve.wait_ge(ada_used, b + 1)
                if b >= 2:
                    dve.wait_ge(mod_summed, b - 1)
                v.tensor_copy(rows[:, b % 2, :], PB[b % 2][:, 0:ADA_N]).then_inc(rows_ready, 1)

            for b in range(ADA_FIRST):
                ada_rows(b)
            dve.wait_ge(mod_summed, ADA_FIRST)
            dve.wait_ge(small_loaded, 16)
            modulation(SH1, GT1)
            own.link(v.scalar_tensor_tensor(gs[:, 0, :, :], mod[:, SC1:SC1 + NC, :], 1.0,
                                            small[:, S_G:S_G + NC, None].to_broadcast([P, NC, 2]),
                                            ALU.add, ALU.mult))
            for c in range(NC):
                for s in range(2):
                    cols = xn[:, c, s * T:(s + 1) * T]
                    ins = v.tensor_scalar(cols, cols, gs[:, 0, c, s:s + 1], mod[:, SH1 + c, s:s + 1],
                                          ALU.mult, ALU.add)
                ins.then_inc(h_ready, 1)
            for c in range(NC):
                dve.wait_ge(h_ready, c + 1)
                dve.wait_ge(h_hi_ready, c + 1)
                v.tensor_tensor(h_lo[:, c, :], xn[:, c, :], h_hi[:, c, :].bitcast(f32),
                                ALU.subtract).then_inc(h_lo_ready, 1)

            with dve.Fori(0, VP0 // 4) as i:
                for k in range(4):
                    lo_of(4 * i + k + 2, (k + 2) % 4)
            for n in range(VP0, WO0):
                lead(n)

            def rope(g):
                for e in range(2):
                    j = 2 * (g % 2) + e
                    src = kT[:, j, 0:T] if g < 2 else qraw[:, j, :]
                    t1, t2 = rows[:, 0, :], rows[:, 1, :]
                    if e == 0:
                        dve.wait_ge(swapped, g + 1)
                    own.add(v.tensor_tensor(t1, src, tab[:, R_COS:R_COS + T], ALU.mult))
                    own.link(v.tensor_tensor(t2, PB[4 + g][:, e * T:(e + 1) * T], tab[:, R_SIN:R_SIN + T], ALU.mult))
                    if g < 2:
                        last = v.tensor_tensor(src, t1, t2, ALU.add)
                    else:
                        v.tensor_tensor(qz[0:HD, 2 * j, :], t1[0:HD, :], t2[0:HD, :], ALU.add)
                        last = v.tensor_tensor(qz[HD:P, 2 * j + 1, :], t1[HD:P, :], t2[HD:P, :], ALU.add)
                    own.link(last)
                return last

            dve.wait_ge(tab_loaded, 16)
            dve.wait_ge(kq_copied, 12)
            for g in range(4):
                rope(g)
            v.memset(fin[:, 15:16], 0.0).then_inc(roped, 1)

            for b in range(ADA_FIRST, ADA_BLOCKS):
                ada_rows(b)
            dve.wait_ge(mod_summed, ADA_BLOCKS)
            modulation(GT1, NMOD * NC)
            own.add(v.scalar_tensor_tensor(gs[:, 1, :, :], mod[:, SC2:SC2 + NC, :], 1.0,
                                           small[:, S_G + 2 * NC:S_G + 3 * NC, None].to_broadcast([P, NC, 2]),
                                           ALU.add, ALU.mult))
            own.add(v.tensor_tensor(gg[:, 0, :], mod[:, GT1:GT1 + NC, 0], small[:, S_G + NC:S_G + 2 * NC], ALU.mult))
            v.tensor_tensor(gg[:, 1, :], mod[:, GT2:GT2 + NC, 0], small[:, S_G + 3 * NC:S_G + 4 * NC],
                            ALU.mult).then_inc(mod_ready, 1)

            pairs = tab[:, R_LAM:R_LAM + 4 * HD].rearrange("p (a b d) -> p a b d", a=2, b=2)
            own.link(v.tensor_tensor(lamt[:, :, :], pairs[:, :, 0, :], pairs[:, :, 1, :], ALU.mult))
            v.tensor_reduce(lam[:, 2:4], lamt[:, :, :], AX, ALU.add).then_inc(lam_dot, 1)
            dve.wait_ge(lam_exp, 1)
            own.link(v.tensor_tensor(lam[:, 2:3], lam[:, 1:2], lam[:, 0:1], ALU.subtract))
            own.link(v.tensor_scalar(lam[:, 2:3], lam[:, 2:3], -LAMBDA_INIT, None, ALU.add))

            def maxima(u):
                for k in maps_of[u]:
                    dve.wait_ge(scored, k + 1)
                    if units[u][0] == "d":
                        own.link(v.tensor_reduce(mraw[:, k % 4:k % 4 + 1], PB[k % 4][:, :], AX, ALU.max, negate=True))
                        v.tensor_scalar(nmax[:, k % 4:k % 4 + 1], mraw[:, k % 4:k % 4 + 1], SCALE, None,
                                        ALU.mult).then_inc(max_ready, 1)
                    else:
                        v.tensor_reduce(nmax[:, k % 4:k % 4 + 1], PB[k % 4][:, :], AX, ALU.max,
                                        negate=True).then_inc(max_ready, 1)

            def probabilities(u):
                ks = [k % 4 for k in maps_of[u]]
                dve.wait_ge(exp_done, maps_of[u][-1] + 1)
                if u >= 2:
                    dve.wait_ge(transposed, u - 1)
                for k in ks:
                    own.add(v.reciprocal(rinv[:, k:k + 1], rsum[:, k:k + 1]))
                own.wait()
                if units[u][0] == "d":
                    a, b = ks
                    own.link(v.tensor_tensor(rinv[:, b:b + 1], rinv[:, b:b + 1], lam[:, 2:3], ALU.mult))
                    own.link(v.tensor_scalar(prob_e[:, b, :], prob_e[:, b, :], rinv[:, b:b + 1], None, ALU.mult))
                    v.scalar_tensor_tensor(prob[:, u % 2, :], prob_e[:, a, :], rinv[:, a:a + 1], prob_e[:, b, :],
                                           ALU.mult, ALU.add).then_inc(prob_ready, 1)
                else:
                    a, = ks
                    v.tensor_scalar(prob[:, u % 2, :], prob_e[:, a, :], rinv[:, a:a + 1], None,
                                    ALU.mult).then_inc(prob_ready, 1)

            def copy_head(head):
                dve.wait_ge(pv_done, head + 1)
                if head < DIFF_HEADS:
                    dst, src = attf[:, 4 + head, :], PB[6 + head % 2][:, 0:T]
                else:
                    h = head - DIFF_HEADS
                    part = slice(HD * (h % 2), HD * (h % 2) + HD)
                    dst, src = attf[part, h // 2, :], PB[6 + head % 2][part, 0:T]
                v.tensor_copy(dst, src).then_inc(att_copied, 1)

            maxima(0)
            for u in range(N_UNITS):
                if u + 1 < N_UNITS:
                    maxima(u + 1)
                probabilities(u)
                if u >= 3 and u % 2:
                    copy_head((u - 3) // 2)
            copy_head(N_AHEADS - 1)

            dve.wait_ge(att_copied, N_AHEADS)
            for c in range(4):
                v.engine_nop().then_inc(att_ready, 1)
            for b in range(2):
                dve.wait_ge(dstd_done, b + 1)
                std = prob_e[:, 2 + b, :]
                own.link(v.reciprocal(std, std))
                two = attf[:, 4 + 2 * b:6 + 2 * b, :].rearrange("p a t -> p (a t)")
                own.link(v.tensor_tensor(two, two, std, ALU.mult))
                v.tensor_scalar(two, two, small[:, S_LN:S_LN + 1], 1.0 - LAMBDA_INIT, ALU.mult,
                                ALU.mult).then_inc(att_ready, 2)
            for c in range(NC):
                dve.wait_ge(att_ready, c + 1)
                dve.wait_ge(tok_hi_ready, c + 1)
                v.tensor_tensor(tok_lo[:, c, :], attf[:, c, :], tok_hi[:, c, :].bitcast(f32),
                                ALU.subtract).then_inc(tok_lo_ready, 1)
            for n in range(WO0, WQ0):
                lead(n)

            dve.wait_ge(ystd_done, 1)
            own.link(v.reciprocal(rstd[:, 0:T], rstd[:, 0:T]))
            for b in range(4):
                own.link(v.tensor_tensor(ytmp[:, 2 * b:2 * b + 2, :], PB[b][:, :].rearrange("p (a t) -> p a t", a=2),
                                         rstd[:, None, 0:T].to_broadcast([P, 2, T]), ALU.mult))
                for c in (2 * b, 2 * b + 1):
                    v.scalar_tensor_tensor(x1T[:, c, :], ytmp[:, c, :], gg[:, 0, c:c + 1], xT[:, c, 0:T],
                                           ALU.mult, ALU.add).then_inc(x1_ready, 1)
            dve.wait_ge(x1std_done, 1)
            own.link(v.reciprocal(rstd[:, 0:T], rstd[:, 0:T]))
            for c in range(NC):
                own.link(v.tensor_tensor(ytmp[:, c, :], x1T[:, c, :], rstd[:, 0:T], ALU.mult))
                v.tensor_scalar(ytmp[:, c, :], ytmp[:, c, :], gs[:, 1, c, 0:1], mod[:, SH2 + c, 0:1],
                                ALU.mult, ALU.add).then_inc(h2_ready, 1)
            for c in range(NC):
                dve.wait_ge(h2_ready, c + 1)
                dve.wait_ge(tok_hi_ready, NC + c + 1)
                v.tensor_tensor(tok_lo[:, c, :], ytmp[:, c, :], tok_hi[:, c, :].bitcast(f32),
                                ALU.subtract).then_inc(tok_lo_ready, 1)

            with dve.Fori(WQ0 // 4, U0 // 4) as i:
                for k in range(4):
                    lo_of(4 * i + k + 2, (k + 2) % 4)

            def top16(values, scratch):
                own.link_drained(v.max(m16[:, 0:8], values))
                own.add(v.max_index(i16[:, 0:8], m16[:, 0:8], values))
                own.link_drained(v.match_replace(scratch, m16[:, 0:8], values, REMOVED))
                own.link_drained(v.max(m16[:, 8:16], scratch))
                own.link(v.max_index(i16[:, 8:16], m16[:, 8:16], scratch))

            dve.wait_ge(s_copied, 8)
            with repeat(dve, 8, own, 4 * 8) as i:
                for k in range(4):
                    lo_of(U0 + 4 * i + k + 2, (k + 2) % 4)
                    row = 4 * i + k
                    own.link_drained(v.tensor_copy(work[:, 0, :], sc[:, ds(row, 1), :].rearrange("p a n -> p (a n)")))
                    top16(work[:, 0, :], work[:, 1, :])
                    own.add(v.tensor_copy(sv[:, ds(row, 1), :].rearrange("p a n -> p (a n)"), m16[:, :]))
                    own.link(v.tensor_copy(si[:, ds(row, 1), :].rearrange("p a n -> p (a n)"), i16[:, :]))
            for tile in range(2):
                with repeat(dve, PH, own, 13) as h:
                    n = U0 + 32 + 32 * tile + 4 * h
                    row = 16 * tile + 2 * h
                    lo_of(n + 2, 2)
                    first = sv[:, ds(row, 1), :].rearrange("p a n -> p (a n)")
                    second = sv[:, ds(row + 1, 1), :].rearrange("p a n -> p (a n)")
                    own.link_drained(v.tensor_tensor(cand[:, 0, :].rearrange("p (a b) -> p a b", b=TOPK),
                                             first[:, :, None].to_broadcast([P, TOPK, TOPK]),
                                             second[:, None, :].to_broadcast([P, TOPK, TOPK]), ALU.add))
                    top16(cand[:, 0, :], cand[:, 1, :])
                    lo_of(n + 3, 3)
                    own.add(v.tensor_copy(best[:, tile, ds(h, 1), :].rearrange("p a n -> p (a n)"), m16[:, :]))
                    own.add(v.tensor_scalar(ab[:, 0, :], i16[:, :], 4, None, ALU.logical_shift_right))
                    own.link(v.tensor_scalar(ab[:, 1, :], i16[:, :], TOPK - 1, None, ALU.bitwise_and))
                    own.link(v.tensor_copy(abf[:, :, :], ab[:, :, :]))
                    own.link(v.tensor_tensor(eq[:, :, :, :], abf[:, :, :, None].to_broadcast([P, 2, TOPK, TOPK]),
                                             iota16[:, None, None, :].to_broadcast([P, 2, TOPK, TOPK]), ALU.is_equal))
                    lo_of(n + 4, 0)
                    own.link(v.tensor_tensor(eq[:, :, :, :], eq[:, :, :, :],
                                             si[:, ds(row, 2), None, :].to_broadcast([P, 2, TOPK, TOPK]), ALU.mult))
                    own.link(v.tensor_reduce(ijs[:, tile, :, ds(h, 1), :].rearrange("p s a n -> p s (a n)"),
                                             eq[:, :, :, :], AX, ALU.add))
                    lo_of(n + 5, 1)
            all_best = best[:, :, :, :].rearrange("p t h k -> p (t h) k")
            v.tensor_tensor(gate[:, :, :], all_best, all_best[:, :, 0:1].to_broadcast([P, 2 * PH, TOPK]),
                            ALU.subtract).then_inc(best_ready, 1)
            for n in range(U0 + 96, U0 + 100):
                lead(n)
            dve.wait_ge(gexp_done, 1)
            own.link(v.tensor_reduce(gsum[:, :], gate[:, :, :], AX, ALU.add))
            own.link(v.reciprocal(gsum[:, :], gsum[:, :]))
            v.tensor_tensor(gate[:, :, :], gate[:, :, :], gsum[:, :, None].to_broadcast([P, 2 * PH, TOPK]),
                            ALU.mult).then_inc(gate_ready, 1)
            for n in range(U0 + 100, U0 + 104):
                lead(n)
            dve.wait_ge(slotT_done, 1)
            for s in range(3):
                src = PB[2] if s < 2 else PB[3]
                v.tensor_copy(slot[:, s, :], src[:, (s % 2) * T:(s % 2 + 1) * T]).then_inc(slot_ready, 1)
            with dve.Fori((U0 + 104) // 4, V0 // 4) as i:
                for k in range(4):
                    lo_of(4 * i + k + 2, (k + 2) % 4)

            def gate_rows(q, half):
                for e in range(4):
                    v.tensor_scalar(ghj[:, 4 * half + e, :], iota, slot[:, 1, ds(4 * q + e, 1)],
                                    slot[:, 2, ds(4 * q + e, 1)], ALU.is_equal, ALU.mult).then_inc(ghj_ready, 1)

            def weigh(q, half):
                dve.wait_ge(gate_done, q + 1)
                cells = act_t[:, :, ds(4 * q, 4)].rearrange("p i t -> p t i")
                v.tensor_tensor(cells, PB[6 + half][:, :].rearrange("p (t i) -> p t i", t=4), cells,
                                ALU.mult).then_inc(weighted, 1)

            dve.wait_ge(slot_ready, 3)
            dve.wait_ge(act_done, NK)
            gate_rows(0, 0)
            gate_rows(1, 1)
            with dve.Fori(0, T // 8 - 1) as i:
                for half in range(2):
                    q = 2 * i + half
                    weigh(q, half)
                    gate_rows(q + 2, half)
            weigh(T // 4 - 2, 0)
            weigh(T // 4 - 1, 1)

            def weight_lo(i, k):
                dve.wait_ge(w_hi_ready, i + 1)
                v.tensor_tensor(w_lo[:, k % 2, :], act_t[:, ds(i, 1), :].rearrange("p a t -> p (a t)"),
                                w_hi[:, k % 2, :].bitcast(f32), ALU.subtract).then_inc(w_lo_ready, 1)

            dve.wait_ge(weighted, T // 4)
            weight_lo(0, 0)
            weight_lo(1, 1)
            with dve.Fori(0, NK // 4 - 1) as i:
                for k in range(4):
                    lo_of(V0 + 4 * i + k + 2, (k + 2) % 4)
                    dve.wait_ge(piece_done, V0 + 4 * i + k + 1)
                    weight_lo(4 * i + k + 2, k)
            for n in range(PIECES - 4, PIECES - 2):
                lead(n)
                dve.wait_ge(piece_done, n + 1)
                weight_lo(n - V0 + 2, n % 4)

            dve.wait_ge(fsq_done, 4)
            sums = fin[:, 0:4].rearrange("p (t h) -> p t h", h=2)
            v.tensor_tensor(fin[:, 4:6], sums[:, :, 0], sums[:, :, 1], ALU.add).then_inc(fss_ready, 1)
            dve.wait_ge(fstd_done, 1)
            own.link(v.reciprocal(fin[:, 8:10], fin[:, 6:8]))
            for g in range(4):
                half = slice((g % 2) * 512, (g % 2 + 1) * 512)
                own.link(v.scalar_tensor_tensor(fout[:, g, 0:512], PB[g][:, :], fin[:, 8 + g // 2:9 + g // 2],
                                                ggB[:, half], ALU.mult, ALU.mult))
                v.tensor_tensor(fout[:, g, 0:512], fout[:, g, 0:512], x1n[:, g // 2, half],
                                ALU.add).then_inc(out_ready, 1)

        @block.tensor
        def _(pe):
            mm = nc.tensor.matmul
            hi_c = hi[:, :, :].rearrange("p s (c n) -> p s c n", n=P)
            lo_c = lo[:, :, :].rearrange("p s (c n) -> p s c n", n=P)

            def weights_piece(n, k, right_hi, right_lo, out):
                pe.wait_ge(hi_ready, n + 1)
                for c in range(NC):
                    mm(out, hi_c[:, k % 2, c, :], right_hi[:, c, :], start=(c == 0), stop=False)
                    last = mm(out, hi_c[:, k % 2, c, :], right_lo[:, c, :], start=False, stop=False)
                last.then_inc(hi_used, 1)
                pe.wait_ge(lo_ready, n + 1)
                for c in range(NC):
                    last = mm(out, lo_c[:, k % 2, c, :], right_hi[:, c, :], start=False, stop=(c == NC - 1))
                last.then_inc(piece_done, 1)

            pe.wait_ge(cst_loaded, 16)
            for c in range(NC):
                pe.wait_ge(xsq_done, c // 2 + 1)
                last = mm(PB[3][:, :], ones, xsq[:, c, :], start=(c == 0), stop=(c == NC - 1))
            last.then_inc(xss_done, 1)

            def ada_block(b, k):
                pe.wait_ge(ada_loaded[k], 16 * (b // 4 + 1))
                if b >= 2:
                    pe.wait_ge(rows_ready, b - 1)
                for c in range(NC):
                    g = c % 4
                    last = mm(PB[b % 2][32 * g:32 * g + 32, 0:ADA_N], cS[:, c, :], ada[:, k, c, :],
                              start=(c < 4), stop=(c >= 4))
                last.then_inc(ada_used, 1)

            def ada_sum(b):
                pe.wait_ge(rows_ready, b + 1)
                for e in range(ADA_N // P):
                    col = 2 * (b * (ADA_N // P) + e)
                    last = mm(PB[2][:, col:col + 2], rows[:, b % 2, e * P:(e + 1) * P], sel, start=True, stop=True)
                last.then_inc(mod_summed, 1)

            def ada_blocks(first, last):
                for b in range(first, last):
                    ada_block(b, b % 4)
                    if b > first:
                        ada_sum(b - 1)
                ada_sum(last - 1)

            pe.wait_ge(silu_done, 1)
            ada_blocks(0, ADA_FIRST)

            pe.wait_ge(h_hi_ready, NC)
            pe.wait_ge(h_lo_ready, NC)
            for n in range(2):
                weights_piece(n, n, h_hi[:, :, :], h_lo[:, :, :], PB[4 + n][:, :])
            with pe.Fori(1, QP0 // 2) as i:
                for k in range(2):
                    pe.wait_ge(kq_copied, 2 * i + k - 1)
                    weights_piece(2 * i + k, k, h_hi[:, :, :], h_lo[:, :, :], PB[4 + k][:, :])
            with pe.Fori(QP0 // 2, VP0 // 2) as i:
                for k in range(2):
                    pe.wait_ge(kq_copied, 2 * i + k - 1)
                    weights_piece(2 * i + k, k, h_hi[:, :, 0:T], h_lo[:, :, 0:T], PB[4 + k][:, 0:T])
            for g in range(2):
                for p in range(4):
                    n = VP0 + 4 * g + p
                    wide = [t[:, n % 2, :].rearrange("p (c n) -> p c n", c=2) for t in (hi, lo)]
                    pe.wait_ge(hi_ready, n + 1)
                    for tt in range(4):
                        if p == 0 and g:
                            pe.wait_ge(v_copied, tt + 1)
                        for e in range(2):
                            c = 2 * p + e
                            mm(PB[tt][:, :], h_hi[:, c, tt * P:(tt + 1) * P], wide[0][:, e, :],
                               start=(c == 0), stop=False)
                            last = mm(PB[tt][:, :], h_lo[:, c, tt * P:(tt + 1) * P], wide[0][:, e, :],
                                      start=False, stop=False)
                    last.then_inc(hi_used, 1)
                    pe.wait_ge(lo_ready, n + 1)
                    for tt in range(4):
                        for e in range(2):
                            c = 2 * p + e
                            last = mm(PB[tt][:, :], h_hi[:, c, tt * P:(tt + 1) * P], wide[1][:, e, :],
                                      start=False, stop=(c == NC - 1))
                    last.then_inc(piece_done, 1)

            pe.wait_ge(kq_copied, 16)
            for g in range(4):
                for e in range(2):
                    j = 2 * (g % 2) + e
                    last = mm(PB[4 + g][:, e * T:(e + 1) * T], perm, kT[:, j, 0:T] if g < 2 else qraw[:, j, :],
                              start=True, stop=True)
                last.then_inc(swapped, 1)
            pe.wait_ge(v_copied, 8)
            ada_blocks(ADA_FIRST, ADA_BLOCKS)

            def scores(u):
                kind, head, tile = units[u]
                for m, k in enumerate(maps_of[u]):
                    if k >= 4:
                        pe.wait_ge(exp_done, k - 3)
                    out = PB[k % 4]
                    if kind == "d":
                        flat = m * DIFF_HEADS + head
                        chunk, q = flat // 2, flat
                    else:
                        chunk, q = 4 + head // 2, 2 * DIFF_HEADS + head
                    left = qz[:, q, tile * P:(tile + 1) * P]
                    if kind == "d":
                        last = mm(out[:, :], left, kT[:, chunk, :], start=True, stop=True)
                    else:
                        mm(out[:, T:LC], left, kT[:, chunk, T:LC], start=True, stop=True)
                        mm(out[:, 0:T], left, kT[:, chunk, 0:T], start=True, stop=False)
                        pe.wait_ge(bias_ready, 1)
                        last = mm(out[:, 0:T], ident, bias[:, 2 * head + tile, :], start=False, stop=True)
                    last.then_inc(scored, 1)

            def attend(head):
                pe.wait_ge(probT_ready, 2 * head + 2)
                if head >= 2:
                    pe.wait_ge(att_copied, head - 1)
                for kc in range(4):
                    if head < DIFF_HEADS:
                        left = vN[:, kc, 512 + P * head:512 + P * (head + 1)]
                        out = PB[6 + head % 2][:, 0:T]
                    else:
                        h = head - DIFF_HEADS
                        left = vN[:, kc, HD * h:HD * (h + 1)]
                        out = PB[6 + head % 2][HD * (h % 2):HD * (h % 2) + HD, 0:T]
                    last = mm(out, left, probT[:, head % 2, kc, :], start=(kc == 0), stop=(kc == 3))
                last.then_inc(pv_done, 1)

            pe.wait_ge(roped, 1)
            pe.wait_ge(mod_ready, 1)
            scores(0)
            scores(1)
            for u in range(N_UNITS):
                if u + 2 < N_UNITS:
                    scores(u + 2)
                pe.wait_ge(prob_ready, u + 1)
                if u >= 2:
                    pe.wait_ge(probT_ready, u - 1)
                for kc in range(4):
                    last = nc.tensor.transpose(PB[4 + u % 2][:, kc * P:(kc + 1) * P],
                                               prob[:, u % 2, kc * P:(kc + 1) * P], ident)
                last.then_inc(transposed, 1)
                if u >= 2 and u % 2 == 0:
                    attend(u // 2 - 1)
            attend(N_AHEADS - 1)
            pe.wait_ge(dsq_done, 1)
            pe.wait_ge(exp_done, maps_of[-1][-1] + 1)
            for b in range(2):
                mm(PB[b][:, :], ones, prob_e[:, b, :], start=True, stop=True).then_inc(dss_done, 1)

            pe.wait_ge(tok_hi_ready, NC)
            pe.wait_ge(tok_lo_ready, NC)
            for n in range(WO0, WQ0):
                j = n - WO0
                weights_piece(n, n, tok_hi[:, :, :], tok_lo[:, :, :], PB[j // 2][:, (j % 2) * T:(j % 2 + 1) * T])
            for c in range(NC):
                pe.wait_ge(ysq_done, c // 2 + 1)
                last = mm(PB[4][:, 0:T], ones, ysq[:, c, :], start=(c == 0), stop=(c == NC - 1))
            last.then_inc(yss_done, 1)
            for c in range(NC):
                pe.wait_ge(x1sq_done, c + 1)
                last = mm(PB[5][:, 0:T], ones, ysq[:, c, :], start=(c == 0), stop=(c == NC - 1))
            last.then_inc(x1ss_done, 1)

            pe.wait_ge(tok_hi_ready, 2 * NC)
            pe.wait_ge(tok_lo_ready, 2 * NC)
            for k in range(2):
                weights_piece(WQ0 + k, k, tok_hi[:, :, :], tok_lo[:, :, :], PB[6 + k][:, 0:T])
            with pe.Fori(1, 8) as i:
                for k in range(2):
                    pe.wait_ge(q_copied, 2 * i + k - 1)
                    weights_piece(WQ0 + 2 * i + k, k, tok_hi[:, :, :], tok_lo[:, :, :], PB[6 + k][:, 0:T])
            pe.wait_ge(q_copied, 16)
            pe.wait_ge(keys_loaded, 16)
            for g in range(8):
                if g >= 4:
                    pe.wait_ge(s_copied, g - 3)
                for e in range(4):
                    row = 4 * g + e
                    tile, hp = row // 16, row % 16
                    last = mm(PB[g % 4][:, e * NK:(e + 1) * NK], qT[:, hp, tile * P:(tile + 1) * P],
                              keys[:, hp, :], start=True, stop=True)
                last.then_inc(s_done, 1)

            def expert_rows(first, last):
                with pe.Fori(first // 2, last // 2) as i:
                    for k in range(2):
                        pe.wait_ge(act_done, 2 * i + k - 1)
                        weights_piece(U0 + 2 * i + k, k, tok_hi[:, :, :], tok_lo[:, :, :], PB[k][:, 0:T])

            pe.wait_ge(s_copied, 8)
            for k in range(2):
                weights_piece(U0 + k, k, tok_hi[:, :, :], tok_lo[:, :, :], PB[k][:, 0:T])
            expert_rows(2, 104)
            pe.wait_ge(gate_ready, 1)
            for s in range(3):
                for tile in range(2):
                    if s < 2:
                        src = ijs[:, tile, s, :, :].rearrange("p h k -> p (h k)")
                    else:
                        src = gate[:, tile * PH:(tile + 1) * PH, :].rearrange("p h k -> p (h k)")
                    out = (PB[2] if s < 2 else PB[3])[:, (s % 2) * T + tile * P:(s % 2) * T + (tile + 1) * P]
                    last = nc.tensor.transpose(out, src, ident)
            last.then_inc(slotT_done, 1)
            expert_rows(104, NK)

            pe.wait_ge(act_done, NK)
            pe.wait_ge(slot_ready, 3)
            for g in range(4):
                for e in range(4):
                    c = 4 * (g % 2) + e
                    last = nc.tensor.transpose(PB[g][:, e * P:(e + 1) * P],
                                               x1T[:, c, (g // 2) * P:(g // 2 + 1) * P], ident)
                last.then_inc(final_rows, 1)
            for g in range(2):
                for e in range(4):
                    c = 4 * g + e
                    last = mm(PB[4 + g][:, e * P:(e + 1) * P], gg[:, 1, c:c + 1].to_broadcast([P, P]), ident,
                              start=True, stop=True)
                last.then_inc(final_rows, 1)

            def gate_quad(q, half):
                for e in range(4):
                    pe.wait_ge(ohi_ready, 4 * q + e + 1)
                    pe.wait_ge(ghj_ready, 4 * q + e + 1)
                    last = mm(PB[6 + half][:, e * NK:(e + 1) * NK], ghj[:, 4 * half + e, :],
                              ohi[:, 4 * half + e, :], start=True, stop=True)
                last.then_inc(gate_done, 1)

            gate_quad(0, 0)
            gate_quad(1, 1)
            with pe.Fori(1, T // 8) as i:
                for half in range(2):
                    pe.wait_ge(weighted, 2 * i + half - 1)
                    gate_quad(2 * i + half, half)

            pe.wait_ge(final_rows_copied, 4)

            def value_piece(n, i, k, first=False, final=False):
                wide = [t[:, k, :].rearrange("p (c n) -> p c n", c=2) for t in (hi, lo)]
                pe.wait_ge(hi_ready, n + 1)
                pe.wait_ge(w_hi_ready, i + 1)
                pe.wait_ge(w_lo_ready, i + 1)
                for tt in range(2):
                    for w in (w_hi, w_lo):
                        for e in range(2):
                            last = mm(PB[2 * tt + e][:, :], w[:, k, tt * P:(tt + 1) * P], wide[0][:, e, :],
                                      start=first and w is w_hi, stop=False)
                last.then_inc(hi_used, 1)
                pe.wait_ge(lo_ready, n + 1)
                for tt in range(2):
                    for e in range(2):
                        last = mm(PB[2 * tt + e][:, :], w_hi[:, k, tt * P:(tt + 1) * P], wide[1][:, e, :],
                                  start=False, stop=final)
                last.then_inc(piece_done, 1)

            value_piece(V0, 0, 0, first=True)
            value_piece(V0 + 1, 1, 1)
            with pe.Fori(1, NK // 2 - 1) as i:
                for k in range(2):
                    value_piece(V0 + 2 * i + k, 2 * i + k, k)
            value_piece(PIECES - 2, NK - 2, 0)
            value_piece(PIECES - 1, NK - 1, 1, final=True)


def constants():
    import numpy as np
    cst = np.zeros((P, C_END), np.float32)
    cst[:, C_ID:C_ID + P] = np.eye(P)
    cst[:, C_ONE:C_ONE + P] = 1.0
    cst[:, C_IOTA:C_IOTA + P] = np.arange(P)
    cst[np.arange(P), C_PERM + (np.arange(P) ^ 1)] = 1.0
    for g in range(4):
        for m in range(2):
            cst[32 * g + m, C_SEL + m] = 1.0
    cst[:, C_I16:C_I16 + TOPK] = np.arange(TOPK)
    t = np.arange(T)
    freq = np.float32(10000.0) ** (-np.arange(HD // 4, dtype=np.float32) / (HD // 4))
    row, col = (t // GRID_W).astype(np.float32), (t % GRID_W).astype(np.float32)
    ang = np.concatenate([row[:, None] * freq, col[:, None] * freq], axis=-1)
    d = np.arange(P) % HD
    cos, sin = np.cos(ang)[:, d // 2].T, np.sin(ang)[:, d // 2].T
    tab = np.zeros((P, R_LAM), np.float32)
    tab[:, R_COS:R_COS + T] = cos
    tab[:, R_SIN:R_SIN + T] = np.where(d % 2 == 0, -1.0, 1.0)[:, None] * sin
    c = np.arange(P) % GRID_W
    start = np.clip(c - WIN_C // 2, 0, GRID_W - WIN_C)
    kc = np.arange(T) % GRID_W
    inside = (kc[None, :] >= start[:, None]) & (kc[None, :] < start[:, None] + WIN_C)
    tab[:, R_MASK:R_MASK + T] = np.where(inside, 0.0, MASKED)
    return cst, tab


def kernel(**inputs):
    import numpy as np
    import concourse.bacc as bacc
    from concourse.bass_utils import run_bass_kernel_spmd

    a = {k: np.asarray(x) for k, x in inputs.items()}

    def columns(w):
        return w.reshape(NC, P, -1, P).transpose(2, 1, 0, 3).reshape(-1, P, PW)

    def wide(w):
        return w.reshape(4, 2, P, 512).transpose(0, 2, 1, 3).reshape(4, P, PW)

    w_in = a["w_in"][0]
    qa, ka, va, qd, kd, vd = (w_in[:, 512 * k:512 * (k + 1)] for k in range(6))
    u = a["peer_u"][0].reshape(NK, P, NC, P).transpose(0, 3, 2, 1).reshape(NK, P, PW)
    stream = np.concatenate([columns(kd), columns(ka), columns(qd), columns(qa), wide(va), wide(vd),
                             columns(a["w_out"][0]), columns(a["peer_wq"][0]), u,
                             a["peer_v"][0].reshape(NK, P, PW)])
    tokens = np.concatenate([a["x"][0], a["ctx"][0]])
    cond = np.stack([a["c"][0], a["c_ctx"]])
    cst, tab = constants()
    t = np.arange(T)
    r_off = t[None, :] // GRID_W - t[:, None] // GRID_W + WIN_R - 1
    c_off = np.clip(t[None, :] % GRID_W - t[:, None] % GRID_W + WIN_C - 1, 0, 2 * WIN_C - 2)
    bias = a["na_rel_bias"][0][:, r_off, c_off].reshape(NA_HEADS, 2, P, T)
    arrays = {
        "xT": tokens.T.reshape(NC, P, LC).transpose(1, 0, 2),
        "cT": cond.T.reshape(NC, P, 2).transpose(1, 0, 2),
        "cst": cst,
        "small": np.concatenate([a["b_ada"][0].reshape(-1, P).T, a["g_norm"][0].reshape(-1, P).T,
                                 a["diff_subln"][0][:, None]], axis=1),
        "tab": np.concatenate([tab, np.broadcast_to(a["diff_lambda"][0].reshape(1, -1), (P, 4 * HD))], axis=1),
        "ada": a["w_ada"][0].reshape(NC, P, ADA_BLOCKS, ADA_N).transpose(2, 1, 0, 3).reshape(ADA_BLOCKS, P, -1),
        "bias": bias.transpose(2, 0, 1, 3).reshape(P, 16, T),
        "keys": a["peer_keys"][0].reshape(16, NK, P).transpose(2, 0, 1),
        "stream": stream,
    }
    arrays = {f"in_{k}": np.ascontiguousarray(x) for k, x in arrays.items()}
    nc = bacc.Bacc("TRN2", target_bir_lowering=False, num_devices=1)
    args = [nc.dram_tensor(k, x.shape, mybir.dt.float32, kind="ExternalInput").ap() for k, x in arrays.items()]
    out = nc.dram_tensor("out_dram", (1, T, D), mybir.dt.float32, kind="ExternalOutput").ap()
    program(nc, *args, out)
    got = run_bass_kernel_spmd(nc, [arrays], core_ids=[0])
    return got.results[0]["out_dram"]
```

```python
import concourse.bass as bass
from concourse import mybir
from contextlib import ExitStack, contextmanager

D = 1024
T = 256
CTX = 256
LC = T + CTX
P = 128
NC = D // P
HD = 64
GRID_W = 64
WIN_C = 16
WIN_R = 8
NA_HEADS = 8
DIFF_HEADS = 4
LAMBDA_INIT = 0.2
EPS = 1e-6
SCALE = HD ** -0.5
PH = 8
NK = 128
TOPK = 16
NMOD = 6
MASKED = -1e30
POOL_HOT = 2
REMOVED = -3.0e38
PW = 1024

KP0, QP0, VP0, WO0, WQ0, U0, V0 = 0, 8, 16, 24, 32, 48, 176
PIECES = 304
ADA_N = 256
ADA_BLOCKS = NMOD * D // ADA_N
ADA_FIRST = 2 * D // ADA_N
SH1, SC1, GT1, SH2, SC2, GT2 = (k * NC for k in range(NMOD))

C_ID, C_ONE, C_IOTA, C_PERM, C_SEL, C_I16, C_END = 0, 128, 256, 384, 512, 514, 530
S_B, S_G, S_LN, S_END = 0, 48, 80, 81
R_COS, R_SIN, R_MASK, R_LAM, R_END = 0, 256, 512, 768, 1024


class Steps:

    def __init__(self, eng, sem):
        self.eng, self.sem, self.n, self.local = eng, sem, 0, 0

    def add(self, ins):
        ins.then_inc(self.sem, 1)
        self.n = self.n + 1
        self.local += 1

    def wait(self):
        self.eng.wait_ge(self.sem, self.n)

    def link(self, ins):
        self.add(ins)
        self.wait()

    def drained(self):
        self.eng.drain()


@contextmanager
def repeat(eng, times, steps, per_time):
    base, local = steps.n, steps.local
    with eng.Fori(0, times) as i:
        steps.n = base + i * per_time
        yield i
    assert steps.local - local == per_time, (steps.local - local, per_time)
    steps.n = base + times * per_time


def program(nc, xT_d, cT_d, cst_d, small_d, tab_d, ada_d, bias_d, keys_d, stream_d, out_d):
    f32, f32r, u32 = mybir.dt.float32, mybir.dt.float32r, mybir.dt.uint32
    ALU = mybir.AluOpType
    ACT = mybir.ActivationFunctionType
    AX = mybir.AxisListType.X
    ds = bass.ds

    whole = ExitStack()
    with whole:
        def on(stack, name, shape, dt=f32):
            return stack.enter_context(nc.sbuf_tensor(name, shape, dt))

        def sem(name):
            return whole.enter_context(nc.semaphore(name))

        raw = on(whole, "raw", [P, 4, PW])
        hi = on(whole, "hi", [P, 2, PW], f32r)
        lo = on(whole, "lo", [P, 2, PW], f32r)
        x1T = on(whole, "x1T", [P, NC, T])
        cst = on(whole, "cst", [P, C_END])
        small = on(whole, "small", [P, S_END])
        mod = on(whole, "mod", [P, NMOD * NC, 2])
        gs = on(whole, "gs", [P, 2, NC, 2])
        gg = on(whole, "gg", [P, 2, NC])
        fin = on(whole, "fin", [P, 16])
        epsc = on(whole, "epsc", [P, 1])

        place1 = ExitStack()
        tok_hi = on(place1, "tok_hi", [P, NC, T], f32r)
        tok_lo = on(place1, "tok_lo", [P, NC, T], f32r)
        place1.close()
        x1n = on(whole, "x1n", [P, 2, D])
        ggB = on(whole, "ggB", [P, D])
        w_hi = on(whole, "w_hi", [P, 2, T], f32r)
        w_lo = on(whole, "w_lo", [P, 2, T], f32r)

        place2 = ExitStack()
        xT = on(place2, "xT", [P, NC, LC])
        kT = on(place2, "kT", [P, NC, LC])
        qplace = ExitStack()
        qraw = on(qplace, "qraw", [P, 4, T])
        qplace.close()
        dss = on(place2, "dss", [P, 4, T])
        qz = on(place2, "qz", [P, 16, T])
        vN = on(place2, "vN", [P, 4, D])
        ada = on(place2, "ada", [P, 4, NC, ADA_N])
        cT = on(place2, "cT", [P, NC, 2])
        cS = on(place2, "cS", [P, NC, 32])
        rows = on(place2, "rows", [P, 2, ADA_N])
        turned = on(place2, "turned", [P, 2, T])
        rstd = on(place2, "rstd", [P, LC])
        tab = on(place2, "tab", [P, R_END])
        lamt = on(place2, "lamt", [P, 2, HD])
        lam = on(place2, "lam", [P, 4])
        mraw = on(place2, "mraw", [P, 4])
        nmax = on(place2, "nmax", [P, 4])
        rsum = on(place2, "rsum", [P, 4])
        rinv = on(place2, "rinv", [P, 4])
        hplace = ExitStack()
        h_hi = on(hplace, "h_hi", [P, NC, LC], f32r)
        h_lo = on(hplace, "h_lo", [P, NC, LC], f32r)
        hplace.close()
        prob_e = on(hplace, "prob_e", [P, 4, LC])
        prob = on(hplace, "prob", [P, 2, LC])
        probT = on(hplace, "probT", [P, 2, 4, T])
        attf = on(hplace, "attf", [P, NC, T])
        dsq = on(hplace, "dsq", [P, 2, T])
        hplace.close()
        ysq = on(hplace, "ysq", [P, NC, T])
        ytmp = on(hplace, "ytmp", [P, NC, T])
        hplace.close()
        place2.close()
        xn = vN[:, :, :].rearrange("p a (b t) -> p (a b) t", t=LC)
        xsq = kT
        bias = ada[:, 0:2, :, :].rearrange("p a c n -> p (a c) n")

        early = ExitStack()
        qT = on(early, "qT", [P, 16, T])
        keys = on(early, "keys", [P, 16, NK])
        early.close()
        TAIL = 96
        late = ExitStack()
        on(late, "below_tail", [P, TAIL * T])
        sc = on(late, "sc", [P, 32, NK])
        sv = on(late, "sv", [P, 32, TOPK])
        si = on(late, "si", [P, 32, TOPK])
        work = on(late, "work", [P, 4, NK])
        m16 = on(late, "m16", [P, 4, TOPK])
        i16 = on(late, "i16", [P, 4, TOPK], u32)
        cand = on(late, "cand", [P, TOPK * TOPK])
        ab = on(late, "ab", [P, 2, TOPK], u32)
        abf = on(late, "abf", [P, 2, TOPK])
        eq = on(late, "eq", [P, 2, TOPK, TOPK])
        best = on(late, "best", [P, 2, PH, TOPK])
        ijs = on(late, "ijs", [P, 2, 2, PH, TOPK])
        gate = on(late, "gate", [P, 2 * PH, TOPK])
        gsum = on(late, "gsum", [P, 2 * PH])
        late.close()

        act_t = on(whole, "act_t", [P, NK, T])
        slot = on(whole, "slot", [P, 3, T])
        ohi = on(whole, "ohi", [P, 8, NK])
        idx = on(whole, "idx", [P, 8])
        ghj = on(whole, "ghj", [P, 8, NK])
        fout = act_t[:, 0:16, :].rearrange("p (a c) t -> p a (c t)", a=4)

        PB = [whole.enter_context(nc.psum_tensor(f"PB{b}", [P, 512], f32)) for b in range(8)]

        x_loaded, c_loaded, cst_loaded, small_loaded, tab_loaded = map(
            sem, ["x_loaded", "c_loaded", "cst_loaded", "small_loaded", "tab_loaded"])
        bias_loaded, keys_loaded = sem("bias_loaded"), sem("keys_loaded")
        ada_first = [sem(f"ada_first{k}") for k in range(4)]
        ada_loaded = [sem(f"ada_loaded{k}") for k in range(4)]
        raw_loaded = [sem(f"raw_loaded{k}") for k in range(4)]
        hi_ready, lo_ready = sem("hi_ready"), sem("lo_ready")
        hi_used, piece_done = sem("hi_used"), sem("piece_done")
        dve_step, act_step, pool_step = sem("dve_step"), sem("act_step"), sem("pool_step")
        zeroed, silu_done, xsq_done, xss_done, std_done = map(
            sem, ["zeroed", "silu_done", "xsq_done", "xss_done", "std_done"])
        ada_used, rows_ready, mod_summed, mod_ready = map(
            sem, ["ada_used", "rows_ready", "mod_summed", "mod_ready"])
        h_ready, h_hi_ready, h_lo_ready = sem("h_ready"), sem("h_hi_ready"), sem("h_lo_ready")
        kq_copied, v_copied = sem("kq_copied"), sem("v_copied")
        swapped, roped = sem("swapped"), sem("roped")
        lam_dot, lam_exp = sem("lam_dot"), sem("lam_exp")
        bias_ready = sem("bias_ready")
        scored, max_ready, exp_done, prob_ready = map(sem, ["scored", "max_ready", "exp_done", "prob_ready"])
        transposed, probT_ready, pv_done, att_copied = map(
            sem, ["transposed", "probT_ready", "pv_done", "att_copied"])
        dsq_done, dss_done, dss_copied, dstd_done, att_ready = map(
            sem, ["dsq_done", "dss_done", "dss_copied", "dstd_done", "att_ready"])
        tok_hi_ready, tok_lo_ready = sem("tok_hi_ready"), sem("tok_lo_ready")
        ysq_done, yss_done, ystd_done, x1_ready = map(sem, ["ysq_done", "yss_done", "ystd_done", "x1_ready"])
        x1sq_done, x1ss_done, x1std_done, h2_ready = map(
            sem, ["x1sq_done", "x1ss_done", "x1std_done", "h2_ready"])
        q_copied, s_done, s_copied = sem("q_copied"), sem("s_done"), sem("s_copied")
        act_done = sem("act_done")
        best_ready, gexp_done, gate_ready, slotT_done, slot_ready = map(
            sem, ["best_ready", "gexp_done", "gate_ready", "slotT_done", "slot_ready"])
        ohi_ready, ghj_ready, gate_done, weighted = map(sem, ["ohi_ready", "ghj_ready", "gate_done", "weighted"])
        final_rows, final_rows_copied = sem("final_rows"), sem("final_rows_copied")
        w_hi_ready, w_lo_ready = sem("w_hi_ready"), sem("w_lo_ready")
        fsq_done, fss_ready, fstd_done, y_ready, out_ready, out_stored = map(
            sem, ["fsq_done", "fss_ready", "fstd_done", "y_ready", "out_ready", "out_stored"])

        ident = cst[:, C_ID:C_ID + P]
        ones = cst[:, C_ONE:C_ONE + P]
        iota = cst[:, C_IOTA:C_IOTA + P]
        perm = cst[:, C_PERM:C_PERM + P]
        sel = cst[:, C_SEL:C_SEL + 2]
        iota16 = cst[:, C_I16:C_I16 + TOPK]

        units = [("d", h, t) for h in range(DIFF_HEADS) for t in range(2)]
        units += [("n", h, t) for h in range(NA_HEADS) for t in range(2)]
        maps_of, k = [], 0
        for kind, _, _ in units:
            n = 2 if kind == "d" else 1
            maps_of.append(list(range(k, k + n)))
            k += n
        N_UNITS = len(units)
        N_AHEADS = DIFF_HEADS + NA_HEADS
        def ada_bank(b):
            return 5 if b < ADA_FIRST and b % 2 else 6

        ATT_ORDER = [4, 5, 6, 7, 0, 1, 2, 3]
        unit_of_map = [u for u, ks in enumerate(maps_of) for _ in ks]

        block = whole.enter_context(nc.Block())

        @block.sync
        def _(sp):
            def load(n, k):
                sp.dma_start(raw[:, k, :], stream_d[ds(n, 1), :, :].rearrange("a p w -> p (a w)")
                             ).then_inc(raw_loaded[k], 16)

            sp.wait_ge(ada_first[3], 16)
            for k in range(4):
                load(k, k)
            with sp.Fori(1, PIECES // 4) as i:
                for k in range(4):
                    sp.wait_ge(lo_ready, 4 * i + k - 3)
                    load(4 * i + k, k)
            for k in range(4):
                sp.wait_ge(out_ready, k + 1)
                sp.dma_start(out_d[0, (k // 2) * P:(k // 2 + 1) * P, (k % 2) * 512:(k % 2 + 1) * 512],
                             fout[:, k, 0:512]).then_inc(out_stored, 16)
            sp.wait_ge(out_stored, 64)

        @block.gpsimd
        def _(pool):
            own = Steps(pool, pool_step)
            def load_ada(b, k):
                pool.dma_start(ada[:, k, :, :],
                               ada_d[ds(b, 1), :, :].rearrange("a p (c n) -> p (a c) n", c=NC)
                               ).then_inc(ada_loaded[k], 16)

            with pool.Fori(1, ADA_BLOCKS // 4) as i:
                for k in range(4):
                    pool.wait_ge(ada_used, 4 * i + k - 3)
                    load_ada(4 * i + k, k)
            pool.wait_ge(ada_used, ADA_BLOCKS)
            pool.dma_start(bias, bias_d).then_inc(bias_loaded, 16)
            pool.wait_ge(bias_loaded, 16)
            pool.wait_ge(tab_loaded, 16)
            nc.gpsimd.tensor_tensor(bias, bias, tab[:, None, R_MASK:R_MASK + T].to_broadcast([P, 16, T]),
                                    ALU.add).then_inc(bias_ready, 1)
            pool.wait_ge(x1_ready, NC)
            pool.wait_ge(pv_done, N_AHEADS)
            pool.dma_start(keys[:, :, :], keys_d).then_inc(keys_loaded, 16)
            pool.wait_ge(slot_ready, 3)
            pool.wait_ge(act_done, NK)

            def one_hot(q, half):
                own.add(nc.gpsimd.tensor_copy(idx[:, 4 * half:4 * half + POOL_HOT], slot[:, 0, ds(4 * q, POOL_HOT)]))
                own.drained()
                for e in range(4 * half, 4 * half + POOL_HOT):
                    nc.gpsimd.tensor_scalar(ohi[:, e, :], iota, idx[:, e:e + 1], None,
                                            ALU.is_equal).then_inc(ohi_ready, 1)

            one_hot(0, 0)
            one_hot(1, 1)
            with repeat(pool, T // 8 - 1, own, 2) as i:
                for half in range(2):
                    pool.wait_ge(gate_done, 2 * i + half + 1)
                    one_hot(2 * i + half + 2, half)
            pool.wait_ge(final_rows_copied, 6)
            for g in range(4):
                pool.wait_ge(y_ready, g + 1)
                nc.gpsimd.tensor_tensor(fout[:, g, 0:512], fout[:, g, 0:512],
                                        x1n[:, g // 2, (g % 2) * 512:(g % 2 + 1) * 512],
                                        ALU.add).then_inc(out_ready, 1)

        @block.scalar
        def _(act):
            def hi_of(m, turn, k):
                act.wait_ge(raw_loaded[k], 16 * turn + 16)
                if not (isinstance(m, int) and m < 2):
                    act.wait_ge(hi_used, m - 1)
                    act.wait_ge(lo_ready, m - 1)
                nc.scalar.copy(hi[:, k % 2, :], raw[:, k, :]).then_inc(hi_ready, 1)

            def lead(n):
                m = n + 2
                if m < PIECES:
                    hi_of(m, m // 4, m % 4)

            act.dma_start(cT[:, :, :], cT_d).then_inc(c_loaded, 16)
            act.dma_start(cst[:, :], cst_d).then_inc(cst_loaded, 16)
            act.dma_start(xT[:, :, :], xT_d).then_inc(x_loaded, 16)
            for k in range(4):
                act.dma_start(ada[:, k, :, :], ada_d[k].rearrange("p (c n) -> p c n", c=NC)
                              ).then_inc(ada_first[k], 16)
            act.dma_start(small[:, :], small_d).then_inc(small_loaded, 16)
            act.dma_start(tab[:, :], tab_d).then_inc(tab_loaded, 16)

            act.wait_ge(c_loaded, 16)
            act.wait_ge(zeroed, 1)
            nc.scalar.activation(cS[:, :, 0:2], cT[:, :, :], ACT.Silu).then_inc(silu_done, 1)
            act.wait_ge(x_loaded, 16)
            for g in range(4):
                nc.scalar.activation(xsq[:, 2 * g:2 * g + 2, :], xT[:, 2 * g:2 * g + 2, :],
                                     ACT.Square).then_inc(xsq_done, 1)
            act.wait_ge(zeroed, 2)
            act.wait_ge(xss_done, 1)
            nc.scalar.activation(rstd[:, :], PB[3][:, :], ACT.Sqrt, bias=epsc[:, 0:1],
                                 scale=1.0 / D).then_inc(std_done, 1)
            hi_of(0, 0, 0)
            hi_of(1, 0, 1)
            for c in range(NC):
                act.wait_ge(h_ready, c + 1)
                nc.scalar.copy(h_hi[:, c, :], xn[:, c, :]).then_inc(h_hi_ready, 1)

            with act.Fori(0, 2) as i:
                for k in range(4):
                    n = 4 * i + k
                    hi_of(n + 2, i + (k + 2) // 4, (k + 2) % 4)
                    act.wait_ge(piece_done, n + 1)
                    nc.scalar.copy(kT[:, ds(n, 1), :].rearrange("p a t -> p (a t)"),
                                   PB[4 + k % 2][:, :]).then_inc(kq_copied, 1)
            act.wait_ge(zeroed, 3)
            for n in range(QP0, VP0):
                lead(n)
                act.wait_ge(piece_done, n + 1)
                src = PB[4 + n % 2]
                if n < QP0 + 4:
                    nc.scalar.copy(qraw[:, n - QP0, :], src[:, 0:T]).then_inc(kq_copied, 1)
                else:
                    h = DIFF_HEADS * 2 + 2 * (n - QP0 - 4)
                    nc.scalar.mul(qz[0:HD, h, :], src[0:HD, 0:T], SCALE)
                    nc.scalar.mul(qz[HD:P, h + 1, :], src[HD:P, 0:T], SCALE).then_inc(kq_copied, 1)
            for g in range(2):
                for n in range(VP0 + 4 * g, VP0 + 4 * g + 4):
                    lead(n)
                act.wait_ge(piece_done, VP0 + 4 * g + 4)
                for tt in range(4):
                    nc.scalar.copy(vN[:, tt, 512 * g:512 * g + 512], PB[tt][:, :]).then_inc(v_copied, 1)

            act.wait_ge(lam_dot, 1)
            nc.scalar.activation(lam[:, 0:2], lam[:, 2:4], ACT.Exp).then_inc(lam_exp, 1)

            def exps(u):
                for k in maps_of[u]:
                    act.wait_ge(max_ready, k + 1)
                    if k >= 4:
                        act.wait_ge(prob_ready, unit_of_map[k - 4] + 1)
                    nc.scalar.activation(prob_e[:, k % 4, :], PB[k % 4][:, :], ACT.Exp,
                                         bias=nmax[:, k % 4:k % 4 + 1],
                                         scale=SCALE if units[u][0] == "d" else 1.0,
                                         accum_out=rsum[:, k % 4:k % 4 + 1]).then_inc(exp_done, 1)

            def attention_hi(first, last):
                for i in range(first, last):
                    if i < 4:
                        act.wait_ge(att_ready, i + 1)
                    else:
                        act.wait_ge(att_copied, DIFF_HEADS + 2 * (i - 3))
                    c = ATT_ORDER[i]
                    nc.scalar.copy(tok_hi[:, c, :], attf[:, c, :]).then_inc(tok_hi_ready, 1)

            exps(0)
            for u in range(N_UNITS):
                if u + 1 < N_UNITS:
                    exps(u + 1)
                act.wait_ge(transposed, u + 1)
                head, tile = u // 2, u % 2
                if head >= 2:
                    act.wait_ge(pv_done, head - 1)
                nc.scalar.copy(probT[:, head % 2, :, tile * P:(tile + 1) * P],
                               PB[4 + u % 2][:, :].rearrange("p (c q) -> p c q", c=4)
                               ).then_inc(probT_ready, 1)
                if u in (3, 5, 7, 9):
                    d = (u - 3) // 2
                    act.wait_ge(att_copied, d + 1)
                    if d >= 2:
                        act.wait_ge(dss_done, d - 1)
                    nc.scalar.activation(dsq[:, d % 2, :], attf[:, 4 + d, :], ACT.Square).then_inc(dsq_done, 1)
                if u == 11:
                    act.wait_ge(dss_copied, DIFF_HEADS)
                    nc.scalar.activation(dss[:, :, :], dss[:, :, :], ACT.Sqrt, bias=epsc[:, 0:1],
                                         scale=1.0 / P).then_inc(dstd_done, 1)
                if u == 13:
                    attention_hi(0, 4)
                if u in (14, 18, 22):
                    attention_hi(4 + (u - 14) // 4, 5 + (u - 14) // 4)
            attention_hi(7, 8)

            act.wait_ge(tok_lo_ready, NC)
            for b in range(4):
                lead(WO0 + 2 * b)
                lead(WO0 + 2 * b + 1)
                act.wait_ge(piece_done, WO0 + 2 * b + 2)
                nc.scalar.activation(ysq[:, 2 * b:2 * b + 2, :].rearrange("p a t -> p (a t)"), PB[b][:, :],
                                     ACT.Square).then_inc(ysq_done, 1)
            act.wait_ge(yss_done, 1)
            nc.scalar.activation(rstd[:, 0:T], PB[4][:, 0:T], ACT.Sqrt, bias=epsc[:, 0:1],
                                 scale=1.0 / D).then_inc(ystd_done, 1)
            for c in range(NC):
                act.wait_ge(x1_ready, c + 1)
                nc.scalar.activation(ysq[:, c, :], x1T[:, c, :], ACT.Square).then_inc(x1sq_done, 1)
            act.wait_ge(x1ss_done, 1)
            nc.scalar.activation(rstd[:, 0:T], PB[5][:, 0:T], ACT.Sqrt, bias=epsc[:, 0:1],
                                 scale=1.0 / D).then_inc(x1std_done, 1)
            for c in range(NC):
                act.wait_ge(h2_ready, c + 1)
                nc.scalar.copy(tok_hi[:, c, :], ytmp[:, c, :]).then_inc(tok_hi_ready, 1)

            act.wait_ge(tok_lo_ready, 2 * NC)
            with act.Fori(0, 4) as i:
                for k in range(4):
                    n = WQ0 + 4 * i + k
                    hi_of(n + 2, WQ0 // 4 + i + (k + 2) // 4, (k + 2) % 4)
                    act.wait_ge(piece_done, n + 1)
                    nc.scalar.copy(qT[:, ds(4 * i + k, 1), :].rearrange("p a t -> p (a t)"),
                                   PB[6 + k % 2][:, 0:T]).then_inc(q_copied, 1)
            for g in range(8):
                act.wait_ge(s_done, g + 1)
                nc.scalar.copy(sc[:, 4 * g:4 * g + 4, :].rearrange("p a n -> p (a n)"),
                               PB[g % 4][:, :]).then_inc(s_copied, 1)

            def gelus(first, last):
                with act.Fori(first // 4, last // 4) as i:
                    for k in range(4):
                        n = U0 + 4 * i + k
                        hi_of(n + 2, U0 // 4 + i + (k + 2) // 4, (k + 2) % 4)
                        act.wait_ge(piece_done, n + 1)
                        nc.scalar.activation(act_t[:, ds(4 * i + k, 1), :].rearrange("p a t -> p (a t)"),
                                             PB[k % 2][:, 0:T], ACT.Gelu).then_inc(act_done, 1)

            gelus(0, 100)
            act.wait_ge(best_ready, 1)
            nc.scalar.activation(gate[:, :, :], gate[:, :, :], ACT.Exp).then_inc(gexp_done, 1)
            gelus(100, 108)
            act.wait_ge(slotT_done, 1)
            gelus(108, NK)

            for g in range(6):
                act.wait_ge(final_rows, g + 1)
                dst = (x1n[:, g // 2, (g % 2) * 512:(g % 2 + 1) * 512] if g < 4
                       else ggB[:, (g - 4) * 512:(g - 3) * 512])
                nc.scalar.copy(dst, PB[g][:, :]).then_inc(final_rows_copied, 1)

            act.wait_ge(weighted, T // 4)

            def weight_hi(i, k):
                nc.scalar.copy(w_hi[:, k % 2, :], act_t[:, ds(i, 1), :].rearrange("p a t -> p (a t)")
                               ).then_inc(w_hi_ready, 1)

            weight_hi(0, 0)
            weight_hi(1, 1)
            with act.Fori(0, NK // 4 - 1) as i:
                for k in range(4):
                    n = V0 + 4 * i + k
                    hi_of(n + 2, V0 // 4 + i + (k + 2) // 4, (k + 2) % 4)
                    act.wait_ge(piece_done, n + 1)
                    weight_hi(4 * i + k + 2, k)
            for n in range(PIECES - 4, PIECES - 2):
                lead(n)
                act.wait_ge(piece_done, n + 1)
                weight_hi(n - V0 + 2, n % 4)

            act.wait_ge(piece_done, PIECES)
            for g in range(4):
                nc.scalar.activation(fout[:, g, 0:512], PB[g][:, :], ACT.Square,
                                     accum_out=fin[:, g:g + 1]).then_inc(fsq_done, 1)
            act.wait_ge(fss_ready, 1)
            nc.scalar.activation(fin[:, 6:8], fin[:, 4:6], ACT.Sqrt, bias=epsc[:, 0:1],
                                 scale=1.0 / D).then_inc(fstd_done, 1)

        @block.vector
        def _(dve):
            own = Steps(dve, dve_step)
            v = nc.vector

            def lo_of(m, k):
                dve.wait_ge(hi_ready, m + 1)
                if not (isinstance(m, int) and m < 2):
                    dve.wait_ge(piece_done, m - 1)
                v.tensor_tensor(lo[:, k % 2, :], raw[:, k, :], hi[:, k % 2, :].bitcast(f32),
                                ALU.subtract).then_inc(lo_ready, 1)

            def lead(n):
                if n + 2 < PIECES:
                    lo_of(n + 2, (n + 2) % 4)

            v.memset(cS[:, :, :], 0.0).then_inc(zeroed, 1)
            v.memset(epsc[:, :], EPS).then_inc(zeroed, 1)
            v.memset(qz[:, :, :], 0.0).then_inc(zeroed, 1)

            def modulation(first, last):
                own.link(v.tensor_tensor(mod[:, first:last, :],
                                         PB[7][:, 2 * first:2 * last].rearrange("p (c m) -> p c m", m=2),
                                         small[:, S_B + first:S_B + last, None].to_broadcast([P, last - first, 2]),
                                         ALU.add))

            def ada_rows(b):
                dve.wait_ge(ada_used, b + 1)
                if b >= 2:
                    dve.wait_ge(mod_summed, b - 1)
                v.tensor_copy(rows[:, b % 2, :], PB[ada_bank(b)][:, 0:ADA_N]).then_inc(rows_ready, 1)

            ada_rows(0)
            ada_rows(1)
            dve.wait_ge(std_done, 1)
            own.link(v.reciprocal(rstd[:, :], rstd[:, :]))
            for c in range(NC):
                own.add(v.tensor_tensor(xn[:, c, :], xT[:, c, :], rstd[:, :], ALU.mult))
                if c % 2:
                    ada_rows(2 + c // 2)
            own.wait()
            for b in range(6, ADA_FIRST):
                ada_rows(b)
            lo_of(0, 0)
            lo_of(1, 1)
            dve.wait_ge(mod_summed, ADA_FIRST)
            dve.wait_ge(small_loaded, 16)
            modulation(SH1, GT1)
            own.link(v.scalar_tensor_tensor(gs[:, 0, :, :], mod[:, SC1:SC1 + NC, :], 1.0,
                                            small[:, S_G:S_G + NC, None].to_broadcast([P, NC, 2]),
                                            ALU.add, ALU.mult))
            def h_rest(c):
                dve.wait_ge(h_ready, c + 1)
                dve.wait_ge(h_hi_ready, c + 1)
                v.tensor_tensor(h_lo[:, c, :], xn[:, c, :], h_hi[:, c, :].bitcast(f32),
                                ALU.subtract).then_inc(h_lo_ready, 1)

            for c in range(NC):
                for s in range(2):
                    cols = xn[:, c, s * T:(s + 1) * T]
                    ins = v.tensor_scalar(cols, cols, gs[:, 0, c, s:s + 1], mod[:, SH1 + c, s:s + 1],
                                          ALU.mult, ALU.add)
                ins.then_inc(h_ready, 1)
                if c >= 2:
                    h_rest(c - 2)
            h_rest(NC - 2)
            h_rest(NC - 1)

            def rope(g):
                dve.wait_ge(swapped, g + 1)
                if g:
                    dve.wait_ge(roped, g)
                for e in range(2):
                    j = 2 * (g % 2) + e
                    src = kT[:, j, 0:T] if g < 2 else qraw[:, j, :]
                    t1, t2 = turned[:, 0, :], turned[:, 1, :]
                    own.add(v.tensor_tensor(t1, src, tab[:, R_COS:R_COS + T], ALU.mult))
                    own.link(v.tensor_tensor(t2, PB[4 + g % 2][:, e * T:(e + 1) * T], tab[:, R_SIN:R_SIN + T],
                                             ALU.mult))
                    if g < 2:
                        last = v.tensor_tensor(src, t1, t2, ALU.add)
                    else:
                        v.tensor_tensor(qz[0:HD, 2 * j, :], t1[0:HD, :], t2[0:HD, :], ALU.add)
                        last = v.tensor_tensor(qz[HD:P, 2 * j + 1, :], t1[HD:P, :], t2[HD:P, :], ALU.add)
                    if e == 0:
                        own.link(last)
                last.then_inc(roped, 1)

            for n in range(KP0, QP0):
                lead(n)
                ada_rows(ADA_FIRST + n)
            with dve.Fori(QP0 // 4, VP0 // 4) as i:
                for k in range(4):
                    lo_of(4 * i + k + 2, (k + 2) % 4)
            dve.wait_ge(tab_loaded, 16)
            dve.wait_ge(kq_copied, 12)
            for n in range(VP0, WO0):
                lead(n)
                if n in (VP0, VP0 + 3):
                    for g in range(2):
                        rope((n - VP0) // 3 * 2 + g)
                ada_rows(QP0 + ADA_FIRST + n - VP0)
            dve.wait_ge(mod_summed, ADA_BLOCKS)
            modulation(GT1, NMOD * NC)
            own.add(v.scalar_tensor_tensor(gs[:, 1, :, :], mod[:, SC2:SC2 + NC, :], 1.0,
                                           small[:, S_G + 2 * NC:S_G + 3 * NC, None].to_broadcast([P, NC, 2]),
                                           ALU.add, ALU.mult))
            own.add(v.tensor_tensor(gg[:, 0, :], mod[:, GT1:GT1 + NC, 0], small[:, S_G + NC:S_G + 2 * NC], ALU.mult))
            v.tensor_tensor(gg[:, 1, :], mod[:, GT2:GT2 + NC, 0], small[:, S_G + 3 * NC:S_G + 4 * NC],
                            ALU.mult).then_inc(mod_ready, 1)

            pairs = tab[:, R_LAM:R_LAM + 4 * HD].rearrange("p (a b d) -> p a b d", a=2, b=2)
            own.link(v.tensor_tensor(lamt[:, :, :], pairs[:, :, 0, :], pairs[:, :, 1, :], ALU.mult))
            v.tensor_reduce(lam[:, 2:4], lamt[:, :, :], AX, ALU.add).then_inc(lam_dot, 1)
            dve.wait_ge(lam_exp, 1)
            own.link(v.tensor_tensor(lam[:, 2:3], lam[:, 1:2], lam[:, 0:1], ALU.subtract))
            own.link(v.tensor_scalar(lam[:, 2:3], lam[:, 2:3], -LAMBDA_INIT, None, ALU.add))

            def maxima(u):
                for k in maps_of[u]:
                    dve.wait_ge(scored, k + 1)
                    if units[u][0] == "d":
                        own.link(v.tensor_reduce(mraw[:, k % 4:k % 4 + 1], PB[k % 4][:, :], AX, ALU.max, negate=True))
                        v.tensor_scalar(nmax[:, k % 4:k % 4 + 1], mraw[:, k % 4:k % 4 + 1], SCALE, None,
                                        ALU.mult).then_inc(max_ready, 1)
                    else:
                        v.tensor_reduce(nmax[:, k % 4:k % 4 + 1], PB[k % 4][:, :], AX, ALU.max,
                                        negate=True).then_inc(max_ready, 1)

            def probabilities(u):
                ks = [k % 4 for k in maps_of[u]]
                dve.wait_ge(exp_done, maps_of[u][-1] + 1)
                if u >= 2:
                    dve.wait_ge(transposed, u - 1)
                for k in ks:
                    own.add(v.reciprocal(rinv[:, k:k + 1], rsum[:, k:k + 1]))
                own.wait()
                if units[u][0] == "d":
                    a, b = ks
                    own.link(v.tensor_tensor(rinv[:, b:b + 1], rinv[:, b:b + 1], lam[:, 2:3], ALU.mult))
                    own.link(v.tensor_scalar(prob_e[:, b, :], prob_e[:, b, :], rinv[:, b:b + 1], None, ALU.mult))
                    v.scalar_tensor_tensor(prob[:, u % 2, :], prob_e[:, a, :], rinv[:, a:a + 1], prob_e[:, b, :],
                                           ALU.mult, ALU.add).then_inc(prob_ready, 1)
                else:
                    a, = ks
                    v.tensor_scalar(prob[:, u % 2, :], prob_e[:, a, :], rinv[:, a:a + 1], None,
                                    ALU.mult).then_inc(prob_ready, 1)

            def copy_head(head):
                dve.wait_ge(pv_done, head + 1)
                if head < DIFF_HEADS:
                    dst, src = attf[:, 4 + head, :], PB[6 + head % 2][:, 0:T]
                else:
                    h = head - DIFF_HEADS
                    part = slice(HD * (h % 2), HD * (h % 2) + HD)
                    dst, src = attf[part, h // 2, :], PB[6 + head % 2][part, 0:T]
                v.tensor_copy(dst, src).then_inc(att_copied, 1)

            def attention_lo(first, last):
                for i in range(first, last):
                    dve.wait_ge(tok_hi_ready, i + 1)
                    c = ATT_ORDER[i]
                    v.tensor_tensor(tok_lo[:, c, :], attf[:, c, :], tok_hi[:, c, :].bitcast(f32),
                                    ALU.subtract).then_inc(tok_lo_ready, 1)

            maxima(0)
            for u in range(N_UNITS):
                if u + 1 < N_UNITS:
                    maxima(u + 1)
                probabilities(u)
                if u >= 3 and u % 2:
                    copy_head((u - 3) // 2)
                if u in (4, 6, 8, 10):
                    d = u // 2 - 2
                    dve.wait_ge(dss_done, d + 1)
                    v.tensor_copy(dss[:, d, :], PB[6 + d % 2][:, T:2 * T]).then_inc(dss_copied, 1)
                if u == 12:
                    dve.wait_ge(dstd_done, 1)
                    dve.wait_ge(att_copied, DIFF_HEADS)
                    own.link(v.reciprocal(dss[:, :, :], dss[:, :, :]))
                    own.link(v.tensor_tensor(attf[:, 4:8, :], attf[:, 4:8, :], dss[:, :, :], ALU.mult))
                    v.tensor_scalar(attf[:, 4:8, :], attf[:, 4:8, :], small[:, S_LN:S_LN + 1], 1.0 - LAMBDA_INIT,
                                    ALU.mult, ALU.mult).then_inc(att_ready, 4)
                if u == 14:
                    attention_lo(0, 4)
                if u in (15, 19, 23):
                    attention_lo(4 + (u - 15) // 4, 5 + (u - 15) // 4)
            copy_head(N_AHEADS - 1)
            attention_lo(7, 8)

            for n in range(WO0, WQ0):
                lead(n)

            dve.wait_ge(ystd_done, 1)
            own.link(v.reciprocal(rstd[:, 0:T], rstd[:, 0:T]))
            for b in range(4):
                own.link(v.tensor_tensor(ytmp[:, 2 * b:2 * b + 2, :], PB[b][:, :].rearrange("p (a t) -> p a t", a=2),
                                         rstd[:, None, 0:T].to_broadcast([P, 2, T]), ALU.mult))
                for c in (2 * b, 2 * b + 1):
                    v.scalar_tensor_tensor(x1T[:, c, :], ytmp[:, c, :], gg[:, 0, c:c + 1], xT[:, c, 0:T],
                                           ALU.mult, ALU.add).then_inc(x1_ready, 1)
            dve.wait_ge(x1std_done, 1)
            own.link(v.reciprocal(rstd[:, 0:T], rstd[:, 0:T]))
            def h2_rest(c):
                dve.wait_ge(tok_hi_ready, NC + c + 1)
                v.tensor_tensor(tok_lo[:, c, :], ytmp[:, c, :], tok_hi[:, c, :].bitcast(f32),
                                ALU.subtract).then_inc(tok_lo_ready, 1)

            own.add(v.tensor_tensor(ytmp[:, 0, :], x1T[:, 0, :], rstd[:, 0:T], ALU.mult))
            for c in range(NC):
                own.wait()
                if c + 1 < NC:
                    own.add(v.tensor_tensor(ytmp[:, c + 1, :], x1T[:, c + 1, :], rstd[:, 0:T], ALU.mult))
                v.tensor_scalar(ytmp[:, c, :], ytmp[:, c, :], gs[:, 1, c, 0:1], mod[:, SH2 + c, 0:1],
                                ALU.mult, ALU.add).then_inc(h2_ready, 1)
                if c >= 2:
                    h2_rest(c - 2)
            h2_rest(NC - 2)
            h2_rest(NC - 1)

            with dve.Fori(WQ0 // 4, U0 // 4) as i:
                for k in range(4):
                    lo_of(4 * i + k + 2, (k + 2) % 4)

            def top16(values, between):
                rs = range(len(values))
                own.drained()
                for r in rs:
                    own.add(v.max(m16[:, r, 0:8], values[r]))
                between()
                own.drained()
                for r in rs:
                    own.add(v.max_index(i16[:, r, 0:8], m16[:, r, 0:8], values[r]))
                for r in rs:
                    own.add(v.match_replace(values[r], m16[:, r, 0:8], values[r], REMOVED))
                between()
                own.drained()
                for r in rs:
                    own.add(v.max(m16[:, r, 8:16], values[r]))
                between()
                own.drained()
                for r in rs:
                    own.add(v.max_index(i16[:, r, 8:16], m16[:, r, 8:16], values[r]))

            def pieces(n, ks):
                ks = iter(ks)

                def one():
                    k = next(ks, None)
                    if k is not None:
                        lo_of(n + 2 + k, (k + 2) % 4)
                return one

            dve.wait_ge(s_copied, 8)
            with repeat(dve, 8, own, 1 + 4 * 5 + 2) as i:
                one = pieces(U0 + 4 * i, range(4))
                one()
                own.add(v.tensor_copy(work[:, :, :], sc[:, ds(4 * i, 4), :]))
                top16([work[:, r, :] for r in range(4)], one)
                own.wait()
                own.add(v.tensor_copy(sv[:, ds(4 * i, 4), :], m16[:, :, :]))
                own.add(v.tensor_copy(si[:, ds(4 * i, 4), :], i16[:, :, :]))
            own.wait()
            for tile in range(2):
                with repeat(dve, PH, own, 13) as h:
                    n = U0 + 32 + 32 * tile + 4 * h
                    row = 16 * tile + 2 * h
                    one = pieces(n, range(3))
                    first = sv[:, ds(row, 1), :].rearrange("p a n -> p (a n)")
                    second = sv[:, ds(row + 1, 1), :].rearrange("p a n -> p (a n)")
                    own.add(v.tensor_tensor(cand[:, :].rearrange("p (a b) -> p a b", b=TOPK),
                                            first[:, :, None].to_broadcast([P, TOPK, TOPK]),
                                            second[:, None, :].to_broadcast([P, TOPK, TOPK]), ALU.add))
                    top16([cand[:, :]], one)
                    own.wait()
                    own.add(v.tensor_copy(best[:, tile, ds(h, 1), :].rearrange("p a n -> p (a n)"), m16[:, 0, :]))
                    own.add(v.tensor_scalar(ab[:, 0, :], i16[:, 0, :], 4, None, ALU.logical_shift_right))
                    own.link(v.tensor_scalar(ab[:, 1, :], i16[:, 0, :], TOPK - 1, None, ALU.bitwise_and))
                    own.link(v.tensor_copy(abf[:, :, :], ab[:, :, :]))
                    own.link(v.tensor_tensor(eq[:, :, :, :], abf[:, :, :, None].to_broadcast([P, 2, TOPK, TOPK]),
                                             iota16[:, None, None, :].to_broadcast([P, 2, TOPK, TOPK]), ALU.is_equal))
                    own.link(v.tensor_tensor(eq[:, :, :, :], eq[:, :, :, :],
                                             si[:, ds(row, 2), None, :].to_broadcast([P, 2, TOPK, TOPK]), ALU.mult))
                    own.link(v.tensor_reduce(ijs[:, tile, :, ds(h, 1), :].rearrange("p s a n -> p s (a n)"),
                                             eq[:, :, :, :], AX, ALU.add))
                    lo_of(n + 5, 1)
            all_best = best[:, :, :, :].rearrange("p t h k -> p (t h) k")
            v.tensor_tensor(gate[:, :, :], all_best, all_best[:, :, 0:1].to_broadcast([P, 2 * PH, TOPK]),
                            ALU.subtract).then_inc(best_ready, 1)
            for n in range(U0 + 96, U0 + 100):
                lead(n)
            dve.wait_ge(gexp_done, 1)
            own.link(v.tensor_reduce(gsum[:, :], gate[:, :, :], AX, ALU.add))
            own.link(v.reciprocal(gsum[:, :], gsum[:, :]))
            v.tensor_tensor(gate[:, :, :], gate[:, :, :], gsum[:, :, None].to_broadcast([P, 2 * PH, TOPK]),
                            ALU.mult).then_inc(gate_ready, 1)
            for n in range(U0 + 100, U0 + 104):
                lead(n)
            dve.wait_ge(slotT_done, 1)
            for s in range(3):
                src = PB[2] if s < 2 else PB[3]
                v.tensor_copy(slot[:, s, :], src[:, (s % 2) * T:(s % 2 + 1) * T]).then_inc(slot_ready, 1)
            with dve.Fori((U0 + 104) // 4, V0 // 4) as i:
                for k in range(4):
                    lo_of(4 * i + k + 2, (k + 2) % 4)

            def gate_rows(q, half):
                for e in range(4):
                    if e >= POOL_HOT:
                        v.tensor_scalar(ohi[:, 4 * half + e, :], iota, slot[:, 0, ds(4 * q + e, 1)], None,
                                        ALU.is_equal)
                    v.tensor_scalar(ghj[:, 4 * half + e, :], iota, slot[:, 1, ds(4 * q + e, 1)],
                                    slot[:, 2, ds(4 * q + e, 1)], ALU.is_equal, ALU.mult).then_inc(ghj_ready, 1)

            def weigh(q, half):
                dve.wait_ge(gate_done, q + 1)
                cells = act_t[:, :, ds(4 * q, 4)].rearrange("p i t -> p t i")
                v.tensor_tensor(cells, PB[6 + half][:, :].rearrange("p (t i) -> p t i", t=4), cells,
                                ALU.mult).then_inc(weighted, 1)

            dve.wait_ge(slot_ready, 3)
            dve.wait_ge(act_done, NK)
            gate_rows(0, 0)
            gate_rows(1, 1)
            with dve.Fori(0, T // 8 - 1) as i:
                for half in range(2):
                    q = 2 * i + half
                    weigh(q, half)
                    gate_rows(q + 2, half)
            weigh(T // 4 - 2, 0)
            weigh(T // 4 - 1, 1)

            def weight_lo(i, k):
                dve.wait_ge(w_hi_ready, i + 1)
                v.tensor_tensor(w_lo[:, k % 2, :], act_t[:, ds(i, 1), :].rearrange("p a t -> p (a t)"),
                                w_hi[:, k % 2, :].bitcast(f32), ALU.subtract).then_inc(w_lo_ready, 1)

            dve.wait_ge(weighted, T // 4)
            weight_lo(0, 0)
            weight_lo(1, 1)
            with dve.Fori(0, NK // 4 - 1) as i:
                for k in range(4):
                    lo_of(V0 + 4 * i + k + 2, (k + 2) % 4)
                    dve.wait_ge(piece_done, V0 + 4 * i + k + 1)
                    weight_lo(4 * i + k + 2, k)
            for n in range(PIECES - 4, PIECES - 2):
                lead(n)
                dve.wait_ge(piece_done, n + 1)
                weight_lo(n - V0 + 2, n % 4)

            dve.wait_ge(fsq_done, 4)
            sums = fin[:, 0:4].rearrange("p (t h) -> p t h", h=2)
            v.tensor_tensor(fin[:, 4:6], sums[:, :, 0], sums[:, :, 1], ALU.add).then_inc(fss_ready, 1)
            dve.wait_ge(fstd_done, 1)
            own.link(v.reciprocal(fin[:, 8:10], fin[:, 6:8]))
            for g in range(4):
                half = slice((g % 2) * 512, (g % 2 + 1) * 512)
                v.scalar_tensor_tensor(fout[:, g, 0:512], PB[g][:, :], fin[:, 8 + g // 2:9 + g // 2],
                                       ggB[:, half], ALU.mult, ALU.mult).then_inc(y_ready, 1)

        @block.tensor
        def _(pe):
            mm = nc.tensor.matmul
            hi_c = hi[:, :, :].rearrange("p s (c n) -> p s c n", n=P)
            lo_c = lo[:, :, :].rearrange("p s (c n) -> p s c n", n=P)

            def weights_piece(n, k, right_hi, right_lo, out, order=range(NC), right_ready=None):
                pe.wait_ge(hi_ready, n + 1)
                for i, c in enumerate(order):
                    if right_ready:
                        for ready, before in right_ready:
                            pe.wait_ge(ready, before + i + 1)
                    mm(out, hi_c[:, k % 2, c, :], right_hi[:, c, :], start=(i == 0), stop=False)
                    last = mm(out, hi_c[:, k % 2, c, :], right_lo[:, c, :], start=False, stop=False)
                last.then_inc(hi_used, 1)
                pe.wait_ge(lo_ready, n + 1)
                for i, c in enumerate(order):
                    last = mm(out, lo_c[:, k % 2, c, :], right_hi[:, c, :], start=False, stop=(i == NC - 1))
                last.then_inc(piece_done, 1)

            def ada_block(b, k):
                pe.wait_ge(*(ada_first[k], 16) if b < 4 else (ada_loaded[k], 16 * (b // 4)))
                if b >= 2:
                    pe.wait_ge(rows_ready, b - 1 if b < ADA_FIRST else b)
                for c in range(NC):
                    g = c % 4
                    last = mm(PB[ada_bank(b)][32 * g:32 * g + 32, 0:ADA_N], cS[:, c, :], ada[:, k, c, :],
                              start=(c < 4), stop=(c >= 4))
                last.then_inc(ada_used, 1)

            def ada_sum(b):
                pe.wait_ge(rows_ready, b + 1)
                for e in range(ADA_N // P):
                    col = 2 * (b * (ADA_N // P) + e)
                    last = mm(PB[7][:, col:col + 2], rows[:, b % 2, e * P:(e + 1) * P], sel, start=True, stop=True)
                last.then_inc(mod_summed, 1)

            pe.wait_ge(silu_done, 1)
            pe.wait_ge(cst_loaded, 16)
            ada_block(0, 0)
            ada_block(1, 1)
            ada_sum(0)
            for c in range(NC):
                pe.wait_ge(xsq_done, c // 2 + 1)
                last = mm(PB[3][:, :], ones, xsq[:, c, :], start=(c == 0), stop=(c == NC - 1))
            last.then_inc(xss_done, 1)
            for b in range(2, ADA_FIRST):
                ada_block(b, b % 4)
                ada_sum(b - 1)
            ada_sum(ADA_FIRST - 1)

            for n in range(KP0, QP0):
                if n >= 2:
                    pe.wait_ge(kq_copied, n - 1)
                weights_piece(n, n, h_hi[:, :, :], h_lo[:, :, :], PB[4 + n % 2][:, :],
                              right_ready=None if n else ((h_hi_ready, 0), (h_lo_ready, 0)))
                ada_block(ADA_FIRST + n, n % 4)
                if n:
                    ada_sum(ADA_FIRST + n - 1)
            ada_sum(QP0 + ADA_FIRST - 1)
            with pe.Fori(QP0 // 2, VP0 // 2) as i:
                for k in range(2):
                    pe.wait_ge(kq_copied, 2 * i + k - 1)
                    weights_piece(2 * i + k, k, h_hi[:, :, 0:T], h_lo[:, :, 0:T], PB[4 + k][:, 0:T])

            def exchange(g):
                pe.wait_ge(kq_copied, 16)
                if g >= 2:
                    pe.wait_ge(roped, g - 1)
                for e in range(2):
                    j = 2 * (g % 2) + e
                    last = mm(PB[4 + g % 2][:, e * T:(e + 1) * T], perm, kT[:, j, 0:T] if g < 2 else qraw[:, j, :],
                              start=True, stop=True)
                last.then_inc(swapped, 1)

            for g in range(2):
                for p in range(4):
                    n = VP0 + 4 * g + p
                    wide = [t[:, n % 2, :].rearrange("p (c n) -> p c n", c=2) for t in (hi, lo)]
                    pe.wait_ge(hi_ready, n + 1)
                    for tt in range(4):
                        if p == 0 and g:
                            pe.wait_ge(v_copied, tt + 1)
                        for e in range(2):
                            c = 2 * p + e
                            mm(PB[tt][:, :], h_hi[:, c, tt * P:(tt + 1) * P], wide[0][:, e, :],
                               start=(c == 0), stop=False)
                            last = mm(PB[tt][:, :], h_lo[:, c, tt * P:(tt + 1) * P], wide[0][:, e, :],
                                      start=False, stop=False)
                    last.then_inc(hi_used, 1)
                    pe.wait_ge(lo_ready, n + 1)
                    for tt in range(4):
                        for e in range(2):
                            c = 2 * p + e
                            last = mm(PB[tt][:, :], h_hi[:, c, tt * P:(tt + 1) * P], wide[1][:, e, :],
                                      start=False, stop=(c == NC - 1))
                    last.then_inc(piece_done, 1)
                    if g == 0 and p in (0, 3):
                        exchange(p // 3 * 2)
                        exchange(p // 3 * 2 + 1)
                    b = QP0 + ADA_FIRST + 4 * g + p
                    ada_block(b, b % 4)
                    if b > QP0 + ADA_FIRST:
                        ada_sum(b - 1)
            ada_sum(ADA_BLOCKS - 1)

            def scores(u):
                kind, head, tile = units[u]
                for m, k in enumerate(maps_of[u]):
                    if k >= 4:
                        pe.wait_ge(exp_done, k - 3)
                    out = PB[k % 4]
                    if kind == "d":
                        flat = m * DIFF_HEADS + head
                        chunk, q = flat // 2, flat
                    else:
                        chunk, q = 4 + head // 2, 2 * DIFF_HEADS + head
                    left = qz[:, q, tile * P:(tile + 1) * P]
                    if kind == "d":
                        last = mm(out[:, :], left, kT[:, chunk, :], start=True, stop=True)
                    else:
                        mm(out[:, T:LC], left, kT[:, chunk, T:LC], start=True, stop=True)
                        mm(out[:, 0:T], left, kT[:, chunk, 0:T], start=True, stop=False)
                        pe.wait_ge(bias_ready, 1)
                        last = mm(out[:, 0:T], ident, bias[:, 2 * head + tile, :], start=False, stop=True)
                    last.then_inc(scored, 1)

            def attend(head):
                pe.wait_ge(probT_ready, 2 * head + 2)
                if head == 0:
                    pe.wait_ge(mod_ready, 1)
                if head >= 2:
                    pe.wait_ge(att_copied, head - 1)
                if 2 <= head < DIFF_HEADS + 2:
                    pe.wait_ge(dss_copied, head - 1)
                for kc in range(4):
                    if head < DIFF_HEADS:
                        left = vN[:, kc, 512 + P * head:512 + P * (head + 1)]
                        out = PB[6 + head % 2][:, 0:T]
                    else:
                        h = head - DIFF_HEADS
                        left = vN[:, kc, HD * h:HD * (h + 1)]
                        out = PB[6 + head % 2][HD * (h % 2):HD * (h % 2) + HD, 0:T]
                    last = mm(out, left, probT[:, head % 2, kc, :], start=(kc == 0), stop=(kc == 3))
                last.then_inc(pv_done, 1)

            pe.wait_ge(roped, 4)
            pe.wait_ge(v_copied, 8)
            scores(0)
            scores(1)
            for u in range(N_UNITS):
                if u + 2 < N_UNITS:
                    scores(u + 2)
                pe.wait_ge(prob_ready, u + 1)
                if u >= 2:
                    pe.wait_ge(probT_ready, u - 1)
                for kc in range(4):
                    last = nc.tensor.transpose(PB[4 + u % 2][:, kc * P:(kc + 1) * P],
                                               prob[:, u % 2, kc * P:(kc + 1) * P], ident)
                last.then_inc(transposed, 1)
                if u >= 2 and u % 2 == 0:
                    attend(u // 2 - 1)
                if u in (3, 5, 7, 9):
                    d = (u - 3) // 2
                    pe.wait_ge(dsq_done, d + 1)
                    mm(PB[6 + d % 2][:, T:2 * T], ones, dsq[:, d % 2, :], start=True, stop=True
                       ).then_inc(dss_done, 1)
            attend(N_AHEADS - 1)

            pe.wait_ge(exp_done, maps_of[-1][-1] + 1)

            def y_squares(b):
                pe.wait_ge(ysq_done, b + 1)
                for c in (2 * b, 2 * b + 1):
                    last = mm(PB[4][:, 0:T], ones, ysq[:, c, :], start=(c == 0), stop=(c == NC - 1))
                return last

            for n in range(WO0, WQ0):
                j = n - WO0
                weights_piece(n, n, tok_hi[:, :, :], tok_lo[:, :, :], PB[j // 2][:, (j % 2) * T:(j % 2 + 1) * T],
                              order=ATT_ORDER, right_ready=None if j else ((tok_hi_ready, 0), (tok_lo_ready, 0)))
                if j in (3, 5, 7):
                    y_squares((j - 3) // 2)
            y_squares(3).then_inc(yss_done, 1)
            for c in range(NC):
                pe.wait_ge(x1sq_done, c + 1)
                last = mm(PB[5][:, 0:T], ones, ysq[:, c, :], start=(c == 0), stop=(c == NC - 1))
            last.then_inc(x1ss_done, 1)

            for k in range(2):
                weights_piece(WQ0 + k, k, tok_hi[:, :, :], tok_lo[:, :, :], PB[6 + k][:, 0:T],
                              right_ready=None if k else ((tok_hi_ready, NC), (tok_lo_ready, NC)))
            with pe.Fori(1, 8) as i:
                for k in range(2):
                    pe.wait_ge(q_copied, 2 * i + k - 1)
                    weights_piece(WQ0 + 2 * i + k, k, tok_hi[:, :, :], tok_lo[:, :, :], PB[6 + k][:, 0:T])
            pe.wait_ge(q_copied, 16)
            pe.wait_ge(keys_loaded, 16)
            for g in range(8):
                if g >= 4:
                    pe.wait_ge(s_copied, g - 3)
                for e in range(4):
                    row = 4 * g + e
                    tile, hp = row // 16, row % 16
                    last = mm(PB[g % 4][:, e * NK:(e + 1) * NK], qT[:, hp, tile * P:(tile + 1) * P],
                              keys[:, hp, :], start=True, stop=True)
                last.then_inc(s_done, 1)

            def expert_rows(first, last):
                with pe.Fori(first // 2, last // 2) as i:
                    for k in range(2):
                        pe.wait_ge(act_done, 2 * i + k - 1)
                        weights_piece(U0 + 2 * i + k, k, tok_hi[:, :, :], tok_lo[:, :, :], PB[k][:, 0:T])

            pe.wait_ge(s_copied, 8)
            for k in range(2):
                weights_piece(U0 + k, k, tok_hi[:, :, :], tok_lo[:, :, :], PB[k][:, 0:T])
            expert_rows(2, 104)
            pe.wait_ge(gate_ready, 1)
            for s in range(3):
                for tile in range(2):
                    if s < 2:
                        src = ijs[:, tile, s, :, :].rearrange("p h k -> p (h k)")
                    else:
                        src = gate[:, tile * PH:(tile + 1) * PH, :].rearrange("p h k -> p (h k)")
                    out = (PB[2] if s < 2 else PB[3])[:, (s % 2) * T + tile * P:(s % 2) * T + (tile + 1) * P]
                    last = nc.tensor.transpose(out, src, ident)
            last.then_inc(slotT_done, 1)
            expert_rows(104, NK)

            pe.wait_ge(act_done, NK)
            pe.wait_ge(slot_ready, 3)
            for g in range(4):
                for e in range(4):
                    c = 4 * (g % 2) + e
                    last = nc.tensor.transpose(PB[g][:, e * P:(e + 1) * P],
                                               x1T[:, c, (g // 2) * P:(g // 2 + 1) * P], ident)
                last.then_inc(final_rows, 1)
            for g in range(2):
                for e in range(4):
                    c = 4 * g + e
                    last = mm(PB[4 + g][:, e * P:(e + 1) * P], gg[:, 1, c:c + 1].to_broadcast([P, P]), ident,
                              start=True, stop=True)
                last.then_inc(final_rows, 1)

            def gate_quad(q, half):
                for e in range(4):
                    if e < POOL_HOT:
                        pe.wait_ge(ohi_ready, POOL_HOT * q + e + 1)
                    pe.wait_ge(ghj_ready, 4 * q + e + 1)
                    last = mm(PB[6 + half][:, e * NK:(e + 1) * NK], ghj[:, 4 * half + e, :],
                              ohi[:, 4 * half + e, :], start=True, stop=True)
                last.then_inc(gate_done, 1)

            gate_quad(0, 0)
            gate_quad(1, 1)
            with pe.Fori(1, T // 8) as i:
                for half in range(2):
                    pe.wait_ge(weighted, 2 * i + half - 1)
                    gate_quad(2 * i + half, half)

            pe.wait_ge(final_rows_copied, 4)

            def value_piece(n, i, k, first=False, final=False):
                wide = [t[:, k, :].rearrange("p (c n) -> p c n", c=2) for t in (hi, lo)]
                pe.wait_ge(hi_ready, n + 1)
                pe.wait_ge(w_hi_ready, i + 1)
                pe.wait_ge(w_lo_ready, i + 1)
                for tt in range(2):
                    for w in (w_hi, w_lo):
                        for e in range(2):
                            last = mm(PB[2 * tt + e][:, :], w[:, k, tt * P:(tt + 1) * P], wide[0][:, e, :],
                                      start=first and w is w_hi, stop=False)
                last.then_inc(hi_used, 1)
                pe.wait_ge(lo_ready, n + 1)
                for tt in range(2):
                    for e in range(2):
                        last = mm(PB[2 * tt + e][:, :], w_hi[:, k, tt * P:(tt + 1) * P], wide[1][:, e, :],
                                  start=False, stop=final)
                last.then_inc(piece_done, 1)

            value_piece(V0, 0, 0, first=True)
            value_piece(V0 + 1, 1, 1)
            with pe.Fori(1, NK // 2 - 1) as i:
                for k in range(2):
                    value_piece(V0 + 2 * i + k, 2 * i + k, k)
            value_piece(PIECES - 2, NK - 2, 0)
            value_piece(PIECES - 1, NK - 1, 1, final=True)


def constants():
    import numpy as np
    cst = np.zeros((P, C_END), np.float32)
    cst[:, C_ID:C_ID + P] = np.eye(P)
    cst[:, C_ONE:C_ONE + P] = 1.0
    cst[:, C_IOTA:C_IOTA + P] = np.arange(P)
    cst[np.arange(P), C_PERM + (np.arange(P) ^ 1)] = 1.0
    for g in range(4):
        for m in range(2):
            cst[32 * g + m, C_SEL + m] = 1.0
    cst[:, C_I16:C_I16 + TOPK] = np.arange(TOPK)
    t = np.arange(T)
    freq = np.float32(10000.0) ** (-np.arange(HD // 4, dtype=np.float32) / (HD // 4))
    row, col = (t // GRID_W).astype(np.float32), (t % GRID_W).astype(np.float32)
    ang = np.concatenate([row[:, None] * freq, col[:, None] * freq], axis=-1)
    d = np.arange(P) % HD
    cos, sin = np.cos(ang)[:, d // 2].T, np.sin(ang)[:, d // 2].T
    tab = np.zeros((P, R_LAM), np.float32)
    tab[:, R_COS:R_COS + T] = cos
    tab[:, R_SIN:R_SIN + T] = np.where(d % 2 == 0, -1.0, 1.0)[:, None] * sin
    c = np.arange(P) % GRID_W
    start = np.clip(c - WIN_C // 2, 0, GRID_W - WIN_C)
    kc = np.arange(T) % GRID_W
    inside = (kc[None, :] >= start[:, None]) & (kc[None, :] < start[:, None] + WIN_C)
    tab[:, R_MASK:R_MASK + T] = np.where(inside, 0.0, MASKED)
    return cst, tab


def kernel(**inputs):
    import numpy as np
    import concourse.bacc as bacc
    from concourse.bass_utils import run_bass_kernel_spmd

    a = {k: np.asarray(x) for k, x in inputs.items()}

    def columns(w):
        return w.reshape(NC, P, -1, P).transpose(2, 1, 0, 3).reshape(-1, P, PW)

    def wide(w):
        return w.reshape(4, 2, P, 512).transpose(0, 2, 1, 3).reshape(4, P, PW)

    w_in = a["w_in"][0]
    qa, ka, va, qd, kd, vd = (w_in[:, 512 * k:512 * (k + 1)] for k in range(6))
    u = a["peer_u"][0].reshape(NK, P, NC, P).transpose(0, 3, 2, 1).reshape(NK, P, PW)
    stream = np.concatenate([columns(kd), columns(ka), columns(qd), columns(qa), wide(va), wide(vd),
                             columns(a["w_out"][0]), columns(a["peer_wq"][0]), u,
                             a["peer_v"][0].reshape(NK, P, PW)])
    tokens = np.concatenate([a["x"][0], a["ctx"][0]])
    cond = np.stack([a["c"][0], a["c_ctx"]])
    cst, tab = constants()
    t = np.arange(T)
    r_off = t[None, :] // GRID_W - t[:, None] // GRID_W + WIN_R - 1
    c_off = np.clip(t[None, :] % GRID_W - t[:, None] % GRID_W + WIN_C - 1, 0, 2 * WIN_C - 2)
    bias = a["na_rel_bias"][0][:, r_off, c_off].reshape(NA_HEADS, 2, P, T)
    arrays = {
        "xT": tokens.T.reshape(NC, P, LC).transpose(1, 0, 2),
        "cT": cond.T.reshape(NC, P, 2).transpose(1, 0, 2),
        "cst": cst,
        "small": np.concatenate([a["b_ada"][0].reshape(-1, P).T, a["g_norm"][0].reshape(-1, P).T,
                                 a["diff_subln"][0][:, None]], axis=1),
        "tab": np.concatenate([tab, np.broadcast_to(a["diff_lambda"][0].reshape(1, -1), (P, 4 * HD))], axis=1),
        "ada": a["w_ada"][0].reshape(NC, P, ADA_BLOCKS, ADA_N).transpose(2, 1, 0, 3).reshape(ADA_BLOCKS, P, -1),
        "bias": bias.transpose(2, 0, 1, 3).reshape(P, 16, T),
        "keys": a["peer_keys"][0].reshape(16, NK, P).transpose(2, 0, 1),
        "stream": stream,
    }
    arrays = {f"in_{k}": np.ascontiguousarray(x) for k, x in arrays.items()}
    nc = bacc.Bacc("TRN2", target_bir_lowering=False, num_devices=1)
    args = [nc.dram_tensor(k, x.shape, mybir.dt.float32, kind="ExternalInput").ap() for k, x in arrays.items()]
    out = nc.dram_tensor("out_dram", (1, T, D), mybir.dt.float32, kind="ExternalOutput").ap()
    program(nc, *args, out)
    got = run_bass_kernel_spmd(nc, [arrays], core_ids=[0])
    return got.results[0]["out_dram"]
```

```python
import concourse.bass as bass
from concourse import mybir
from contextlib import ExitStack, contextmanager

D = 1024
T = 256
CTX = 256
LC = T + CTX
P = 128
NC = D // P
HD = 64
GRID_W = 64
WIN_C = 16
WIN_R = 8
NA_HEADS = 8
DIFF_HEADS = 4
LAMBDA_INIT = 0.2
EPS = 1e-6
SCALE = HD ** -0.5
PH = 8
NK = 128
TOPK = 16
NMOD = 6
MASKED = -1e30
REMOVED = -3.0e38
PW = 1024

HALF = NK // 2
GATES0 = 84

KP0, QP0, VP0, WO0, WQ0, U0, V0 = 0, 8, 16, 24, 32, 48, 176
PIECES = 304
ADA_N = 256
ADA_BLOCKS = NMOD * D // ADA_N
ADA_FIRST = 2 * D // ADA_N
ADA_LATE = ADA_BLOCKS - D // ADA_N
SH1, SC1, GT1, SH2, SC2, GT2 = (k * NC for k in range(NMOD))

C_ID, C_ONE, C_IOTA, C_PERM, C_SEL, C_I16, C_END = 0, 128, 256, 384, 512, 514, 530
S_B, S_G, S_LN, S_END = 0, 48, 80, 81
R_COS, R_SIN, R_MASK, R_LAM, R_END = 0, 256, 512, 768, 1024


class Steps:

    def __init__(self, eng, sem):
        self.eng, self.sem, self.n, self.local = eng, sem, 0, 0

    def add(self, ins):
        ins.then_inc(self.sem, 1)
        self.n = self.n + 1
        self.local += 1

    def wait(self):
        self.eng.wait_ge(self.sem, self.n)

    def link(self, ins):
        self.add(ins)
        self.wait()

    def drained(self):
        self.eng.drain()


@contextmanager
def repeat(eng, times, steps, per_time):
    base, local = steps.n, steps.local
    with eng.Fori(0, times) as i:
        steps.n = base + i * per_time
        yield i
    assert steps.local - local == per_time, (steps.local - local, per_time)
    steps.n = base + times * per_time


def program(nc, xT_d, cT_d, cst_d, small_d, tab_d, ada_d, bias_d, keys_d, stream_d, out_d):
    f32, f32r, u32 = mybir.dt.float32, mybir.dt.float32r, mybir.dt.uint32
    ALU = mybir.AluOpType
    ACT = mybir.ActivationFunctionType
    AX = mybir.AxisListType.X
    ds = bass.ds

    whole = ExitStack()
    with whole:
        def on(stack, name, shape, dt=f32):
            return stack.enter_context(nc.sbuf_tensor(name, shape, dt))

        def sem(name):
            return whole.enter_context(nc.semaphore(name))

        raw = on(whole, "raw", [P, 4, PW])
        hi = on(whole, "hi", [P, 2, PW], f32r)
        lo = on(whole, "lo", [P, 2, PW], f32r)
        x1T = on(whole, "x1T", [P, NC, T])
        cst = on(whole, "cst", [P, C_END])
        small = on(whole, "small", [P, S_END])
        mod = on(whole, "mod", [P, NMOD * NC, 2])
        gs = on(whole, "gs", [P, 2, NC, 2])
        gg = on(whole, "gg", [P, 2, NC])
        fin = on(whole, "fin", [P, 16])
        mhalf = on(whole, "mhalf", [P, 8])
        passed = on(whole, "passed", [P, 1])
        lng = on(whole, "lng", [P, 1])
        var = on(whole, "var", [P, 16])
        rms = on(whole, "rms", [P, 16])
        w_hi = on(whole, "w_hi", [P, 2, T], f32r)
        w_lo = on(whole, "w_lo", [P, 2, T], f32r)

        place1 = ExitStack()
        tok_hi = on(place1, "tok_hi", [P, NC, T], f32r)
        tok_lo = on(place1, "tok_lo", [P, NC, T], f32r)
        place1.close()
        x1n = on(whole, "x1n", [P, 2, D])
        ggB = on(whole, "ggB", [P, D])
        on(whole, "rest_of_place1", [P, D])

        place2 = ExitStack()
        xT = on(place2, "xT", [P, NC, LC])
        kT = on(place2, "kT", [P, NC, LC])
        qraw = on(place2, "qraw", [P, 4, T])
        dvar = on(place2, "dvar", [P, 8])
        drms = on(place2, "drms", [P, 8])
        qz = on(place2, "qz", [P, 16, T])
        vN = on(place2, "vN", [P, 4, D])
        ada = on(place2, "ada", [P, 4, NC, ADA_N])
        cT = on(place2, "cT", [P, NC, 2])
        cS = on(place2, "cS", [P, NC, 32])
        rows = on(place2, "rows", [P, 2, ADA_N])
        turned = on(place2, "turned", [P, 2, T])
        diag = turned[:, :, :].rearrange("p a (b t) -> p (a b) t", t=P)
        rstd = on(place2, "rstd", [P, LC])
        tab = on(place2, "tab", [P, R_END])
        lamt = on(place2, "lamt", [P, 2, HD])
        lam = on(place2, "lam", [P, 4])
        mraw = on(place2, "mraw", [P, 4])
        nmax = on(place2, "nmax", [P, 4])
        rsum = on(place2, "rsum", [P, 4])
        rinv = on(place2, "rinv", [P, 4])
        hplace = ExitStack()
        h_hi = on(hplace, "h_hi", [P, NC, LC], f32r)
        h_lo = on(hplace, "h_lo", [P, NC, LC], f32r)
        hplace.close()
        prob_e = on(hplace, "prob_e", [P, 4, LC])
        prob = on(hplace, "prob", [P, 2, LC])
        probT = on(hplace, "probT", [P, 2, 4, T])
        attf = on(hplace, "attf", [P, NC, T])
        dsq = on(hplace, "dsq", [P, 2, T])
        hplace.close()
        ysq = on(hplace, "ysq", [P, NC, T])
        ytmp = on(hplace, "ytmp", [P, NC, T])
        hplace.close()
        place2.close()
        xn = vN[:, :, :].rearrange("p a (b t) -> p (a b) t", t=LC)
        xsq = kT
        bias = ada[:, 0:2, :, :].rearrange("p a c n -> p (a c) n")

        early = ExitStack()
        qT = on(early, "qT", [P, 16, T])
        keys = on(early, "keys", [P, 16, NK])
        early.close()
        TAIL = 96
        late = ExitStack()
        on(late, "below_tail", [P, TAIL * T])
        sc = on(late, "sc", [P, 32, NK])
        sv = on(late, "sv", [P, 32, TOPK])
        si = on(late, "si", [P, 32, TOPK])
        work = on(late, "work", [P, 4, NK])
        m16 = on(late, "m16", [P, 4, TOPK])
        i16 = on(late, "i16", [P, 4, TOPK], u32)
        cand = on(late, "cand", [P, TOPK * TOPK])
        ab = on(late, "ab", [P, 2, TOPK], u32)
        abf = on(late, "abf", [P, 2, TOPK])
        eq = on(late, "eq", [P, 2, TOPK, TOPK])
        best = on(late, "best", [P, 2, PH, TOPK])
        ijs = on(late, "ijs", [P, 2, 2, PH, TOPK])
        gate = on(late, "gate", [P, 2 * PH, TOPK])
        gsum = on(late, "gsum", [P, 2 * PH])
        late.close()

        act_t = on(whole, "act_t", [P, NK, T])
        slot = on(whole, "slot", [P, 3, T])
        ohi = on(whole, "ohi", [P, 16, HALF])
        idx = on(whole, "idx", [P, 16])
        ghj = on(whole, "ghj", [P, 16, NK])
        fout = act_t[:, 0:16, :].rearrange("p (a c) t -> p a (c t)", a=4)

        PB = [whole.enter_context(nc.psum_tensor(f"PB{b}", [P, 512], f32)) for b in range(8)]

        x_loaded, c_loaded, cst_loaded, small_loaded, tab_loaded = map(
            sem, ["x_loaded", "c_loaded", "cst_loaded", "small_loaded", "tab_loaded"])
        bias_loaded, keys_loaded = sem("bias_loaded"), sem("keys_loaded")
        ada_first = [sem(f"ada_first{k}") for k in range(4)]
        ada_loaded = [sem(f"ada_loaded{k}") for k in range(4)]
        raw_loaded = [sem(f"raw_loaded{k}") for k in range(4)]
        hi_ready, lo_ready, pool_lo_ready = sem("hi_ready"), sem("lo_ready"), sem("pool_lo_ready")
        hi_used, piece_done = sem("hi_used"), sem("piece_done")
        dve_step, pool_step = sem("dve_step"), sem("pool_step")
        zeroed, silu_done = sem("zeroed"), sem("silu_done")
        xsq_done, xcol_done, xvar_ready, xrms_ready, xdiag_ready, xbc_done, xbc_copied = map(
            sem, ["xsq_done", "xcol_done", "xvar_ready", "xrms_ready", "xdiag_ready", "xbc_done", "xbc_copied"])
        xsum_ready, ysum_ready, x1sum_ready = map(sem, ["xsum_ready", "ysum_ready", "x1sum_ready"])
        ada_used, rows_ready, late_rows_ready, mod_summed, mod_ready, late_mod_ready = map(
            sem, ["ada_used", "rows_ready", "late_rows_ready", "mod_summed", "mod_ready", "late_mod_ready"])
        h_ready, hc_ready, h_hi_ready, h_lo_ready = map(sem, ["h_ready", "hc_ready", "h_hi_ready", "h_lo_ready"])
        kq_copied, v_copied = sem("kq_copied"), sem("v_copied")
        swapped, roped = sem("swapped"), sem("roped")
        lam_dot, lam_exp = sem("lam_dot"), sem("lam_exp")
        bias_ready = sem("bias_ready")
        scored, max_ready, exp_done, prob_ready = map(sem, ["scored", "max_ready", "exp_done", "prob_ready"])
        transposed, probT_ready, pv_done, att_copied = map(
            sem, ["transposed", "probT_ready", "pv_done", "att_copied"])
        dsq_done, dcol_done, dvar_ready, drms_ready, ddiag_ready, dbc_done, att_ready = map(
            sem, ["dsq_done", "dcol_done", "dvar_ready", "drms_ready", "ddiag_ready", "dbc_done", "att_ready"])
        tok_hi_ready, tok_lo_ready = sem("tok_hi_ready"), sem("tok_lo_ready")
        ysq_done, yg_ready, ycol_done, yvar_ready, yrms_ready, ydiag_ready, ybc_done, x1_ready = map(
            sem, ["ysq_done", "yg_ready", "ycol_done", "yvar_ready", "yrms_ready", "ydiag_ready", "ybc_done",
                  "x1_ready"])
        x1sq_done, x1col_done, x1var_ready, x1rms_ready, x1diag_ready, x1bc_done, h2_ready = map(
            sem, ["x1sq_done", "x1col_done", "x1var_ready", "x1rms_ready", "x1diag_ready", "x1bc_done",
                  "h2_ready"])
        x1r_ready = sem("x1r_ready")
        q_copied, s_done, s_copied = sem("q_copied"), sem("s_done"), sem("s_copied")
        act_done = sem("act_done")
        best_ready, gexp_done, gate_ready, slotT_done, slot_ready = map(
            sem, ["best_ready", "gexp_done", "gate_ready", "slotT_done", "slot_ready"])
        ohi_ready, ghj_ready, gate_done, weighted = map(sem, ["ohi_ready", "ghj_ready", "gate_done", "weighted"])
        out1_ready = sem("out1_ready")
        final_rows, final_rows_copied = sem("final_rows"), sem("final_rows_copied")
        w_hi_ready, w_lo_ready = sem("w_hi_ready"), sem("w_lo_ready")
        ftile_done, fsq_done, fvar_ready, frms_ready, y_ready, out_ready, out_stored = map(
            sem, ["ftile_done", "fsq_done", "fvar_ready", "frms_ready", "y_ready", "out_ready", "out_stored"])

        ident = cst[:, C_ID:C_ID + P]
        ones = cst[:, C_ONE:C_ONE + P]
        iota = cst[:, C_IOTA:C_IOTA + P]
        perm = cst[:, C_PERM:C_PERM + P]
        sel = cst[:, C_SEL:C_SEL + 2]
        iota16 = cst[:, C_I16:C_I16 + TOPK]

        units = [("d", h, t) for h in range(DIFF_HEADS) for t in range(2)]
        units += [("n", h, t) for h in range(NA_HEADS) for t in range(2)]
        maps_of, k = [], 0
        for kind, _, _ in units:
            n = 2 if kind == "d" else 1
            maps_of.append(list(range(k, k + n)))
            k += n
        N_UNITS = len(units)
        N_AHEADS = DIFF_HEADS + NA_HEADS
        def ada_bank(b):
            return 5 if (b < ADA_FIRST or b >= ADA_LATE) and b % 2 else 6

        ATT_ORDER = [4, 5, 6, 7, 0, 1, 2, 3]
        unit_of_map = [u for u, ks in enumerate(maps_of) for _ in ks]

        SELECT = 80
        QUADS = T // 4
        TWELVE_AT = [0, 1, 3, 4, 6, 7, 9, 10, 12]
        EIGHT_AT = [0, 2, 3, 5, 6, 7, 8]

        block = whole.enter_context(nc.Block())

        @block.sync
        def _(sp):
            def load(n, k):
                sp.dma_start(raw[:, k, :], stream_d[ds(n, 1), :, :].rearrange("a p w -> p (a w)")
                             ).then_inc(raw_loaded[k], 16)

            sp.wait_ge(ada_loaded[1], 16)
            for k in range(4):
                load(k, k)
            with sp.Fori(1, PIECES // 4) as i:
                for k in range(4):
                    sp.wait_ge(lo_ready, 4 * i + k - 3)
                    load(4 * i + k, k)
            for k in range(4):
                sp.wait_ge(*((out_ready, k + 1) if k < 2 else (out1_ready, k - 1)))
                sp.dma_start(out_d[0, (k // 2) * P:(k // 2 + 1) * P, (k % 2) * 512:(k % 2 + 1) * 512],
                             fout[:, k, 0:512]).then_inc(out_stored, 16)
            sp.wait_ge(out_stored, 64)

        @block.gpsimd
        def _(pool):
            own = Steps(pool, pool_step)
            def load_ada(b, k):
                pool.dma_start(ada[:, k, :, :],
                               ada_d[ds(b, 1), :, :].rearrange("a p (c n) -> p (a c) n", c=NC)
                               ).then_inc(ada_loaded[k], 16)

            def inverse_root(out, of, ready, count, done):
                pool.wait_ge(ready, count)
                nc.gpsimd.tensor_tensor(out, of, mhalf[:, 0:out.shape[1]], ALU.pow).then_inc(done, 1)

            own.link(nc.gpsimd.memset(mhalf[:, :], -0.5))
            for k in range(4):
                pool.wait_ge(ada_used, k + 1)
                load_ada(4 + k, k)
                if k == 1:
                    inverse_root(rms[:, 0:4], var[:, 0:4], xvar_ready, 4, xrms_ready)
            with pool.Fori(2, ADA_LATE // 4) as i:
                for k in range(4):
                    pool.wait_ge(ada_used, 4 * i + k - 3)
                    load_ada(4 * i + k, k)
            pool.wait_ge(ada_used, ADA_LATE)
            pool.dma_start(bias, bias_d).then_inc(bias_loaded, 16)
            pool.wait_ge(bias_loaded, 16)
            pool.wait_ge(tab_loaded, 16)
            nc.gpsimd.tensor_tensor(bias, bias, tab[:, None, R_MASK:R_MASK + T].to_broadcast([P, 16, T]),
                                    ALU.add).then_inc(bias_ready, 1)
            for d in range(DIFF_HEADS):
                inverse_root(drms[:, 2 * d:2 * d + 2], dvar[:, 2 * d:2 * d + 2], dvar_ready, 2 * d + 2, drms_ready)
            pool.wait_ge(scored, len(unit_of_map))
            for b in range(ADA_LATE, ADA_BLOCKS):
                load_ada(b, b % 4)
            inverse_root(rms[:, 4:6], var[:, 4:6], yvar_ready, 2, yrms_ready)
            inverse_root(rms[:, 6:8], var[:, 6:8], x1var_ready, 2, x1rms_ready)
            pool.wait_ge(x1_ready, 4)
            pool.wait_ge(pv_done, N_AHEADS)
            pool.dma_start(keys[:, :, :], keys_d).then_inc(keys_loaded, 16)
            with pool.Fori(0, SELECT // 4) as i:
                for k in (3, 5):
                    m = U0 + 4 * i + k
                    pool.wait_ge(hi_ready, m + 1)
                    pool.wait_ge(piece_done, m - 1)
                    nc.gpsimd.tensor_tensor(lo[:, k % 2, :], raw[:, k % 4, :], hi[:, k % 2, :].bitcast(f32),
                                            ALU.subtract).then_inc(pool_lo_ready, 1)
            pool.wait_ge(slot_ready, 3)

            def one_hot(q, part, b):
                own.add(nc.gpsimd.tensor_copy(idx[:, 4 * b:4 * b + 4], slot[:, 0, ds(4 * q, 4)]))
                own.drained()
                for e in range(4 * b, 4 * b + 4):
                    nc.gpsimd.tensor_scalar(ohi[:, e, :], iota[:, HALF * part:HALF * (part + 1)], idx[:, e:e + 1],
                                            None, ALU.is_equal).then_inc(ohi_ready, 1)

            for part in range(2):
                for b in range(4):
                    if part:
                        pool.wait_ge(gate_done, QUADS - 3 + b)
                    one_hot(b, part, b)
                with repeat(pool, QUADS // 4 - 1, own, 4) as i:
                    for b in range(4):
                        pool.wait_ge(gate_done, QUADS * part + 4 * i + b + 1)
                        one_hot(4 * i + b + 4, part, b)
            for t in range(2):
                inverse_root(rms[:, 8 + t:9 + t], fin[:, 4 + t:5 + t], fvar_ready, t + 1, frms_ready)
            pool.wait_ge(final_rows_copied, 6)
            for g in (0, 1):
                pool.wait_ge(y_ready, g + 1)
                nc.gpsimd.tensor_tensor(fout[:, g, 0:512], fout[:, g, 0:512], x1n[:, 0, g * 512:(g + 1) * 512],
                                        ALU.add).then_inc(out_ready, 1)

        @block.scalar
        def _(act):
            def hi_of(m, turn, k):
                act.wait_ge(raw_loaded[k], 16 * turn + 16)
                if not (isinstance(m, int) and m < 2):
                    act.wait_ge(hi_used, m - 1)
                    act.wait_ge(lo_ready, m - 1)
                nc.scalar.copy(hi[:, k % 2, :], raw[:, k, :]).then_inc(hi_ready, 1)

            def lead(n):
                m = n + 2
                if m < PIECES:
                    hi_of(m, m // 4, m % 4)

            act.dma_start(cT[:, :, :], cT_d).then_inc(c_loaded, 16)
            act.dma_start(cst[:, :], cst_d).then_inc(cst_loaded, 16)
            act.dma_start(xT[:, :, :], xT_d).then_inc(x_loaded, 16)
            for k in range(4):
                act.dma_start(ada[:, k, :, :], ada_d[k].rearrange("p (c n) -> p c n", c=NC)
                              ).then_inc(ada_first[k], 16)
            act.dma_start(small[:, :], small_d).then_inc(small_loaded, 16)

            act.wait_ge(c_loaded, 16)
            act.wait_ge(zeroed, 1)
            nc.scalar.activation(cS[:, :, 0:2], cT[:, :, :], ACT.Silu).then_inc(silu_done, 1)
            act.wait_ge(x_loaded, 16)
            for g in range(4):
                nc.scalar.activation(xsq[:, 2 * g:2 * g + 2, :], xT[:, 2 * g:2 * g + 2, :],
                                     ACT.Square).then_inc(xsq_done, 1)
            act.wait_ge(xbc_done, 1)
            nc.scalar.copy(rstd[:, :], PB[3][:, :]).then_inc(xbc_copied, 1)
            hi_of(0, 0, 0)
            hi_of(1, 0, 1)
            act.dma_start(tab[:, :], tab_d).then_inc(tab_loaded, 16)

            def round_h(c):
                act.wait_ge(h_ready, c + 1)
                act.wait_ge(hc_ready, c + 1)
                nc.scalar.copy(h_hi[:, c, :], xn[:, c, :]).then_inc(h_hi_ready, 1)

            act.wait_ge(h_ready, 1)
            for c in range(NC):
                nc.scalar.activation(xn[:, c, T:], xn[:, c, T:], ACT.Identity, bias=mod[:, SH1 + c, 1:2],
                                     scale=gs[:, 0, c, 1:2]).then_inc(hc_ready, 1)
                if c:
                    round_h(c - 1)
            round_h(NC - 1)

            with act.Fori(0, 2) as i:
                for k in range(4):
                    n = 4 * i + k
                    hi_of(n + 2, i + (k + 2) // 4, (k + 2) % 4)
                    act.wait_ge(piece_done, n + 1)
                    nc.scalar.copy(kT[:, ds(n, 1), :].rearrange("p a t -> p (a t)"),
                                   PB[4 + k % 2][:, :]).then_inc(kq_copied, 1)
            act.wait_ge(zeroed, 2)
            for n in range(QP0, VP0):
                lead(n)
                act.wait_ge(piece_done, n + 1)
                src = PB[4 + n % 2]
                if n < QP0 + 4:
                    nc.scalar.copy(qraw[:, n - QP0, :], src[:, 0:T]).then_inc(kq_copied, 1)
                else:
                    h = DIFF_HEADS * 2 + 2 * (n - QP0 - 4)
                    nc.scalar.mul(qz[0:HD, h, :], src[0:HD, 0:T], SCALE)
                    nc.scalar.mul(qz[HD:P, h + 1, :], src[HD:P, 0:T], SCALE).then_inc(kq_copied, 1)
            for g in range(2):
                for n in range(VP0 + 4 * g, VP0 + 4 * g + 4):
                    lead(n)
                act.wait_ge(piece_done, VP0 + 4 * g + 4)
                for tt in range(4):
                    nc.scalar.copy(vN[:, tt, 512 * g:512 * g + 512], PB[tt][:, :]).then_inc(v_copied, 1)

            act.wait_ge(lam_dot, 1)
            nc.scalar.activation(lam[:, 0:2], lam[:, 2:4], ACT.Exp).then_inc(lam_exp, 1)

            def exps(u):
                for k in maps_of[u]:
                    act.wait_ge(max_ready, k + 1)
                    if k >= 4:
                        act.wait_ge(prob_ready, unit_of_map[k - 4] + 1)
                    nc.scalar.activation(prob_e[:, k % 4, :], PB[k % 4][:, :], ACT.Exp,
                                         bias=nmax[:, k % 4:k % 4 + 1],
                                         scale=SCALE if units[u][0] == "d" else 1.0,
                                         accum_out=rsum[:, k % 4:k % 4 + 1]).then_inc(exp_done, 1)

            def attention_hi(first, last):
                for i in range(first, last):
                    if i < 4:
                        act.wait_ge(att_ready, i + 1)
                    else:
                        act.wait_ge(att_copied, DIFF_HEADS + 2 * (i - 3))
                    c = ATT_ORDER[i]
                    nc.scalar.copy(tok_hi[:, c, :], attf[:, c, :]).then_inc(tok_hi_ready, 1)

            exps(0)
            for u in range(N_UNITS):
                if u + 1 < N_UNITS:
                    exps(u + 1)
                act.wait_ge(transposed, u + 1)
                head, tile = u // 2, u % 2
                if head >= 2:
                    act.wait_ge(pv_done, head - 1)
                nc.scalar.copy(probT[:, head % 2, :, tile * P:(tile + 1) * P],
                               PB[4 + u % 2][:, :].rearrange("p (c q) -> p c q", c=4)
                               ).then_inc(probT_ready, 1)
                if u in (3, 5, 7, 9):
                    d = (u - 3) // 2
                    act.wait_ge(att_copied, d + 1)
                    if d >= 2:
                        act.wait_ge(dcol_done, d - 1)
                    nc.scalar.activation(dsq[:, d % 2, :], attf[:, 4 + d, :], ACT.Square).then_inc(dsq_done, 1)
                if u == 15:
                    attention_hi(0, 4)
                if u in (16, 19, 22):
                    attention_hi(4 + (u - 16) // 3, 5 + (u - 16) // 3)
            attention_hi(7, 8)

            act.wait_ge(tok_lo_ready, NC)
            for b in range(4):
                lead(WO0 + 2 * b)
                lead(WO0 + 2 * b + 1)
                act.wait_ge(piece_done, WO0 + 2 * b + 2)
                nc.scalar.activation(ysq[:, 2 * b:2 * b + 2, :].rearrange("p a t -> p (a t)"), PB[b][:, :],
                                     ACT.Square).then_inc(ysq_done, 1)
                if b == 0:
                    act.wait_ge(mod_ready, 1)
                for c in (2 * b, 2 * b + 1):
                    nc.scalar.mul(ytmp[:, c, :], PB[b][:, (c % 2) * T:(c % 2 + 1) * T], gg[:, 0, c:c + 1]
                                  ).then_inc(yg_ready, 1)
            def late_rows(b):
                act.wait_ge(ada_used, b + 1)
                act.wait_ge(mod_summed, b - 1)
                nc.scalar.copy(rows[:, b % 2, :], PB[ada_bank(b)][:, 0:ADA_N]).then_inc(late_rows_ready, 1)

            late_rows(ADA_LATE)
            for b in range(4):
                if b:
                    late_rows(ADA_LATE + b)
                act.wait_ge(x1_ready, b + 1)
                nc.scalar.activation(ysq[:, 2 * b:2 * b + 2, :], x1T[:, 2 * b:2 * b + 2, :],
                                     ACT.Square).then_inc(x1sq_done, 1)
            for c in range(NC):
                act.wait_ge(x1r_ready, c + 1)
                nc.scalar.activation(ysq[:, c, :], ytmp[:, c, :], ACT.Identity, bias=mod[:, SH2 + c, 0:1],
                                     scale=gs[:, 1, c, 0:1]).then_inc(h2_ready, 1)
                if c:
                    act.wait_ge(h2_ready, c)
                    nc.scalar.copy(tok_hi[:, c - 1, :], ysq[:, c - 1, :]).then_inc(tok_hi_ready, 1)
            act.wait_ge(h2_ready, NC)
            nc.scalar.copy(tok_hi[:, NC - 1, :], ysq[:, NC - 1, :]).then_inc(tok_hi_ready, 1)

            act.wait_ge(tok_lo_ready, 2 * NC)
            with act.Fori(0, 4) as i:
                for k in range(4):
                    n = WQ0 + 4 * i + k
                    hi_of(n + 2, WQ0 // 4 + i + (k + 2) // 4, (k + 2) % 4)
                    act.wait_ge(piece_done, n + 1)
                    nc.scalar.copy(qT[:, ds(4 * i + k, 1), :].rearrange("p a t -> p (a t)"),
                                   PB[6 + k % 2][:, 0:T]).then_inc(q_copied, 1)
            for g in range(8):
                act.wait_ge(s_done, g + 1)
                nc.scalar.copy(sc[:, 4 * g:4 * g + 4, :].rearrange("p a n -> p (a n)"),
                               PB[g % 4][:, :]).then_inc(s_copied, 1)

            def gelus(first, last):
                with act.Fori(first // 4, last // 4) as i:
                    for k in range(4):
                        n = U0 + 4 * i + k
                        hi_of(n + 2, U0 // 4 + i + (k + 2) // 4, (k + 2) % 4)
                        act.wait_ge(piece_done, n + 1)
                        nc.scalar.activation(act_t[:, ds(4 * i + k, 1), :].rearrange("p a t -> p (a t)"),
                                             PB[k % 2][:, 0:T], ACT.Gelu).then_inc(act_done, 1)

            gelus(0, GATES0 - 4)
            for n in range(U0 + GATES0 - 4, U0 + GATES0):
                lead(n)
                act.wait_ge(piece_done, n + 1)
                nc.scalar.activation(act_t[:, n - U0, :], PB[n % 2][:, 0:T], ACT.Gelu).then_inc(act_done, 1)
                if n == U0 + GATES0 - 4:
                    act.wait_ge(best_ready, 1)
                    nc.scalar.activation(gate[:, :, :], gate[:, :, :], ACT.Exp).then_inc(gexp_done, 1)
            act.wait_ge(slotT_done, 1)
            gelus(GATES0, NK)

            act.wait_ge(weighted, QUADS)

            def weight_hi(i, k):
                nc.scalar.copy(w_hi[:, k % 2, :], act_t[:, ds(i, 1), :].rearrange("p a t -> p (a t)")
                               ).then_inc(w_hi_ready, 1)

            def value_step(m, turn, k):
                hi_of(m + 2, turn + (k + 2) // 4, (k + 2) % 4)
                act.wait_ge(piece_done, m + 1)
                weight_hi(m - V0 + 2, k)

            weight_hi(0, 0)
            weight_hi(1, 1)
            with act.Fori(V0 // 4, V0 // 4 + 15) as turn:
                for k in range(4):
                    value_step(4 * turn + k, turn, k)
            for n in range(V0 + 60, V0 + 68):
                if n == V0 + 62:
                    act.wait_ge(weighted, 2 * QUADS)
                value_step(n, n // 4, n % 4)
                g = n - V0 - 62
                if g >= 0:
                    act.wait_ge(final_rows, g + 1)
                    dst = (x1n[:, g // 2, (g % 2) * 512:(g % 2 + 1) * 512] if g < 4
                           else ggB[:, (g - 4) * 512:(g - 3) * 512])
                    nc.scalar.copy(dst, PB[4 + g % 2][:, :]).then_inc(final_rows_copied, 1)
            with act.Fori(V0 // 4 + 17, PIECES // 4 - 1) as turn:
                for k in range(4):
                    value_step(4 * turn + k, turn, k)
            for n in range(PIECES - 4, PIECES - 2):
                value_step(n, n // 4, n % 4)

            for g in range(4):
                act.wait_ge(ftile_done, g // 2 + 1)
                nc.scalar.activation(fout[:, g, 0:512], PB[g][:, :], ACT.Square,
                                     accum_out=fin[:, g:g + 1]).then_inc(fsq_done, 1)

        @block.vector
        def _(dve):
            own = Steps(dve, dve_step)
            v = nc.vector

            def lo_of(m, k):
                dve.wait_ge(hi_ready, m + 1)
                if not (isinstance(m, int) and m < 2):
                    dve.wait_ge(piece_done, m - 1)
                v.tensor_tensor(lo[:, k % 2, :], raw[:, k, :], hi[:, k % 2, :].bitcast(f32),
                                ALU.subtract).then_inc(lo_ready, 1)

            def lead(n):
                if n + 2 < PIECES:
                    lo_of(n + 2, (n + 2) % 4)

            v.memset(cS[:, :, :], 0.0).then_inc(zeroed, 1)
            v.memset(qz[:, :, :], 0.0).then_inc(zeroed, 1)

            def modulation(first, last):
                own.link(v.tensor_tensor(mod[:, first:last, :],
                                         PB[7][:, 2 * first:2 * last].rearrange("p (c m) -> p c m", m=2),
                                         small[:, S_B + first:S_B + last, None].to_broadcast([P, last - first, 2]),
                                         ALU.add))

            def ada_rows(b):
                dve.wait_ge(ada_used, b + 1)
                if b >= 2:
                    dve.wait_ge(mod_summed, b - 1)
                v.tensor_copy(rows[:, b % 2, :], PB[ada_bank(b)][:, 0:ADA_N]).then_inc(rows_ready, 1)

            def add_squares(squares, b, ready):
                dve.wait_ge(ready, b + 1)
                own.link(v.tensor_tensor(squares[:, 0:2, :], squares[:, 0:2, :], squares[:, 2 * b:2 * b + 2, :],
                                         ALU.add))

            def fold_squares(squares, ready):
                v.tensor_tensor(squares[:, 0, :], squares[:, 0, :], squares[:, 1, :], ALU.add).then_inc(ready, 1)

            for b in range(1, 4):
                add_squares(xsq, b, xsq_done)
            fold_squares(xsq, xsum_ready)
            ada_rows(0)
            ada_rows(1)

            def mean_squares(out, sums, n, ready):
                v.tensor_scalar(out, sums, 1.0 / n, EPS, ALU.mult, ALU.add).then_inc(ready, 1)

            def on_diagonal(columns, done, count, ready):
                dve.wait_ge(done, count)
                for e in range(columns.shape[1]):
                    ins = v.tensor_scalar(diag[:, e, :], ident, columns[:, e:e + 1], None, ALU.mult)
                ins.then_inc(ready, 1)

            for tt in range(4):
                dve.wait_ge(xcol_done, tt + 1)
                mean_squares(var[:, tt:tt + 1], PB[tt][:, 0:1], D, xvar_ready)
            on_diagonal(rms[:, 0:4], xrms_ready, 1, xdiag_ready)
            dve.wait_ge(xbc_copied, 1)
            for c in range(NC):
                own.add(v.tensor_tensor(xn[:, c, :], xT[:, c, :], rstd[:, :], ALU.mult))
                if c % 2:
                    ada_rows(2 + c // 2)
            own.wait()
            for b in range(6, ADA_FIRST):
                ada_rows(b)
            lo_of(0, 0)
            dve.wait_ge(mod_summed, ADA_FIRST)
            dve.wait_ge(small_loaded, 16)
            modulation(SH1, GT1)
            own.link(v.scalar_tensor_tensor(gs[:, 0, :, :], mod[:, SC1:SC1 + NC, :], 1.0,
                                            small[:, S_G:S_G + NC, None].to_broadcast([P, NC, 2]),
                                            ALU.add, ALU.mult))
            def h_rest(c):
                dve.wait_ge(h_ready, c + 1)
                dve.wait_ge(h_hi_ready, c + 1)
                v.tensor_tensor(h_lo[:, c, :], xn[:, c, :], h_hi[:, c, :].bitcast(f32),
                                ALU.subtract).then_inc(h_lo_ready, 1)

            for c in range(NC):
                v.tensor_scalar(xn[:, c, 0:T], xn[:, c, 0:T], gs[:, 0, c, 0:1], mod[:, SH1 + c, 0:1],
                                ALU.mult, ALU.add).then_inc(h_ready, 1)
                if c >= 2:
                    h_rest(c - 2)
            h_rest(NC - 2)
            h_rest(NC - 1)
            lo_of(1, 1)

            def rope(g):
                dve.wait_ge(swapped, g + 1)
                if g:
                    dve.wait_ge(roped, g)
                for e in range(2):
                    j = 2 * (g % 2) + e
                    src = kT[:, j, 0:T] if g < 2 else qraw[:, j, :]
                    t1, t2 = turned[:, 0, :], turned[:, 1, :]
                    own.add(v.tensor_tensor(t1, src, tab[:, R_COS:R_COS + T], ALU.mult))
                    own.link(v.tensor_tensor(t2, PB[4 + g % 2][:, e * T:(e + 1) * T], tab[:, R_SIN:R_SIN + T],
                                             ALU.mult))
                    if g < 2:
                        last = v.tensor_tensor(src, t1, t2, ALU.add)
                    else:
                        v.tensor_tensor(qz[0:HD, 2 * j, :], t1[0:HD, :], t2[0:HD, :], ALU.add)
                        last = v.tensor_tensor(qz[HD:P, 2 * j + 1, :], t1[HD:P, :], t2[HD:P, :], ALU.add)
                    if e == 0:
                        own.link(last)
                last.then_inc(roped, 1)

            for n in range(KP0, QP0):
                lead(n)
                ada_rows(ADA_FIRST + n)
            with dve.Fori(QP0 // 4, VP0 // 4) as i:
                for k in range(4):
                    lo_of(4 * i + k + 2, (k + 2) % 4)
            dve.wait_ge(tab_loaded, 16)
            dve.wait_ge(kq_copied, 12)
            for n in range(VP0, WO0):
                lead(n)
                if n in (VP0, VP0 + 3):
                    for g in range(2):
                        rope((n - VP0) // 3 * 2 + g)
                if QP0 + ADA_FIRST + n - VP0 < ADA_LATE:
                    ada_rows(QP0 + ADA_FIRST + n - VP0)
            dve.wait_ge(mod_summed, ADA_LATE)
            modulation(GT1, GT2)
            own.add(v.scalar_tensor_tensor(gs[:, 1, :, :], mod[:, SC2:SC2 + NC, :], 1.0,
                                           small[:, S_G + 2 * NC:S_G + 3 * NC, None].to_broadcast([P, NC, 2]),
                                           ALU.add, ALU.mult))
            v.tensor_tensor(gg[:, 0, :], mod[:, GT1:GT1 + NC, 0], small[:, S_G + NC:S_G + 2 * NC],
                            ALU.mult).then_inc(mod_ready, 1)

            own.add(v.tensor_scalar(lng[:, :], small[:, S_LN:S_LN + 1], 1.0 - LAMBDA_INIT, None, ALU.mult))
            pairs = tab[:, R_LAM:R_LAM + 4 * HD].rearrange("p (a b d) -> p a b d", a=2, b=2)
            own.link(v.tensor_tensor(lamt[:, :, :], pairs[:, :, 0, :], pairs[:, :, 1, :], ALU.mult))
            v.tensor_reduce(lam[:, 2:4], lamt[:, :, :], AX, ALU.add).then_inc(lam_dot, 1)
            dve.wait_ge(lam_exp, 1)
            own.link(v.tensor_tensor(lam[:, 2:3], lam[:, 1:2], lam[:, 0:1], ALU.subtract))
            own.link(v.tensor_scalar(lam[:, 2:3], lam[:, 2:3], -LAMBDA_INIT, None, ALU.add))

            def maxima(u):
                ks = maps_of[u]
                a = ks[0] % 4
                for e, k in enumerate(ks):
                    dve.wait_ge(scored, k + 1)
                    out = (mraw if units[u][0] == "d" else nmax)[:, a + e:a + e + 1]
                    ins = v.tensor_reduce(out, PB[k % 4][:, :], AX, ALU.max, negate=True)
                    if units[u][0] == "d":
                        own.add(ins)
                    else:
                        ins.then_inc(max_ready, 1)
                if units[u][0] == "d":
                    own.wait()
                    v.tensor_scalar(nmax[:, a:a + 2], mraw[:, a:a + 2], SCALE, None, ALU.mult).then_inc(max_ready, 2)

            def probabilities(u):
                ks = [k % 4 for k in maps_of[u]]
                dve.wait_ge(exp_done, maps_of[u][-1] + 1)
                if u >= 2:
                    dve.wait_ge(transposed, u - 1)
                own.link(v.reciprocal(rinv[:, ks[0]:ks[-1] + 1], rsum[:, ks[0]:ks[-1] + 1]))
                if units[u][0] == "d":
                    a, b = ks
                    own.link(v.tensor_tensor(rinv[:, b:b + 1], rinv[:, b:b + 1], lam[:, 2:3], ALU.mult))
                    own.link(v.tensor_scalar(prob_e[:, b, :], prob_e[:, b, :], rinv[:, b:b + 1], None, ALU.mult))
                    v.scalar_tensor_tensor(prob[:, u % 2, :], prob_e[:, a, :], rinv[:, a:a + 1], prob_e[:, b, :],
                                           ALU.mult, ALU.add).then_inc(prob_ready, 1)
                else:
                    a, = ks
                    v.tensor_scalar(prob[:, u % 2, :], prob_e[:, a, :], rinv[:, a:a + 1], None,
                                    ALU.mult).then_inc(prob_ready, 1)

            def copy_head(head):
                dve.wait_ge(pv_done, head + 1)
                if head < DIFF_HEADS:
                    dst, src = attf[:, 4 + head, :], PB[6 + head % 2][:, 0:T]
                else:
                    h = head - DIFF_HEADS
                    part = slice(HD * (h % 2), HD * (h % 2) + HD)
                    dst, src = attf[part, h // 2, :], PB[6 + head % 2][part, 0:T]
                v.tensor_copy(dst, src).then_inc(att_copied, 1)

            def attention_lo(first, last):
                for i in range(first, last):
                    dve.wait_ge(tok_hi_ready, i + 1)
                    c = ATT_ORDER[i]
                    v.tensor_tensor(tok_lo[:, c, :], attf[:, c, :], tok_hi[:, c, :].bitcast(f32),
                                    ALU.subtract).then_inc(tok_lo_ready, 1)

            maxima(0)
            for u in range(N_UNITS):
                if u + 1 < N_UNITS:
                    maxima(u + 1)
                probabilities(u)
                if u >= 3 and u % 2:
                    copy_head((u - 3) // 2)
                if u in (4, 6, 8, 10):
                    d = u // 2 - 2
                    dve.wait_ge(dcol_done, d + 1)
                    for t in range(2):
                        mean_squares(dvar[:, 2 * d + t:2 * d + t + 1], PB[6 + d % 2][:, t:t + 1], P, dvar_ready)
                if u in (8, 10, 12, 14):
                    d = u // 2 - 4
                    dve.wait_ge(dbc_done, d + 1)
                    v.scalar_tensor_tensor(attf[:, 4 + d, :], attf[:, 4 + d, :], lng[:, 0:1],
                                           PB[6 + (d + 1) % 2][:, 0:T], ALU.mult, ALU.mult).then_inc(att_ready, 1)
                if u in (6, 8, 10, 12):
                    d = u // 2 - 3
                    on_diagonal(drms[:, 2 * d:2 * d + 2], drms_ready, d + 1, ddiag_ready)
                if u == 16:
                    attention_lo(0, 4)
                if u in (17, 20, 23):
                    attention_lo(4 + (u - 17) // 3, 5 + (u - 17) // 3)
            copy_head(N_AHEADS - 1)
            attention_lo(7, 8)

            for n in range(WO0, WQ0):
                lead(n)
                if n - WO0 in (4, 6):
                    add_squares(ysq, (n - WO0) // 2 - 1, ysq_done)
            add_squares(ysq, 3, ysq_done)
            fold_squares(ysq, ysum_ready)

            for t in range(2):
                dve.wait_ge(ycol_done, t + 1)
                mean_squares(var[:, 4 + t:5 + t], PB[4 + t][:, 0:1], D, yvar_ready)
            on_diagonal(rms[:, 4:6], yrms_ready, 1, ydiag_ready)
            dve.wait_ge(yg_ready, NC)
            dve.wait_ge(ybc_done, 1)
            for b in range(4):
                two = slice(2 * b, 2 * b + 2)
                own.link(v.tensor_tensor(ytmp[:, two, :], ytmp[:, two, :],
                                         PB[0][:, None, 0:T].to_broadcast([P, 2, T]), ALU.mult))
                v.tensor_tensor(x1T[:, two, :], ytmp[:, two, :], xT[:, two, 0:T], ALU.add).then_inc(x1_ready, 1)
                if b >= 2:
                    add_squares(ysq, b - 1, x1sq_done)
            add_squares(ysq, 3, x1sq_done)
            fold_squares(ysq, x1sum_ready)
            for t in range(2):
                dve.wait_ge(x1col_done, t + 1)
                mean_squares(var[:, 6 + t:7 + t], PB[4 + t][:, 0:1], D, x1var_ready)
            on_diagonal(rms[:, 6:8], x1rms_ready, 1, x1diag_ready)
            dve.wait_ge(mod_summed, ADA_BLOCKS)
            modulation(GT2, NMOD * NC)
            v.tensor_tensor(gg[:, 1, :], mod[:, GT2:GT2 + NC, 0], small[:, S_G + 3 * NC:S_G + 4 * NC],
                            ALU.mult).then_inc(late_mod_ready, 1)
            dve.wait_ge(x1bc_done, 1)

            def h2_rest(c):
                dve.wait_ge(tok_hi_ready, NC + c + 1)
                v.tensor_tensor(tok_lo[:, c, :], ysq[:, c, :], tok_hi[:, c, :].bitcast(f32),
                                ALU.subtract).then_inc(tok_lo_ready, 1)

            for c in range(NC):
                v.tensor_tensor(ytmp[:, c, :], x1T[:, c, :], PB[5][:, 0:T], ALU.mult).then_inc(x1r_ready, 1)
                if c >= 2:
                    h2_rest(c - 2)
            h2_rest(NC - 2)
            h2_rest(NC - 1)

            with dve.Fori(WQ0 // 4, U0 // 4) as i:
                for k in range(4):
                    lo_of(4 * i + k + 2, (k + 2) % 4)

            def top16(values, *between):
                rs = range(len(values))
                own.drained()
                for r in rs:
                    own.add(v.max(m16[:, r, 0:8], values[r]))
                between[0]()
                own.drained()
                for r in rs:
                    own.add(v.max_index(i16[:, r, 0:8], m16[:, r, 0:8], values[r]))
                for r in rs:
                    own.add(v.match_replace(values[r], m16[:, r, 0:8], values[r], REMOVED))
                between[1]()
                own.drained()
                for r in rs:
                    own.add(v.max(m16[:, r, 8:16], values[r]))
                between[2]()
                own.drained()
                for r in rs:
                    own.add(v.max_index(i16[:, r, 8:16], m16[:, r, 8:16], values[r]))

            def pieces(pairs, ks):
                ks = iter(ks)

                def one():
                    k = next(ks, None)
                    if k is not None and k % 2:
                        dve.wait_ge(pool_lo_ready, pairs + (k + 1) // 2)
                        v.memset(passed[:, :], 0.0).then_inc(lo_ready, 1)
                    elif k is not None:
                        lo_of(U0 + 2 * pairs + 2 + k, (k + 2) % 4)
                return one

            dve.wait_ge(s_copied, 8)
            with repeat(dve, 8, own, 1 + 4 * 5 + 2) as i:
                one = pieces(2 * i, range(4))
                one()
                own.add(v.tensor_copy(work[:, :, :], sc[:, ds(4 * i, 4), :]))
                top16([work[:, r, :] for r in range(4)], one, one, one)
                own.wait()
                own.add(v.tensor_copy(sv[:, ds(4 * i, 4), :], m16[:, :, :]))
                own.add(v.tensor_copy(si[:, ds(4 * i, 4), :], i16[:, :, :]))
            own.wait()
            for tile in range(2):
                with repeat(dve, 2, own, 4 * 13) as i:
                    for e in range(4):
                        h = 4 * i + e
                        row = 16 * tile + 2 * h
                        one = pieces(16 + 12 * tile + 6 * i, range(3 * e, 3 * e + 3))
                        first = sv[:, ds(row, 1), :].rearrange("p a n -> p (a n)")
                        second = sv[:, ds(row + 1, 1), :].rearrange("p a n -> p (a n)")
                        own.add(v.tensor_tensor(cand[:, :].rearrange("p (a b) -> p a b", b=TOPK),
                                                first[:, :, None].to_broadcast([P, TOPK, TOPK]),
                                                second[:, None, :].to_broadcast([P, TOPK, TOPK]), ALU.add))
                        top16([cand[:, :]], one, lambda: None, lambda: None)
                        one()
                        own.wait()
                        own.add(v.tensor_copy(best[:, tile, ds(h, 1), :].rearrange("p a n -> p (a n)"), m16[:, 0, :]))
                        own.add(v.tensor_scalar(ab[:, 0, :], i16[:, 0, :], 4, None, ALU.logical_shift_right))
                        own.link(v.tensor_scalar(ab[:, 1, :], i16[:, 0, :], TOPK - 1, None, ALU.bitwise_and))
                        own.link(v.tensor_copy(abf[:, :, :], ab[:, :, :]))
                        own.link(v.tensor_tensor(eq[:, :, :, :], abf[:, :, :, None].to_broadcast([P, 2, TOPK, TOPK]),
                                                 iota16[:, None, None, :].to_broadcast([P, 2, TOPK, TOPK]),
                                                 ALU.is_equal))
                        own.link(v.tensor_tensor(eq[:, :, :, :], eq[:, :, :, :],
                                                 si[:, ds(row, 2), None, :].to_broadcast([P, 2, TOPK, TOPK]),
                                                 ALU.mult))
                        one()
                        own.add(v.tensor_reduce(ijs[:, tile, :, ds(h, 1), :].rearrange("p s a n -> p s (a n)"),
                                                eq[:, :, :, :], AX, ALU.add))
            own.wait()
            all_best = best[:, :, :, :].rearrange("p t h k -> p (t h) k")
            v.tensor_tensor(gate[:, :, :], all_best, all_best[:, :, 0:1].to_broadcast([P, 2 * PH, TOPK]),
                            ALU.subtract).then_inc(best_ready, 1)
            lead(U0 + GATES0 - 4)
            lead(U0 + GATES0 - 3)
            dve.wait_ge(gexp_done, 1)
            own.link(v.tensor_reduce(gsum[:, :], gate[:, :, :], AX, ALU.add))
            own.link(v.reciprocal(gsum[:, :], gsum[:, :]))
            v.tensor_tensor(gate[:, :, :], gate[:, :, :], gsum[:, :, None].to_broadcast([P, 2 * PH, TOPK]),
                            ALU.mult).then_inc(gate_ready, 1)
            lead(U0 + GATES0 - 2)
            lead(U0 + GATES0 - 1)
            dve.wait_ge(slotT_done, 1)
            for s in range(3):
                src = PB[2] if s < 2 else PB[3]
                v.tensor_copy(slot[:, s, :], src[:, (s % 2) * T:(s % 2 + 1) * T]).then_inc(slot_ready, 1)

            def gate_rows(q, b):
                for e in range(4):
                    v.tensor_scalar(ghj[:, 4 * b + e, :], iota, slot[:, 1, ds(4 * q + e, 1)],
                                    slot[:, 2, ds(4 * q + e, 1)], ALU.is_equal, ALU.mult).then_inc(ghj_ready, 1)

            def weigh(q, part, b):
                dve.wait_ge(gate_done, QUADS * part + q + 1)
                cells = act_t[:, HALF * part:HALF * (part + 1), ds(4 * q, 4)].rearrange("p i t -> p t i")
                v.tensor_tensor(cells, PB[4 + b][:, 0:4 * HALF].rearrange("p (t i) -> p t i", t=4), cells,
                                ALU.mult).then_inc(weighted, 1)

            def quad(q, part, b, ahead=True):
                weigh(q, part, b)
                if ahead:
                    gate_rows(q + 4, b)

            dve.wait_ge(slot_ready, 3)
            for b in range(4):
                gate_rows(b, b)
            with dve.Fori(0, 5) as i:
                for k in range(8):
                    lo_of(U0 + GATES0 + 8 * i + k + 2, (k + 2) % 4)
                    for e in range(TWELVE_AT[k], TWELVE_AT[k + 1]):
                        quad(12 * i + e, 0, e % 4)
            for k in range(4):
                lead(U0 + NK - 4 + k)
                quad(QUADS - 4 + k, 0, k, ahead=False)

            def weight_lo(i, k):
                dve.wait_ge(w_hi_ready, i + 1)
                v.tensor_tensor(w_lo[:, k % 2, :], act_t[:, ds(i, 1), :].rearrange("p a t -> p (a t)"),
                                w_hi[:, k % 2, :].bitcast(f32), ALU.subtract).then_inc(w_lo_ready, 1)

            def value_step(m, k):
                lo_of(m + 2, (k + 2) % 4)
                dve.wait_ge(piece_done, m + 1)
                weight_lo(m - V0 + 2, k)

            weight_lo(0, 0)
            weight_lo(1, 1)
            for b in range(4):
                dve.wait_ge(gate_done, QUADS - 3 + b)
                gate_rows(b, b)
            with dve.Fori(0, 14) as i:
                for k in range(4):
                    value_step(V0 + 4 * i + k, k)
                    quad(4 * i + k, 1, k)
            for k in range(8):
                value_step(V0 + 56 + k, k % 4)
                if k < 6:
                    for e in range(EIGHT_AT[k], EIGHT_AT[k + 1]):
                        quad(56 + e, 1, e % 4, ahead=e < 4)
            with dve.Fori(V0 // 4 + 16, PIECES // 4 - 1) as turn:
                for k in range(4):
                    value_step(4 * turn + k, k)
            for n in range(PIECES - 4, PIECES - 2):
                value_step(n, n % 4)

            for t in range(2):
                dve.wait_ge(fsq_done, 2 * t + 2)
                own.link(v.tensor_tensor(fin[:, 6 + t:7 + t], fin[:, 2 * t:2 * t + 1], fin[:, 2 * t + 1:2 * t + 2],
                                         ALU.add))
                mean_squares(fin[:, 4 + t:5 + t], fin[:, 6 + t:7 + t], D, fvar_ready)
            dve.wait_ge(final_rows_copied, 6)
            for g in range(4):
                dve.wait_ge(frms_ready, g // 2 + 1)
                half = slice((g % 2) * 512, (g % 2 + 1) * 512)
                v.scalar_tensor_tensor(fout[:, g, 0:512], PB[g][:, :], rms[:, 8 + g // 2:9 + g // 2],
                                       ggB[:, half], ALU.mult, ALU.mult).then_inc(y_ready, 1)
            for g in (2, 3):
                dve.wait_ge(y_ready, g + 1)
                v.tensor_tensor(fout[:, g, 0:512], fout[:, g, 0:512], x1n[:, 1, (g % 2) * 512:(g % 2 + 1) * 512],
                                ALU.add).then_inc(out1_ready, 1)

        @block.tensor
        def _(pe):
            mm = nc.tensor.matmul
            hi_c = hi[:, :, :].rearrange("p s (c n) -> p s c n", n=P)
            lo_c = lo[:, :, :].rearrange("p s (c n) -> p s c n", n=P)

            def weights_piece(n, k, right_hi, right_lo, out, order=range(NC), right_ready=None):
                pe.wait_ge(hi_ready, n + 1)
                for i, c in enumerate(order):
                    if right_ready:
                        for ready, before in right_ready:
                            pe.wait_ge(ready, before + i + 1)
                    mm(out, hi_c[:, k % 2, c, :], right_hi[:, c, :], start=(i == 0), stop=False)
                    last = mm(out, hi_c[:, k % 2, c, :], right_lo[:, c, :], start=False, stop=False)
                last.then_inc(hi_used, 1)
                pe.wait_ge(lo_ready, n + 1)
                for i, c in enumerate(order):
                    last = mm(out, lo_c[:, k % 2, c, :], right_hi[:, c, :], start=False, stop=(i == NC - 1))
                last.then_inc(piece_done, 1)

            def ada_block(b, k):
                pe.wait_ge(*(ada_first[k], 16) if b < 4 else (ada_loaded[k], 16 * (b // 4)))
                if b >= ADA_LATE + 2:
                    pe.wait_ge(late_rows_ready, b - ADA_LATE - 1)
                elif 2 <= b < ADA_LATE:
                    pe.wait_ge(rows_ready, b - 1 if b < ADA_FIRST else b)
                for c in range(NC):
                    g = c % 4
                    last = mm(PB[ada_bank(b)][32 * g:32 * g + 32, 0:ADA_N], cS[:, c, :], ada[:, k, c, :],
                              start=(c < 4), stop=(c >= 4))
                last.then_inc(ada_used, 1)

            def ada_sum(b):
                pe.wait_ge(*((rows_ready, b + 1) if b < ADA_LATE else (late_rows_ready, b - ADA_LATE + 1)))
                for e in range(ADA_N // P):
                    col = 2 * (b * (ADA_N // P) + e)
                    last = mm(PB[7][:, col:col + 2], rows[:, b % 2, e * P:(e + 1) * P], sel, start=True, stop=True)
                last.then_inc(mod_summed, 1)

            pe.wait_ge(silu_done, 1)
            pe.wait_ge(cst_loaded, 16)
            ada_block(0, 0)
            ada_block(1, 1)
            ada_sum(0)
            def column_sums(tiles, bank, squares, ready, done):
                pe.wait_ge(ready, 1)
                for tt in range(tiles):
                    mm(PB[bank + tt][:, 0:1], squares[:, 0, tt * P:(tt + 1) * P], ones[:, 0:1],
                       start=True, stop=True).then_inc(done, 1)

            def broadcast(out, n, ready, done):
                pe.wait_ge(ready, 1)
                mm(out[:, 0:n], ones, diag[:, 0:n // P, :].rearrange("p a t -> p (a t)"), start=True,
                   stop=True).then_inc(done, 1)

            column_sums(4, 0, xsq, xsum_ready, xcol_done)
            ada_block(2, 2)
            ada_sum(1)
            pe.wait_ge(xvar_ready, 4)
            broadcast(PB[3], LC, xdiag_ready, xbc_done)
            for b in range(3, ADA_FIRST):
                ada_block(b, b % 4)
                ada_sum(b - 1)
            ada_sum(ADA_FIRST - 1)

            for n in range(KP0, QP0):
                if n >= 2:
                    pe.wait_ge(kq_copied, n - 1)
                weights_piece(n, n, h_hi[:, :, :], h_lo[:, :, :], PB[4 + n % 2][:, :],
                              right_ready=None if n else ((h_hi_ready, 0), (h_lo_ready, 0)))
                ada_block(ADA_FIRST + n, n % 4)
                if n:
                    ada_sum(ADA_FIRST + n - 1)
            ada_sum(QP0 + ADA_FIRST - 1)
            with pe.Fori(QP0 // 2, VP0 // 2) as i:
                for k in range(2):
                    pe.wait_ge(kq_copied, 2 * i + k - 1)
                    weights_piece(2 * i + k, k, h_hi[:, :, 0:T], h_lo[:, :, 0:T], PB[4 + k][:, 0:T])

            def exchange(g):
                pe.wait_ge(kq_copied, 16)
                if g >= 2:
                    pe.wait_ge(roped, g - 1)
                for e in range(2):
                    j = 2 * (g % 2) + e
                    last = mm(PB[4 + g % 2][:, e * T:(e + 1) * T], perm, kT[:, j, 0:T] if g < 2 else qraw[:, j, :],
                              start=True, stop=True)
                last.then_inc(swapped, 1)

            for g in range(2):
                for p in range(4):
                    n = VP0 + 4 * g + p
                    wide = [t[:, n % 2, :].rearrange("p (c n) -> p c n", c=2) for t in (hi, lo)]
                    pe.wait_ge(hi_ready, n + 1)
                    for tt in range(4):
                        if p == 0 and g:
                            pe.wait_ge(v_copied, tt + 1)
                        for e in range(2):
                            c = 2 * p + e
                            mm(PB[tt][:, :], h_hi[:, c, tt * P:(tt + 1) * P], wide[0][:, e, :],
                               start=(c == 0), stop=False)
                            last = mm(PB[tt][:, :], h_lo[:, c, tt * P:(tt + 1) * P], wide[0][:, e, :],
                                      start=False, stop=False)
                    last.then_inc(hi_used, 1)
                    pe.wait_ge(lo_ready, n + 1)
                    for tt in range(4):
                        for e in range(2):
                            c = 2 * p + e
                            last = mm(PB[tt][:, :], h_hi[:, c, tt * P:(tt + 1) * P], wide[1][:, e, :],
                                      start=False, stop=(c == NC - 1))
                    last.then_inc(piece_done, 1)
                    if g == 0 and p in (0, 3):
                        exchange(p // 3 * 2)
                        exchange(p // 3 * 2 + 1)
                    b = QP0 + ADA_FIRST + 4 * g + p
                    if b < ADA_LATE:
                        ada_block(b, b % 4)
                    if QP0 + ADA_FIRST < b <= ADA_LATE:
                        ada_sum(b - 1)

            def scores(u):
                kind, head, tile = units[u]
                for m, k in enumerate(maps_of[u]):
                    if k >= 4:
                        pe.wait_ge(exp_done, k - 3)
                    out = PB[k % 4]
                    if kind == "d":
                        flat = m * DIFF_HEADS + head
                        chunk, q = flat // 2, flat
                    else:
                        chunk, q = 4 + head // 2, 2 * DIFF_HEADS + head
                    left = qz[:, q, tile * P:(tile + 1) * P]
                    if kind == "d":
                        last = mm(out[:, :], left, kT[:, chunk, :], start=True, stop=True)
                    else:
                        mm(out[:, T:LC], left, kT[:, chunk, T:LC], start=True, stop=True)
                        mm(out[:, 0:T], left, kT[:, chunk, 0:T], start=True, stop=False)
                        pe.wait_ge(bias_ready, 1)
                        last = mm(out[:, 0:T], ident, bias[:, 2 * head + tile, :], start=False, stop=True)
                    last.then_inc(scored, 1)

            def attend(head):
                pe.wait_ge(probT_ready, 2 * head + 2)
                if head == 0:
                    pe.wait_ge(mod_ready, 1)
                if head >= 2:
                    pe.wait_ge(att_copied, head - 1)
                if 2 <= head < DIFF_HEADS + 2:
                    pe.wait_ge(dvar_ready, 2 * head - 2)
                if 3 <= head < DIFF_HEADS + 3:
                    pe.wait_ge(att_ready, head - 2)
                for kc in range(4):
                    if head < DIFF_HEADS:
                        left = vN[:, kc, 512 + P * head:512 + P * (head + 1)]
                        out = PB[6 + head % 2][:, 0:T]
                    else:
                        h = head - DIFF_HEADS
                        left = vN[:, kc, HD * h:HD * (h + 1)]
                        out = PB[6 + head % 2][HD * (h % 2):HD * (h % 2) + HD, 0:T]
                    last = mm(out, left, probT[:, head % 2, kc, :], start=(kc == 0), stop=(kc == 3))
                last.then_inc(pv_done, 1)

            pe.wait_ge(roped, 4)
            pe.wait_ge(v_copied, 8)
            scores(0)
            scores(1)
            for u in range(N_UNITS):
                if u + 2 < N_UNITS:
                    scores(u + 2)
                pe.wait_ge(prob_ready, u + 1)
                if u >= 2:
                    pe.wait_ge(probT_ready, u - 1)
                for kc in range(4):
                    last = nc.tensor.transpose(PB[4 + u % 2][:, kc * P:(kc + 1) * P],
                                               prob[:, u % 2, kc * P:(kc + 1) * P], ident)
                last.then_inc(transposed, 1)
                if u in (4, 6, 8, 10):
                    d = u // 2 - 2
                    pe.wait_ge(dsq_done, d + 1)
                    for t in range(2):
                        last = mm(PB[6 + d % 2][:, t:t + 1], dsq[:, d % 2, t * P:(t + 1) * P], ones[:, 0:1],
                                  start=True, stop=True)
                    last.then_inc(dcol_done, 1)
                if u in (7, 9, 11, 13):
                    d = (u - 7) // 2
                    pe.wait_ge(ddiag_ready, d + 1)
                    pe.wait_ge(att_copied, d + 2)
                    pe.wait_ge(dvar_ready, min(2 * d + 4, 8))
                    mm(PB[6 + (d + 1) % 2][:, 0:T], ones, diag[:, 0:2, :].rearrange("p a t -> p (a t)"),
                       start=True, stop=True).then_inc(dbc_done, 1)
                if u >= 2 and u % 2 == 0:
                    attend(u // 2 - 1)
            attend(N_AHEADS - 1)

            pe.wait_ge(exp_done, maps_of[-1][-1] + 1)

            for n in range(WO0, WQ0):
                j = n - WO0
                weights_piece(n, n, tok_hi[:, :, :], tok_lo[:, :, :], PB[j // 2][:, (j % 2) * T:(j % 2 + 1) * T],
                              order=ATT_ORDER, right_ready=None if j else ((tok_hi_ready, 0), (tok_lo_ready, 0)))
            column_sums(2, 4, ysq, ysum_ready, ycol_done)
            pe.wait_ge(att_copied, N_AHEADS)
            ada_block(ADA_LATE, ADA_LATE % 4)
            pe.wait_ge(yg_ready, NC)
            broadcast(PB[0], T, ydiag_ready, ybc_done)
            for b in range(ADA_LATE + 1, ADA_BLOCKS):
                ada_block(b, b % 4)
                ada_sum(b - 1)
            ada_sum(ADA_BLOCKS - 1)
            pe.wait_ge(yvar_ready, 2)
            column_sums(2, 4, ysq, x1sum_ready, x1col_done)
            pe.wait_ge(x1var_ready, 2)
            broadcast(PB[5], T, x1diag_ready, x1bc_done)

            pe.wait_ge(late_mod_ready, 1)
            for k in range(2):
                weights_piece(WQ0 + k, k, tok_hi[:, :, :], tok_lo[:, :, :], PB[6 + k][:, 0:T],
                              right_ready=None if k else ((tok_hi_ready, NC), (tok_lo_ready, NC)))
            with pe.Fori(1, 8) as i:
                for k in range(2):
                    pe.wait_ge(q_copied, 2 * i + k - 1)
                    weights_piece(WQ0 + 2 * i + k, k, tok_hi[:, :, :], tok_lo[:, :, :], PB[6 + k][:, 0:T])
            pe.wait_ge(q_copied, 16)
            pe.wait_ge(keys_loaded, 16)
            for g in range(8):
                if g >= 4:
                    pe.wait_ge(s_copied, g - 3)
                for e in range(4):
                    row = 4 * g + e
                    tile, hp = row // 16, row % 16
                    last = mm(PB[g % 4][:, e * NK:(e + 1) * NK], qT[:, hp, tile * P:(tile + 1) * P],
                              keys[:, hp, :], start=True, stop=True)
                last.then_inc(s_done, 1)

            def expert_rows(first, last):
                with pe.Fori(first // 2, last // 2) as i:
                    for k in range(2):
                        expert_row(2 * i + k, k)

            def expert_row(i, k):
                pe.wait_ge(act_done, i - 1)
                weights_piece(U0 + i, k, tok_hi[:, :, :], tok_lo[:, :, :], PB[k % 2][:, 0:T])

            def gate_quad(q, part, b):
                if not (isinstance(q, int) and q < 4 and not part):
                    pe.wait_ge(weighted, QUADS * part + q - 3)
                for e in range(4):
                    pe.wait_ge(ohi_ready, T * part + 4 * q + e + 1)
                    pe.wait_ge(ghj_ready, T * part + 4 * q + e + 1)
                    last = mm(PB[4 + b][:, e * HALF:(e + 1) * HALF], ghj[:, 4 * b + e, :], ohi[:, 4 * b + e, :],
                              start=True, stop=True)
                last.then_inc(gate_done, 1)

            pe.wait_ge(s_copied, 8)
            for k in range(2):
                weights_piece(U0 + k, k, tok_hi[:, :, :], tok_lo[:, :, :], PB[k][:, 0:T])
            expert_rows(2, GATES0)
            pe.wait_ge(gate_ready, 1)
            for s in range(3):
                for tile in range(2):
                    if s < 2:
                        src = ijs[:, tile, s, :, :].rearrange("p h k -> p (h k)")
                    else:
                        src = gate[:, tile * PH:(tile + 1) * PH, :].rearrange("p h k -> p (h k)")
                    out = (PB[2] if s < 2 else PB[3])[:, (s % 2) * T + tile * P:(s % 2) * T + (tile + 1) * P]
                    last = nc.tensor.transpose(out, src, ident)
            last.then_inc(slotT_done, 1)
            for k in range(8):
                expert_row(GATES0 + k, k)
                for e in range(TWELVE_AT[k], TWELVE_AT[k + 1]):
                    gate_quad(e, 0, e % 4)
            with pe.Fori(1, 5) as i:
                for k in range(8):
                    expert_row(GATES0 + 8 * i + k, k)
                    for e in range(TWELVE_AT[k], TWELVE_AT[k + 1]):
                        gate_quad(12 * i + e, 0, e % 4)
            for k in range(4):
                expert_row(NK - 4 + k, k)
                gate_quad(QUADS - 4 + k, 0, k)

            pe.wait_ge(act_done, NK)
            pe.wait_ge(slot_ready, 3)

            def final_row(g):
                if g >= 2:
                    pe.wait_ge(final_rows_copied, g - 1)
                for e in range(4):
                    c = 4 * (g % 2) + e
                    out = PB[4 + g % 2][:, e * P:(e + 1) * P]
                    if g < 4:
                        last = nc.tensor.transpose(out, x1T[:, c, (g // 2) * P:(g // 2 + 1) * P], ident)
                    else:
                        last = mm(out, gg[:, 1, c:c + 1].to_broadcast([P, P]), ident, start=True, stop=True)
                last.then_inc(final_rows, 1)

            def value_piece(n, i, k, first=False):
                wide = [t[:, k, :].rearrange("p (c n) -> p c n", c=2) for t in (hi, lo)]
                pe.wait_ge(hi_ready, n + 1)
                pe.wait_ge(w_hi_ready, i + 1)
                pe.wait_ge(w_lo_ready, i + 1)
                for tt in range(2):
                    for w in (w_hi, w_lo):
                        for e in range(2):
                            last = mm(PB[2 * tt + e][:, :], w[:, k, tt * P:(tt + 1) * P], wide[0][:, e, :],
                                      start=first and w is w_hi, stop=False)
                last.then_inc(hi_used, 1)
                pe.wait_ge(lo_ready, n + 1)
                for tt in range(2):
                    for e in range(2):
                        last = mm(PB[2 * tt + e][:, :], w_hi[:, k, tt * P:(tt + 1) * P], wide[1][:, e, :],
                                  start=False, stop=False)
                last.then_inc(piece_done, 1)

            def last_piece(k):
                wide = [t[:, k, :].rearrange("p (c n) -> p c n", c=2) for t in (hi, lo)]
                for ready, count in ((hi_ready, PIECES), (lo_ready, PIECES), (w_hi_ready, NK), (w_lo_ready, NK)):
                    pe.wait_ge(ready, count)
                for tt in range(2):
                    for w, right in ((w_hi, 0), (w_lo, 0), (w_hi, 1)):
                        for e in range(2):
                            last = mm(PB[2 * tt + e][:, :], w[:, k, tt * P:(tt + 1) * P], wide[right][:, e, :],
                                      start=False, stop=(right == 1))
                    last.then_inc(ftile_done, 1)

            def value_row(i, k):
                value_piece(V0 + i, i, k % 2)

            for k in range(4):
                value_piece(V0 + k, k, k % 2, first=(k == 0))
                gate_quad(k, 1, k)
            with pe.Fori(1, 14) as i:
                for k in range(4):
                    value_row(4 * i + k, k)
                    gate_quad(4 * i + k, 1, k)
            for k in range(12):
                value_row(56 + k, k)
                if k < 6:
                    for e in range(EIGHT_AT[k], EIGHT_AT[k + 1]):
                        gate_quad(56 + e, 1, e % 4)
                else:
                    if k == 6:
                        pe.wait_ge(weighted, 2 * QUADS)
                    final_row(k - 6)
            with pe.Fori(34, NK // 2 - 1) as i:
                for k in range(2):
                    value_row(2 * i + k, k)
            value_row(NK - 2, 0)
            last_piece(1)


def constants():
    import numpy as np
    cst = np.zeros((P, C_END), np.float32)
    cst[:, C_ID:C_ID + P] = np.eye(P)
    cst[:, C_ONE:C_ONE + P] = 1.0
    cst[:, C_IOTA:C_IOTA + P] = np.arange(P)
    cst[np.arange(P), C_PERM + (np.arange(P) ^ 1)] = 1.0
    for g in range(4):
        for m in range(2):
            cst[32 * g + m, C_SEL + m] = 1.0
    cst[:, C_I16:C_I16 + TOPK] = np.arange(TOPK)
    t = np.arange(T)
    freq = np.float32(10000.0) ** (-np.arange(HD // 4, dtype=np.float32) / (HD // 4))
    row, col = (t // GRID_W).astype(np.float32), (t % GRID_W).astype(np.float32)
    ang = np.concatenate([row[:, None] * freq, col[:, None] * freq], axis=-1)
    d = np.arange(P) % HD
    cos, sin = np.cos(ang)[:, d // 2].T, np.sin(ang)[:, d // 2].T
    tab = np.zeros((P, R_LAM), np.float32)
    tab[:, R_COS:R_COS + T] = cos
    tab[:, R_SIN:R_SIN + T] = np.where(d % 2 == 0, -1.0, 1.0)[:, None] * sin
    c = np.arange(P) % GRID_W
    start = np.clip(c - WIN_C // 2, 0, GRID_W - WIN_C)
    kc = np.arange(T) % GRID_W
    inside = (kc[None, :] >= start[:, None]) & (kc[None, :] < start[:, None] + WIN_C)
    tab[:, R_MASK:R_MASK + T] = np.where(inside, 0.0, MASKED)
    return cst, tab


def kernel(**inputs):
    import numpy as np
    import concourse.bacc as bacc
    from concourse.bass_utils import run_bass_kernel_spmd

    a = {k: np.asarray(x) for k, x in inputs.items()}

    def columns(w):
        return w.reshape(NC, P, -1, P).transpose(2, 1, 0, 3).reshape(-1, P, PW)

    def wide(w):
        return w.reshape(4, 2, P, 512).transpose(0, 2, 1, 3).reshape(4, P, PW)

    w_in = a["w_in"][0]
    qa, ka, va, qd, kd, vd = (w_in[:, 512 * k:512 * (k + 1)] for k in range(6))
    u = a["peer_u"][0].reshape(NK, P, NC, P).transpose(0, 3, 2, 1).reshape(NK, P, PW)
    stream = np.concatenate([columns(kd), columns(ka), columns(qd), columns(qa), wide(va), wide(vd),
                             columns(a["w_out"][0]), columns(a["peer_wq"][0]), u,
                             a["peer_v"][0].reshape(NK, P, PW)])
    tokens = np.concatenate([a["x"][0], a["ctx"][0]])
    cond = np.stack([a["c"][0], a["c_ctx"]])
    cst, tab = constants()
    t = np.arange(T)
    r_off = t[None, :] // GRID_W - t[:, None] // GRID_W + WIN_R - 1
    c_off = np.clip(t[None, :] % GRID_W - t[:, None] % GRID_W + WIN_C - 1, 0, 2 * WIN_C - 2)
    bias = a["na_rel_bias"][0][:, r_off, c_off].reshape(NA_HEADS, 2, P, T)
    arrays = {
        "xT": tokens.T.reshape(NC, P, LC).transpose(1, 0, 2),
        "cT": cond.T.reshape(NC, P, 2).transpose(1, 0, 2),
        "cst": cst,
        "small": np.concatenate([a["b_ada"][0].reshape(-1, P).T, a["g_norm"][0].reshape(-1, P).T,
                                 a["diff_subln"][0][:, None]], axis=1),
        "tab": np.concatenate([tab, np.broadcast_to(a["diff_lambda"][0].reshape(1, -1), (P, 4 * HD))], axis=1),
        "ada": a["w_ada"][0].reshape(NC, P, ADA_BLOCKS, ADA_N).transpose(2, 1, 0, 3).reshape(ADA_BLOCKS, P, -1),
        "bias": bias.transpose(2, 0, 1, 3).reshape(P, 16, T),
        "keys": a["peer_keys"][0].reshape(16, NK, P).transpose(2, 0, 1),
        "stream": stream,
    }
    arrays = {f"in_{k}": np.ascontiguousarray(x) for k, x in arrays.items()}
    nc = bacc.Bacc("TRN2", target_bir_lowering=False, num_devices=1)
    args = [nc.dram_tensor(k, x.shape, mybir.dt.float32, kind="ExternalInput").ap() for k, x in arrays.items()]
    out = nc.dram_tensor("out_dram", (1, T, D), mybir.dt.float32, kind="ExternalOutput").ap()
    program(nc, *args, out)
    got = run_bass_kernel_spmd(nc, [arrays], core_ids=[0])
    return got.results[0]["out_dram"]
```
